# Optimizing a Trainium2 kernel written in Bass

```python
import jax
import jax.numpy as jnp
from jax import lax
import numpy as np

D_MODEL = 1024
BATCH = 1
SEQ = 128
DEPTH = 2
DEC_BATCH = 1
DEC_SEQ = 512
PAST_LEN = 128

GRID_W = 64
CHUNK = 64
N_DIR = 2
N_EVEN = (DEPTH + 1) // 2
N_ODD = DEPTH // 2
ALPHA = (2.0 * DEPTH) ** 0.25
BETA = (8.0 * DEPTH) ** -0.25
H_A = 4
DK_A = 128
DV_A = 128
H_B = 4
DK_B = 128
DV_B = 128
W_A = H_A * DV_A
W_B = H_B * DV_B
EVEN_SIZES = (H_A * DK_A, H_A * DK_A, W_A, W_A, N_DIR * H_A, N_DIR * H_A, H_B * DK_B, H_B * DK_B, W_B, W_B)
EVEN_SPLITS = [int(s) for s in np.cumsum(EVEN_SIZES)[:-1]]
EVEN_IN = int(sum(EVEN_SIZES))
D_INNER = 2 * D_MODEL
P_C = 64
H_C = D_INNER // P_C
G_C = 4
J_C = H_C // G_C
N_C = 128
D_CONV = 5
CONV_DIM = D_INNER + 2 * G_C * N_C
ODD_IN = D_INNER + CONV_DIM + N_DIR * H_C
N_KEYS = 128
N_EXPERTS = N_KEYS * N_KEYS
H_P = 8
D_QK = 256
D_HALF = D_QK // 2
TOPK = 16
PEER_BLOCK = 128

kernel_name = 'bidir_mlstm_retnet_ssd_peer_prefix_trunk'

def _chunks(a):
    b, t = a.shape[0], a.shape[1]
    return jnp.moveaxis(a.reshape(b, t // CHUNK, CHUNK, *a.shape[2:]), 1, 0)

def _unchunks(a):
    a = jnp.moveaxis(a, 0, 1)
    return a.reshape(a.shape[0], a.shape[1] * a.shape[2], *a.shape[3:])

def _flip(a):
    return jnp.flip(a, axis=1)

def _layer_norm(x, g, b, eps=1e-5):
    xf = x.astype(jnp.float32)
    mu = xf.mean(-1, keepdims=True)
    var = jnp.square(xf - mu).mean(-1, keepdims=True)
    return ((xf - mu) * lax.rsqrt(var + eps) * g + b).astype(x.dtype)

def _head_norm(h, w, eps=1e-5):
    mu = h.mean(-1, keepdims=True)
    var = jnp.square(h - mu).mean(-1, keepdims=True)
    return (h - mu) * lax.rsqrt(var + eps) * w

def _modulation(cvec, w, b):
    m = jax.nn.silu(cvec) @ w + b
    return [t[:, None, :] for t in jnp.split(m, 6, axis=-1)]

def _grid_pos_embed(n_tok, dtype):
    rows = n_tok // GRID_W
    r = jnp.repeat(jnp.arange(rows, dtype=jnp.float32), GRID_W)
    col = jnp.tile(jnp.arange(GRID_W, dtype=jnp.float32), rows)
    quarter = D_MODEL // 4
    freqs = 1.0 / (10000.0 ** (jnp.arange(quarter, dtype=jnp.float32) / quarter))
    er = r[:, None] * freqs
    ec = col[:, None] * freqs
    return jnp.concatenate([jnp.sin(er), jnp.cos(er), jnp.sin(ec), jnp.cos(ec)], axis=-1).astype(dtype)

def _mlstm_scan(q, k, v, li, lf, C0, n0, m0):
    causal = jnp.tril(jnp.ones((CHUNK, CHUNK), dtype=bool))

    def step(carry, inp):
        C, n, m = carry
        qc, kc, vc, lic, lfc = inp
        b = jnp.cumsum(lfc, axis=1)
        dlog = jnp.where(causal[None, :, :, None], b[:, :, None] - b[:, None] + lic[:, None], -jnp.inf)
        inter = b + m[:, None]
        m_t = jnp.maximum(inter, dlog.max(axis=2))
        s = jnp.einsum('bthk,bshk->btsh', qc, kc) * jnp.exp(dlog - m_t[:, :, None])
        w_int = jnp.exp(inter - m_t)
        num = jnp.einsum('btsh,bshv->bthv', s, vc) + w_int[..., None] * jnp.einsum('bthk,bhkv->bthv', qc, C)
        den = s.sum(axis=2) + w_int * jnp.einsum('bthk,bhk->bth', qc, n)
        h = num / jnp.maximum(jnp.abs(den), jnp.exp(-m_t))[..., None]
        g = b[:, -1:] - b + lic
        m_new = jnp.maximum(b[:, -1] + m, g.max(axis=1))
        wg = jnp.exp(g - m_new[:, None])
        dec = jnp.exp(b[:, -1] + m - m_new)
        C_new = dec[..., None, None] * C + jnp.einsum('bsh,bshk,bshv->bhkv', wg, kc, vc)
        n_new = dec[..., None] * n + jnp.einsum('bsh,bshk->bhk', wg, kc)
        return (C_new, n_new, m_new), h

    fin, h = lax.scan(step, (C0, n0, m0), (_chunks(q), _chunks(k), _chunks(v), _chunks(li), _chunks(lf)))
    return _unchunks(h), fin

def _retention_scan(q, k, v, log_gamma, S0):
    idx = jnp.arange(CHUNK, dtype=jnp.float32)
    diff = idx[:, None] - idx[None, :]
    decay_mat = jnp.where((diff >= 0)[..., None], jnp.exp(jnp.maximum(diff, 0.0)[..., None] * log_gamma), 0.0)
    xi = jnp.exp((idx[:, None] + 1.0) * log_gamma)
    zeta = jnp.exp((CHUNK - 1.0 - idx)[:, None] * log_gamma)
    g_end = jnp.exp(CHUNK * log_gamma)

    def step(S, inp):
        qc, kc, vc = inp
        s = jnp.einsum('bthk,bshk->btsh', qc, kc) * decay_mat
        o = jnp.einsum('btsh,bshv->bthv', s, vc) + xi[None, :, :, None] * jnp.einsum('bthk,bhkv->bthv', qc, S)
        S_new = g_end[None, :, None, None] * S + jnp.einsum('bshk,bshv,sh->bhkv', kc, vc, zeta)
        return S_new, o

    fin, o = lax.scan(step, S0, (_chunks(q), _chunks(k), _chunks(v)))
    return _unchunks(o), fin

def _ssd_scan(x, bm, cm, dt, a, h0):
    causal = jnp.tril(jnp.ones((CHUNK, CHUNK), dtype=bool))

    def step(h, inp):
        xc, bc, cc, dtc, ac = inp
        acum = jnp.cumsum(ac, axis=1)
        seg = jnp.where(causal[None, :, :, None, None], acum[:, :, None] - acum[:, None], -jnp.inf)
        s = jnp.einsum('btgn,bsgn->btsg', cc, bc)[..., None] * jnp.exp(seg) * dtc[:, None]
        y = jnp.einsum('btsgj,bsgjp->btgjp', s, xc) + jnp.exp(acum)[..., None] * jnp.einsum('btgn,bgjpn->btgjp', cc, h)
        a_end = acum[:, -1]
        w = jnp.exp(a_end[:, None] - acum) * dtc
        h_new = jnp.exp(a_end)[..., None, None] * h + jnp.einsum('bsgj,bsgjp,bsgn->bgjpn', w, xc, bc)
        return h_new, y

    fin, y = lax.scan(step, h0, (_chunks(x), _chunks(bm), _chunks(cm), _chunks(dt), _chunks(a)))
    return _unchunks(y), fin

def _even_mixer(u, w_in, i_bias, f_bias, log_decay, gn_a, gn_b, w_out, C0, n0, m0, S0):
    f32 = jnp.float32
    bsz, t, _ = u.shape
    qa, ka, va, oa, ia, fa, qb, kb, vb, gb = jnp.split(u @ w_in, EVEN_SPLITS, axis=-1)
    qa = qa.reshape(bsz, t, H_A, DK_A).astype(f32)
    ka = ka.reshape(bsz, t, H_A, DK_A).astype(f32) * DK_A ** -0.5
    va = va.reshape(bsz, t, H_A, DV_A).astype(f32)
    li = ia.reshape(bsz, t, N_DIR, H_A).astype(f32) + i_bias.astype(f32)
    lf = jax.nn.log_sigmoid(fa.reshape(bsz, t, N_DIR, H_A).astype(f32) + f_bias.astype(f32))
    C0 = C0.astype(f32)
    n0 = n0.astype(f32)
    m0 = m0.astype(f32)
    S0 = S0.astype(f32)
    ha_f, (Cf, nf, mf) = _mlstm_scan(qa, ka, va, li[:, :, 0], lf[:, :, 0], C0[:, 0], n0[:, 0], m0[:, 0])
    ha_b, (Cb, nb, mb) = _mlstm_scan(_flip(qa), _flip(ka), _flip(va), _flip(li[:, :, 1]), _flip(lf[:, :, 1]), C0[:, 1], n0[:, 1], m0[:, 1])
    ha = _head_norm(ha_f + _flip(ha_b), gn_a) * jax.nn.sigmoid(oa.reshape(bsz, t, H_A, DV_A).astype(f32))
    qb = qb.reshape(bsz, t, H_B, DK_B).astype(f32) * DK_B ** -0.5
    kb = kb.reshape(bsz, t, H_B, DK_B).astype(f32)
    vb = vb.reshape(bsz, t, H_B, DV_B).astype(f32)
    lg = -jnp.exp(log_decay.astype(f32))
    hb_f, Sf = _retention_scan(qb, kb, vb, lg[0], S0[:, 0])
    hb_b, Sb = _retention_scan(_flip(qb), _flip(kb), _flip(vb), lg[1], S0[:, 1])
    hb = _head_norm(hb_f + _flip(hb_b), gn_b) * jax.nn.silu(gb.reshape(bsz, t, H_B, DV_B).astype(f32))
    mixed = jnp.concatenate([ha.reshape(bsz, t, W_A), hb.reshape(bsz, t, W_B)], axis=-1).astype(u.dtype)
    fin = (jnp.stack([Cf, Cb], axis=1), jnp.stack([nf, nb], axis=1), jnp.stack([mf, mb], axis=1), jnp.stack([Sf, Sb], axis=1))
    return mixed @ w_out, fin

def _odd_mixer(u, w_in, conv_w, conv_b, dt_bias, a_log, d_skip, norm_w, w_out, h_st):
    f32 = jnp.float32
    bsz, t, _ = u.shape
    z, xbc, dt = jnp.split(u @ w_in, [D_INNER, D_INNER + CONV_DIM], axis=-1)
    xbc = lax.conv_general_dilated(xbc, conv_w.astype(xbc.dtype)[:, None, :], window_strides=(1,), padding=[(D_CONV // 2, D_CONV // 2)], dimension_numbers=('NWC', 'WIO', 'NWC'), feature_group_count=CONV_DIM)
    xbc = jax.nn.silu(xbc + conv_b)
    xs, bm, cm = jnp.split(xbc, [D_INNER, D_INNER + G_C * N_C], axis=-1)
    xs = xs.reshape(bsz, t, G_C, J_C, P_C).astype(f32)
    bm = bm.reshape(bsz, t, G_C, N_C).astype(f32)
    cm = cm.reshape(bsz, t, G_C, N_C).astype(f32)
    dt = jax.nn.softplus(dt.reshape(bsz, t, N_DIR, G_C, J_C).astype(f32) + dt_bias.astype(f32).reshape(N_DIR, G_C, J_C))
    A = -jnp.exp(a_log.astype(f32)).reshape(N_DIR, G_C, J_C)
    h0 = h_st.astype(f32).reshape(bsz, N_DIR, G_C, J_C, P_C, N_C)
    y_f, hf = _ssd_scan(xs, bm, cm, dt[:, :, 0], dt[:, :, 0] * A[0], h0[:, 0])
    dt_b = _flip(dt[:, :, 1])
    y_b, hb = _ssd_scan(_flip(xs), _flip(bm), _flip(cm), dt_b, dt_b * A[1], h0[:, 1])
    y = y_f + _flip(y_b) + d_skip.astype(f32).reshape(G_C, J_C, 1) * xs
    y = y.reshape(bsz, t, D_INNER) * jax.nn.silu(z.astype(f32))
    y = y * lax.rsqrt(jnp.square(y).mean(-1, keepdims=True) + 1e-5) * norm_w
    fin = jnp.stack([hf.reshape(bsz, H_C, P_C, N_C), hb.reshape(bsz, H_C, P_C, N_C)], axis=1)
    return y.astype(u.dtype) @ w_out, fin

def _peer(x, w_q, sub_keys, u_tab, v_tab):
    bsz, t, d = x.shape
    xt = x.reshape(-1, PEER_BLOCK, d)

    def block(xb):
        q = (xb @ w_q).reshape(PEER_BLOCK, H_P, 2, D_HALF).astype(jnp.float32)
        s = jnp.einsum('thcd,hcnd->thcn', q, sub_keys.astype(jnp.float32))
        sv, si = lax.top_k(s, TOPK)
        cand = (sv[:, :, 0, :, None] + sv[:, :, 1, None, :]).reshape(PEER_BLOCK, H_P, TOPK * TOPK)
        cand_idx = (si[:, :, 0, :, None] * N_KEYS + si[:, :, 1, None, :]).reshape(PEER_BLOCK, H_P, TOPK * TOPK)
        best, pos = lax.top_k(cand, TOPK)
        idx = jnp.take_along_axis(cand_idx, pos, axis=-1)
        g = jax.nn.softmax(best, axis=-1)
        act = jax.nn.gelu(jnp.einsum('thkd,td->thk', u_tab[idx], xb).astype(jnp.float32), approximate=False)
        return jnp.einsum('thk,thkd->td', (g * act).astype(xb.dtype), v_tab[idx])

    return lax.map(block, xt).reshape(bsz, t, d)

def setup_inputs(seed: int = 0) -> dict:
    key = jax.random.key(seed)
    ks = iter(jax.random.split(key, 48))
    f32 = jnp.float32

    def nrm(shape, scale):
        return jax.random.normal(next(ks), shape, f32) * scale

    D = D_MODEL
    ret_base = jnp.log(-jnp.log(1.0 - 2.0 ** (-5.0 - jnp.arange(H_B, dtype=f32))))
    dt0 = jnp.exp(jax.random.uniform(next(ks), (N_ODD, N_DIR, H_C), f32, float(np.log(1e-3)), float(np.log(1e-1))))
    return {
        'x_prompt': nrm((BATCH, SEQ, D), 1.0),
        'x_sample': nrm((DEC_BATCH, DEC_SEQ, D), 1.0),
        'c': nrm((DEC_BATCH, D), 1.0),
        'c_ctx': nrm((D,), 1.0),
        'state_mlstm_C': nrm((DEC_BATCH, N_EVEN, N_DIR, H_A, DK_A, DV_A), 0.2),
        'state_mlstm_n': nrm((DEC_BATCH, N_EVEN, N_DIR, H_A, DK_A), 0.2),
        'state_mlstm_m': nrm((DEC_BATCH, N_EVEN, N_DIR, H_A), 1.0),
        'state_ret': nrm((DEC_BATCH, N_EVEN, N_DIR, H_B, DK_B, DV_B), 0.2),
        'state_ssd': nrm((DEC_BATCH, N_ODD, N_DIR, H_C, P_C, N_C), 0.2),
        'w_mod': nrm((DEPTH, D, 6 * D), D ** -0.5),
        'b_mod': nrm((DEPTH, 6 * D), 0.02),
        'ln1_g': 1.0 + nrm((DEPTH, D), 0.02),
        'ln1_b': nrm((DEPTH, D), 0.02),
        'ln2_g': 1.0 + nrm((DEPTH, D), 0.02),
        'ln2_b': nrm((DEPTH, D), 0.02),
        'even_w_in': nrm((N_EVEN, D, EVEN_IN), D ** -0.5),
        'mlstm_i_bias': nrm((N_EVEN, N_DIR, H_A), 0.1),
        'mlstm_f_bias': jnp.linspace(3.0, 6.0, H_A, dtype=f32) + nrm((N_EVEN, N_DIR, H_A), 0.1),
        'ret_log_decay': ret_base + nrm((N_EVEN, N_DIR, H_B), 0.05),
        'even_gn_a': 1.0 + nrm((N_EVEN, H_A, DV_A), 0.02),
        'even_gn_b': 1.0 + nrm((N_EVEN, H_B, DV_B), 0.02),
        'even_w_out': nrm((N_EVEN, W_A + W_B, D), BETA * (W_A + W_B) ** -0.5),
        'odd_w_in': nrm((N_ODD, D, ODD_IN), D ** -0.5),
        'odd_conv_w': nrm((N_ODD, D_CONV, CONV_DIM), D_CONV ** -0.5),
        'odd_conv_b': nrm((N_ODD, CONV_DIM), 0.02),
        'odd_dt_bias': dt0 + jnp.log(-jnp.expm1(-dt0)),
        'odd_a_log': jnp.log(jax.random.uniform(next(ks), (N_ODD, N_DIR, H_C), f32, 1.0, 16.0)),
        'odd_d': 1.0 + nrm((N_ODD, H_C), 0.1),
        'odd_norm_w': 1.0 + nrm((N_ODD, D_INNER), 0.02),
        'odd_w_out': nrm((N_ODD, D_INNER, D), BETA * D_INNER ** -0.5),
        'peer_w_q': nrm((DEPTH, D, H_P * D_QK), D ** -0.5),
        'peer_sub_keys': nrm((DEPTH, H_P, 2, N_KEYS, D_HALF), D_HALF ** -0.5),
        'peer_u': nrm((DEPTH, N_EXPERTS, D), D ** -0.5),
        'peer_v': nrm((DEPTH, N_EXPERTS, D), BETA),
    }

def reference(x_prompt, x_sample, c, c_ctx, state_mlstm_C, state_mlstm_n, state_mlstm_m, state_ret, state_ssd, w_mod, b_mod, ln1_g, ln1_b, ln2_g, ln2_b, even_w_in, mlstm_i_bias, mlstm_f_bias, ret_log_decay, even_gn_a, even_gn_b, even_w_out, odd_w_in, odd_conv_w, odd_conv_b, odd_dt_bias, odd_a_log, odd_d, odd_norm_w, odd_w_out, peer_w_q, peer_sub_keys, peer_u, peer_v):
    f32 = jnp.float32
    bp = x_prompt.shape[0]
    xp = x_prompt
    xs = x_sample + _grid_pos_embed(x_sample.shape[1], x_sample.dtype)[None]
    new_C, new_n, new_m, new_S, new_h = [], [], [], [], []
    for l in range(DEPTH):
        sh1p, sc1p, g1p, sh2p, sc2p, g2p = _modulation(c_ctx[None, :], w_mod[l], b_mod[l])
        sh1s, sc1s, g1s, sh2s, sc2s, g2s = _modulation(c, w_mod[l], b_mod[l])
        hp = xp * (1 + sc1p) + sh1p
        hs = xs * (1 + sc1s) + sh1s
        j = l // 2
        if l % 2 == 0:
            prm = (even_w_in[j], mlstm_i_bias[j], mlstm_f_bias[j], ret_log_decay[j], even_gn_a[j], even_gn_b[j], even_w_out[j])
            mp, fin = _even_mixer(hp, *prm, jnp.zeros((bp, N_DIR, H_A, DK_A, DV_A), f32), jnp.zeros((bp, N_DIR, H_A, DK_A), f32), jnp.zeros((bp, N_DIR, H_A), f32), jnp.zeros((bp, N_DIR, H_B, DK_B, DV_B), f32))
            ms, _ = _even_mixer(hs, *prm, state_mlstm_C[:, j], state_mlstm_n[:, j], state_mlstm_m[:, j], state_ret[:, j])
            new_C.append(fin[0])
            new_n.append(fin[1])
            new_m.append(fin[2])
            new_S.append(fin[3])
        else:
            prm = (odd_w_in[j], odd_conv_w[j], odd_conv_b[j], odd_dt_bias[j], odd_a_log[j], odd_d[j], odd_norm_w[j], odd_w_out[j])
            mp, fin = _odd_mixer(hp, *prm, jnp.zeros((bp, N_DIR, H_C, P_C, N_C), f32))
            ms, _ = _odd_mixer(hs, *prm, state_ssd[:, j])
            new_h.append(fin)
        xp = _layer_norm(ALPHA * xp + g1p * mp, ln1_g[l], ln1_b[l])
        xs = _layer_norm(ALPHA * xs + g1s * ms, ln1_g[l], ln1_b[l])
        fp = _peer(xp * (1 + sc2p) + sh2p, peer_w_q[l], peer_sub_keys[l], peer_u[l], peer_v[l])
        fs = _peer(xs * (1 + sc2s) + sh2s, peer_w_q[l], peer_sub_keys[l], peer_u[l], peer_v[l])
        xp = _layer_norm(ALPHA * xp + g2p * fp, ln2_g[l], ln2_b[l])
        xs = _layer_norm(ALPHA * xs + g2s * fs, ln2_g[l], ln2_b[l])
    new_mlstm_C = jnp.stack(new_C, axis=1)
    new_mlstm_n = jnp.stack(new_n, axis=1)
    new_mlstm_m = jnp.stack(new_m, axis=1)
    new_ret = jnp.stack(new_S, axis=1)
    new_ssd = jnp.stack(new_h, axis=1)
    return (xp, xs, new_mlstm_C, new_mlstm_n, new_mlstm_m, new_ret, new_ssd)


_drawn_inputs = setup_inputs


def setup_inputs(seed=0):
    import zlib

    import numpy as np

    out = dict(_drawn_inputs(seed))
    spreads = {}
    factors = {'state_mlstm_C': 6.302,
     'state_mlstm_n': 8.0,
     'state_mlstm_m': 8.0,
     'state_ret': 26.007,
     'even_gn_a': 11.204,
     'even_gn_b': 8.683,
     'odd_d': 6.34,
     'odd_norm_w': 6.349}
    for name, (base, spread) in spreads.items():
        noise = np.random.default_rng([zlib.crc32(name.encode()), seed]).standard_normal(out[name].shape)
        drawn = base * np.exp(spread * noise) if base else spread * noise
        out[name] = jnp.asarray(drawn.astype(out[name].dtype))
    for name, factor in factors.items():
        out[name] = (out[name] * factor).astype(out[name].dtype)
    return out
```

```python
import numpy as np
import concourse.bass as bass
from concourse import mybir
from contextlib import ExitStack

D = 1024
P = 128
SEQ, DEC = 128, 512
T = SEQ + DEC
NT = T // P
KD = D // P
DEPTH = 2
GRID_W = 64
ALPHA = (2.0 * DEPTH) ** 0.25
EPS = 1e-5
NH = 4
DH = 128
W_A = NH * DH
D_INNER = 2 * D
P_C, N_C, G_C, J_C = 64, 128, 4, 8
H_C = G_C * J_C
D_CONV = 5
CONV_DIM = D_INNER + 2 * G_C * N_C
GC = J_C * P_C
N_KEYS, H_P, TOPK = 128, 8, 16
HK = H_P * TOPK
NMOD = 6 * D
SLICE = 256
NSLOT = 8
JB = 8
NBLK = N_KEYS // JB
HT = T // 2
NEG = -1.0e30


class Chain:

    def __init__(self, eng, sem):
        self.eng, self.sem, self.n = eng, sem, 0

    def do(self, ins):
        ins.then_inc(self.sem, 1)
        self.n = self.n + 1

    def settle(self):
        self.eng.wait_ge(self.sem, self.n)

    def link(self, ins):
        self.do(ins)
        self.settle()


def trunk(nc, a, o, upto):
    f32 = mybir.dt.float32
    bf16 = mybir.dt.bfloat16
    u32 = mybir.dt.uint32
    ALU = mybir.AluOpType
    ACT = mybir.ActivationFunctionType
    AX = mybir.AxisListType.X

    stages = ["mod", "even", "peer0", "odd", "peer1"]
    run = stages[: stages.index(upto) + 1] if upto else stages

    ctx = ExitStack()

    def sb(name, shape, dt=f32, scope=None):
        return (scope or ctx).enter_context(nc.sbuf_tensor(name, shape, dt))

    def sem(name):
        return ctx.enter_context(nc.semaphore(name))

    x = sb("x", [P, NT, D])
    hT = sb("hT", [P, KD, T])
    ring = sb("ring", [P, NSLOT, KD * SLICE])
    wide = sb("wide", [P, 2 * NT * D])
    f = wide[:, 0:NT * D].rearrange("p (n d) -> p n d", n=NT)
    hi = wide[:, NT * D:2 * NT * D]
    ident = sb("ident", [P, P])
    ones = sb("ones", [P, P])
    modT = sb("modT", [P, DEPTH, 4, KD, 2])
    cT = sb("cT", [P, KD, 2])
    stat = sb("stat", [P, 20, 6])
    mv = sb("mv", [P, 20, 2])
    rstd = sb("rstd", [P, 20])
    eps = sb("eps", [P, 1])
    PS = ctx.enter_context(nc.psum_tensor("PS", [P, 8, 512], f32))

    gdram = nc.dram_tensor("gate_rows", [DEPTH, 2, 2, D], f32, kind="Internal").ap()
    Ad = nc.dram_tensor("expert_acts", [NBLK, P, JB, T], f32, kind="Internal").ap()
    Gd = nc.dram_tensor("expert_gates", [NBLK, P, T // 16, JB, 16], f32, kind="Internal").ap()

    base = ExitStack()
    mrow = sb("mrow", [2, NMOD], scope=base)
    bmod = wide[0:2, 4 * D:4 * D + NMOD]
    base.close()

    ev = ExitStack()
    qT = sb("qT", [P, NH, T], scope=ev)
    kT = sb("kT", [P, NH, T], scope=ev)
    v1 = sb("v1", [P, NT, NH, DH + 1], scope=ev)
    ktok = hi[:, 0:NT * W_A].rearrange("p (n h d) -> p n h d", n=NT, h=NH)
    og = hi[:, NT * W_A:2 * NT * W_A].rearrange("p (n d) -> p n d", n=NT)
    row = sb("row", [NH, 2, T], scope=ev)
    small = sb("gate_small", [NH, 6, 2, NT], scope=ev)
    BE, ML, MP, DEC_, BM = (small[:, i] for i in range(5))
    m0 = sb("m0", [NH, 2], scope=ev)
    gbias = sb("gbias", [NH, 4], scope=ev)
    sel4 = sb("sel4", [NH, NH, P], scope=ev)
    cols = sb("cols", [P, NT, 4, 2, NH], scope=ev)
    decB = sb("decB", [P, NH, 2, NT], scope=ev)
    Cst = sb("Cst", [P, 2, NH, DH + 1], scope=ev)
    Cout = sb("Cout", [P, 2, NH, DH + 1], scope=ev)
    mask = sb("mask", [P, 2, P], scope=ev)
    Dm = sb("Dm", [P, 2, NH, P], scope=ev)
    diff = sb("diff", [P, 2, P], scope=ev)
    icol = sb("icol", [P, 4], scope=ev)
    lg = sb("lg", [P, 2, NH], scope=ev)
    xz = sb("xz", [P, 3, 2, NH], scope=ev)
    gn = sb("gn", [P, 2, W_A], scope=ev)
    eb = sb("eb", [P, 2, P], scope=ev)
    pb = sb("pb", [P, 2, P], scope=ev)
    kw = sb("kw", [P, 2, P], scope=ev)
    nd = sb("nd", [P, 2, DH + 2], scope=ev)
    ev.close()
    grow = wide[0:NH, 0:4 * 2 * T].rearrange("p (k d t) -> p k d t", k=4, d=2)
    b_m = hi[0:NH, 0:4 * T].rearrange("p (k d t) -> p k d t", k=2, d=2)

    ln = ExitStack()
    rowsB = sb("rowsB", [P, 4, D], scope=ln)
    ln.close()

    od = ExitStack()
    xs = sb("xs", [P, NT, GC], scope=od)
    BC = sb("BC", [P, 2, T], scope=od)
    Btok = sb("Btok", [P, NT, N_C], scope=od)
    hst = sb("hst", [P, 2, GC], scope=od)
    hout = sb("hout", [P, 2, GC], scope=od)
    EP = sb("EP", [P, 2, J_C, P], scope=od)
    cpad = sb("cpad", [P, 2, T + 8], scope=od)
    cacc = sb("cacc", [P, 2, T + 2], scope=od)
    sx = EP[:].rearrange("p a j t -> p a (j t)")[:, :, 0:T]
    dtc = sb("dtc", [P, NT, 2, H_C], scope=od)
    av = sb("av", [P, NT, 2, H_C], scope=od)
    nac = sb("nac", [P, NT, 2, H_C], scope=od)
    wup = sb("wup", [P, NT, 2, H_C], scope=od)
    win = sb("win", [P, NT, 2, H_C], scope=od)
    dcy = sb("dcy", [P, NT, 2, H_C], scope=od)
    tri = sb("tri", [P, 2, P], scope=od)
    maskO = sb("maskO", [P, 2, P], scope=od)
    brow = sb("brow", [P, 3, 2 * H_C], scope=od)
    cw = sb("cw", [P, 24, D_CONV + 1], scope=od)
    otmp = sb("otmp", [P, GC], scope=od)
    xw = sb("xw", [P, GC], scope=od)
    od.close()
    oz = ExitStack()
    yT = sb("yT", [P, 2 * KD, T], scope=oz)
    zt = sb("zt", [P, 2, SLICE], scope=oz)
    nw = sb("nw", [P, 2 * KD], scope=oz)
    ssq = sb("ssq", [P, NT], scope=oz)
    rowsO = sb("rowsO", [P, 4, D], scope=oz)
    oz.close()
    y = wide[:, :].rearrange("p (n d) -> p n d", n=NT)

    pu = ExitStack()
    sv = sb("sv", [P, NT, H_P, 2, TOPK], scope=pu)
    si = sb("si", [P, NT, H_P, 2, TOPK], u32, scope=pu)
    hkT = sb("hkT", [P, 3, T], scope=pu)
    qb = sb("qb", [P, 2, T], scope=pu)
    abuf = sb("abuf", [P, 2, 2, T], scope=pu)
    swork = sb("swork", [P, N_KEYS], scope=pu)
    sif = sb("sif", [P, H_P, 2, TOPK], scope=pu)
    best = sb("best", [P, NT, H_P, TOPK], scope=pu)
    pos = sb("pos", [P, H_P, TOPK], u32, scope=pu)
    posi = sb("posi", [P, 2, HK], u32, scope=pu)
    posf = sb("posf", [P, 2, HK], scope=pu)
    hkt = sb("hkt", [P, NT, 3, HK], scope=pu)
    ssum = sb("ssum", [P, NT, H_P], scope=pu)
    cand = sb("cand", [P, 2, TOPK * TOPK], scope=pu)
    iota = sb("iota", [P, N_KEYS], scope=pu)
    pu.close()
    eqb = wide[:, 0:TOPK * HK].rearrange("p (a b) -> p a b", b=TOPK)
    eqc = wide[:, TOPK * HK:2 * TOPK * HK].rearrange("p (a b) -> p a b", b=TOPK)
    gst = wide[:, 0:4096].rearrange("p (s j t) -> p s j t", s=2, j=P)
    hot = wide[:, 4096:8192].rearrange("p (s c t i) -> p s c t i", s=2, c=2, t=8)
    keys = wide[:, 8192:10240].rearrange("p (c n) -> p c n", c=2 * H_P)

    pv = ExitStack()
    rowsP = sb("rowsP", [P, 4, D], scope=pv)
    gb = sb("gb", [P, 2, T // 16, JB, 16], scope=pv)
    pv.close()
    ab = [hT[:, :, :], hi.rearrange("p (j t) -> p j t", j=JB)]

    products = sem("products")
    slot_full = [sem(f"slot_full{i}") for i in range(NSLOT)]
    vec_chain, act_chain, pool_chain = sem("vec_chain"), sem("act_chain"), sem("pool_chain")
    consts_ready, small_loaded = sem("consts_ready"), sem("small_loaded")
    c_ready, mod_evac, mod_rows, mod_cols = sem("c_ready"), sem("mod_evac"), sem("mod_rows"), sem("mod_cols")
    gates_stored, x_loaded, x_ready = sem("gates_stored"), sem("x_loaded"), sem("x_ready")
    h_evac_v, h_evac_a = sem("h_evac_v"), sem("h_evac_a")
    rows_loaded, var_ready, dev_ready, f_ready = sem("rows_loaded"), sem("var_ready"), sem("dev_ready"), sem("f_ready")
    stored = sem("stored")
    even_loaded, proj_a, proj_v = sem("even_loaded"), sem("proj_a"), sem("proj_v")
    gate_exp, gate_act, gates_done, cols_ready = sem("gate_exp"), sem("gate_act"), sem("gates_done"), sem("cols_ready")
    e_ready, exp_ready, p_ready, kw_ready = sem("e_ready"), sem("exp_ready"), sem("p_ready"), sem("kw_ready")
    h_done, state_ready, ret_ready = sem("h_done"), sem("state_ready"), sem("ret_ready")
    diff_ready, decay_ready, norm_done, og_ready = sem("diff_ready"), sem("decay_ready"), sem("norm_done"), sem("og_ready")
    out_evac = sem("out_evac")
    odd_loaded, dt_abs, dt_sp, a_ready, ac_ready, seg_exp = (sem(n) for n in
        ("odd_loaded", "dt_abs", "dt_sp", "a_ready", "ac_ready", "seg_exp"))
    pad_filled, conv_done, act_done, tr_evac, oe_ready, oexp_ready, op_ready, skip_ready, y_intra = (sem(n) for n in
        ("pad_filled", "conv_done", "act_done", "tr_evac", "oe_ready", "oexp_ready", "op_ready", "skip_ready", "y_intra"))
    inter_done, xw_ready, upd_done, hst_loaded, hst_stored, z_silu, z_used, ssq_done, yt_v, yt_a, oo_evac = (sem(n) for n in
        ("inter_done", "xw_ready", "upd_done", "hst_loaded", "hst_stored", "z_silu", "z_used", "ssq_done", "yt_v", "yt_a", "oo_evac"))
    keys_loaded, q_evac, s_used, hk_ready, hk_evac, sm_exp, sm_sub = (sem(n) for n in
        ("keys_loaded", "q_evac", "s_used", "hk_ready", "hk_evac", "sm_exp", "sm_sub"))
    act_gelu, a_stored, hot_ready, g_evac, g_stored, ag_loaded, w_ready, acc_done, iota_ready = (sem(n) for n in
        ("act_gelu", "a_stored", "hot_ready", "g_evac", "g_stored", "ag_loaded0", "w_ready", "acc_done", "iota_ready"))
    ag_loaded, a_stored, g_stored = [ag_loaded, sem("ag_loaded1")], [a_stored, sem("a_stored1")], [g_stored, sem("g_stored1")]
    ev_consts, od_consts, dm_ready, decay_exp, alog_exp, nw_loaded, rr_ready = (sem(n) for n in
        ("ev_consts", "od_consts", "dm_ready", "decay_exp", "alog_exp", "nw_loaded", "rr_ready"))

    at = {}
    slices = []
    UNITS = [(s, h, d) for s in range(NT) for h in range(NH) for d in range(2)]
    NU = len(UNITS)

    def tile_of(step, d):
        return step if d == 0 or step == 0 else NT - step

    def first_on(step, d):
        t = tile_of(step, d)
        other = t if d == 1 else (NT - t if t else 0)
        return step < other or (step == other and d == 0)

    def bc(v, n):
        return v.unsqueeze(len(v.shape)).broadcast_to(list(v.shape) + [n])

    proj = []
    for fam in range(2):
        if fam == 0:
            proj.append(("gate", 0, 0, "v"))
        proj += [("q", fam, i, "a") for i in range(NH)] + [("k", fam, i, "a") for i in range(NH)]
        proj += [("v", fam, (s, t), "v") for s in range(2) for t in range(NT)]
        proj += [("o", fam, (s, t), "a") for s in range(2) for t in range(NT)]
        proj += [("kt", fam, t, "v") for t in range(NT)]
    proj_count, n_a, n_v = {}, 0, 0
    for i, (kind, fam, m, e) in enumerate(proj):
        n_a, n_v = n_a + (e == "a"), n_v + (e == "v")
        proj_count[kind, fam, m] = (i, e, n_a if e == "a" else n_v)

    with ctx, nc.Block() as block:

        @block.tensor
        def _(pe):
            state = {"n": 0, "slice": 0}

            def done(ins, label):
                ins.then_inc(products, 1)
                state["n"] = state["n"] + 1
                at[label] = state["n"]

            def take(src):
                n = state["slice"]
                state["slice"] += 1
                pe.wait_ge(slot_full[n % NSLOT], 16 * (n // NSLOT + 1))
                slices.append([src, None])
                return ring[:, n % NSLOT, 0:src.shape[-1]]

            def release(label):
                slices[-1][1] = label

            def evacuated(kind, fam, m):
                _, e, n = proj_count[kind, fam, m]
                pe.wait_ge(proj_a if e == "a" else proj_v, n)

            pe.wait_ge(consts_ready, 1)
            pe.wait_ge(c_ready, 1)
            for l in range(DEPTH):
                for s in range(NMOD // SLICE):
                    g = l * (NMOD // SLICE) + s
                    w = take(a["w_mod"][l, s]).rearrange("p (k n) -> p k n", k=KD)
                    if g >= 4:
                        pe.wait_ge(mod_evac, g - 3)
                    for k in range(KD):
                        last = nc.tensor.matmul(PS[0:2, g % 4, 0:SLICE], cT[:, k, :], w[:, k, :],
                                                start=(k == 0), stop=(k == KD - 1))
                    done(last, ("mod", l, s))
                    release(("mod", l, s))
                pe.wait_ge(mod_rows, l + 1)
                if l:
                    pe.wait_ge(mod_cols, l)
                for i, kind in enumerate((0, 1, 3, 4)):
                    for k in range(KD):
                        c = (i * KD + k) * 2
                        last = nc.tensor.matmul(PS[:, 4, c:c + 2], mrow[0:2, kind * D + k * P:kind * D + (k + 1) * P],
                                                ident[0:2, 0:2], start=True, stop=True)
                done(last, ("fold", l))

            def modulated(n):
                pe.wait_ge(x_ready, n + 1)
                pe.wait_ge(mod_cols, DEPTH)
                for k in range(KD):
                    if k >= 4:
                        pe.wait_ge(h_evac_v, at_h[n] + k - 3)
                        pe.wait_ge(h_evac_a, at_h[n] + k - 3)
                    b = 2 * (k % 4)
                    for t in range(NT):
                        dst = PS[:, b, 0:P] if t == 0 else PS[:, b + 1, (t - 1) * P:t * P]
                        last = nc.tensor.transpose(dst, x[:, t, k * P:(k + 1) * P], ident[:])
                    done(last, ("h", n, k))
                pe.wait_ge(h_evac_v, at_h[n] + KD)
                pe.wait_ge(h_evac_a, at_h[n] + KD)

            at_h = {0: 0, 4: KD, 1: 2 * KD, 2: 3 * KD, 3: 4 * KD}

            def feature_major(w, m, pair):
                for half in range(2):
                    for k in range(KD):
                        last = nc.tensor.matmul(PS[:, 2 * pair + half, 0:HT], w[:, k, m * P:(m + 1) * P],
                                                hT[:, k, half * HT:(half + 1) * HT], start=(k == 0), stop=(k == KD - 1))
                return last

            def even():
                modulated(0)
                pe.wait_ge(ev_consts, 1)

                def pair_of(kind, fam, m):
                    i = proj_count[kind, fam, m][0]
                    if i >= 4:
                        evacuated(*proj[i - 4][:3])
                    return i % 4

                for fam in range(2):
                    if fam == 0:
                        w = take(a["w_gate"]).rearrange("p (k n) -> p k n", k=KD)
                        done(feature_major(w, 0, pair_of("gate", 0, 0)), ("gate",))
                        release(("gate",))
                    else:
                        pe.wait_ge(h_done, NU)
                        pe.wait_ge(state_ready, NU - 2 * NH)
                    for kind in ("q", "k"):
                        for i in range(NH):
                            if i % 2 == 0:
                                w = take(a["w_even"][fam, {"q": 0, "k": 1}[kind], i // 2]).rearrange("p (k n) -> p k n", k=KD)
                            done(feature_major(w, i % 2, pair_of(kind, fam, i)), (kind, fam, i))
                            release((kind, fam, i))
                    for kind in ("v", "o"):
                        for s in range(2):
                            w = take(a["w_even"][fam, {"v": 2, "o": 3}[kind], s]).rearrange("p (k n) -> p k n", k=KD)
                            for t in range(NT):
                                pr = pair_of(kind, fam, (s, t))
                                for k in range(KD):
                                    last = nc.tensor.matmul(PS[:, 2 * pr, 0:SLICE], hT[:, k, t * P:(t + 1) * P], w[:, k, :],
                                                            start=(k == 0), stop=(k == KD - 1))
                                done(last, (kind, fam, (s, t)))
                            release((kind, fam, (s, NT - 1)))
                    if fam == 0:
                        pe.wait_ge(gates_done, 1)
                        evacuated("o", 0, (1, NT - 1))
                        evacuated("v", 0, (1, NT - 1))
                        for t in range(NT):
                            for kind in range(4):
                                for d in range(2):
                                    c = ((t * 4 + kind) * 2 + d) * NH
                                    last = nc.tensor.matmul(PS[:, 7, c:c + NH], grow[:, kind, d, t * P:(t + 1) * P],
                                                            ident[0:NH, 0:NH], start=True, stop=True)
                        for h in range(NH):
                            last = nc.tensor.matmul(PS[:, 7, 256 + h * 2 * NT:256 + (h + 1) * 2 * NT], sel4[:, h, :],
                                                    DEC_.rearrange("p d t -> p (d t)"), start=True, stop=True)
                        done(last, ("cols",))
                        pe.wait_ge(cols_ready, 1)
                    evacuated("k", fam, NH - 1)
                    for t in range(NT):
                        pr = pair_of("kt", fam, t)
                        for h in range(NH):
                            last = nc.tensor.transpose(PS[:, 2 * pr, h * P:(h + 1) * P], kT[:, h, t * P:(t + 1) * P], ident[:])
                        done(last, ("kt", fam, t))
                    evacuated("kt", fam, NT - 1)
                    evacuated("o", fam, (1, NT - 1))
                    evacuated("v", fam, (1, NT - 1))
                    width = DH + 1 if fam == 0 else DH
                    for i in range(NU + 2):
                        if i < NU:
                            s, h, d = UNITS[i]
                            t = tile_of(s, d)
                            if i >= 2:
                                pe.wait_ge(p_ready, fam * NU + i - 1)
                            last = nc.tensor.matmul(PS[:, i % 2, 0:P], kT[:, h, t * P:(t + 1) * P], qT[:, h, t * P:(t + 1) * P],
                                                    start=True, stop=True)
                            if fam == 0:
                                last = nc.tensor.matmul(PS[:, i % 2, P:2 * P], sel4[:, h, :], row[:, d, t * P:(t + 1) * P],
                                                        start=True, stop=True)
                            done(last, ("S", fam, i))
                        u = i - 2
                        if u >= 0:
                            s, h, d = UNITS[u]
                            t = tile_of(s, d)
                            pe.wait_ge(p_ready, fam * NU + u + 1)
                            if u >= 2:
                                pe.wait_ge(h_done, fam * NU + u - 1)
                            if s < NT - 1:
                                pe.wait_ge(kw_ready, fam * (NU - 2 * NH) + u + 1)
                                last = nc.tensor.matmul(PS[:, 4 + u % 2, 0:width], kw[:, u % 2, :], v1[:, t, h, 0:width],
                                                        start=True, stop=True)
                            if s > 0:
                                pe.wait_ge(even_loaded, 80)
                                if fam == 1:
                                    pe.wait_ge(ret_ready, 16)
                                if s > 1:
                                    pe.wait_ge(state_ready, fam * (NU - 2 * NH) + u - 2 * NH + 1)
                                nc.tensor.matmul(PS[:, 2 + u % 2, 256:256 + width], qT[:, h, t * P:(t + 1) * P],
                                                 Cst[:, d, h, 0:width], start=True, stop=True)
                            last = nc.tensor.matmul(PS[:, 2 + u % 2, 0:width], pb[:, u % 2, :], v1[:, t, h, 0:width],
                                                    start=True, stop=True)
                            done(last, ("H", fam, u))
                pe.wait_ge(norm_done, 2)
                for k in range(KD):
                    if k >= 4:
                        pe.wait_ge(h_evac_v, at_h[4] + k - 3)
                        pe.wait_ge(h_evac_a, at_h[4] + k - 3)
                    b = 2 * (k % 4)
                    for t in range(NT):
                        dst = PS[:, b, 0:P] if t == 0 else PS[:, b + 1, (t - 1) * P:t * P]
                        last = nc.tensor.transpose(dst, f[:, t, k * P:(k + 1) * P], ident[:])
                    done(last, ("h", 4, k))
                pe.wait_ge(h_evac_v, at_h[4] + KD)
                pe.wait_ge(h_evac_a, at_h[4] + KD)
                g = 0
                for s in range(D // SLICE):
                    w = take(a["w_eout"][s]).rearrange("p (k n) -> p k n", k=KD)
                    for t in range(NT):
                        if g >= 8:
                            pe.wait_ge(out_evac, g - 7)
                        for k in range(KD):
                            last = nc.tensor.matmul(PS[:, g % 8, 0:SLICE], hT[:, k, t * P:(t + 1) * P], w[:, k, :],
                                                    start=(k == 0), stop=(k == KD - 1))
                        done(last, ("eo", s, t))
                        g += 1
                    release(("eo", s, NT - 1))

            def peer(l):
                modulated(2 * l + 1)
                sc = 0
                for m in range(2 * H_P):
                    if m % 2 == 0:
                        w = take(a["w_pq"][l, m // 2]).rearrange("p (k n) -> p k n", k=KD)
                    g = l * 2 * H_P + m
                    if m >= 2:
                        pe.wait_ge(q_evac, g - 1)
                    done(feature_major(w, m % 2, m % 2), ("pq", l, m))
                    if m % 2 == 1:
                        release(("pq", l, m))
                    if m == 0:
                        pe.wait_ge(keys_loaded, 16 * (l + 1))
                    pe.wait_ge(q_evac, g + 1)
                    if m >= 2:
                        pe.wait_ge(s_used, NT * (g - 1))
                    for t in range(NT):
                        b = 4 + 2 * (m % 2) + (t == NT - 1)
                        last = nc.tensor.matmul(PS[:, b, (t % 4) * P:(t % 4 + 1) * P], qb[:, m % 2, t * P:(t + 1) * P],
                                                keys[:, m, :], start=True, stop=True)
                    done(last, ("ps", l, m))
                base_n, base_s = state["n"], state["slice"]

                def act_pass(i, build, n0):
                    for jj in range(16):
                        gj = l * N_KEYS + i * 16 + jj
                        if jj % 2 == 0:
                            n = base_s + jj // 2
                            pe.wait_ge(slot_full[n % NSLOT], 16 * (n // NSLOT + 1) + 16 * i)
                            w = ring[:, n % NSLOT, :].rearrange("p (k n) -> p k n", k=KD)
                        if isinstance(i, int) and i == 0 and jj < 2 and l == 0:
                            pass
                        else:
                            pe.wait_ge(act_gelu, gj - 1)
                        last = feature_major(w, jj % 2, jj % 2)
                        last.then_inc(products, 1)
                        if build:
                            q = (i - 3) * 16 + jj
                            gq = l * 80 + q
                            pe.wait_ge(hot_ready, gq + 1)
                            if not (isinstance(i, int) and l == 0 and i == 3 and jj < 2):
                                pe.wait_ge(g_evac, gq - 1)
                            for tk in range(8):
                                b = 4 + 2 * (jj % 2) + tk // 4
                                last = nc.tensor.matmul(PS[:, b, (tk % 4) * P:(tk % 4 + 1) * P], hot[:, jj % 2, 0, tk, :],
                                                        hot[:, jj % 2, 1, tk, :], start=True, stop=True)
                            last.then_inc(products, 1)

                act_pass(0, False, 0)
                with pe.Fori(1, 3) as i:
                    act_pass(i, False, 0)
                n_tr = base_n + 3 * 16
                for t in range(NT):
                    if t == 0:
                        pe.wait_ge(hk_ready, l + 1)
                    if t >= 2:
                        pe.wait_ge(hk_evac, l * NT + t - 1)
                    for c in range(3):
                        last = nc.tensor.transpose(PS[:, 4 + t % 2, c * P:(c + 1) * P], hkt[:, t, c, :], ident[:])
                    last.then_inc(products, 1)
                    at["hk", l, t] = n_tr + t + 1
                pe.wait_ge(hk_evac, l * NT + NT)
                n_b = n_tr + NT
                at["u", l], at["ub", l] = base_n, n_b
                act_pass(3, True, n_b)
                with pe.Fori(4, 8) as i:
                    act_pass(i, True, n_b)
                state["n"] = n_b + 5 * 32
                state["slice"] = base_s + 64
                slices.append(["U", l, base_n, n_b])
                base_n, base_s = state["n"], state["slice"]
                at["v", l] = base_n

                def value_pass(i):
                    for half in range(2):
                        blk = 2 * i + half
                        for q in range(4):
                            n = base_s + 4 * half + q
                            pe.wait_ge(slot_full[n % NSLOT], 16 * (n // NSLOT + 1) + 16 * i)
                        pe.wait_ge(w_ready, l * NBLK + blk + 1)
                        for t in range(NT):
                            g = half * NT + t
                            pr = g % 2
                            gg = l * NBLK * NT + blk * NT + t
                            first = isinstance(i, int) and half == 0 and t < 2
                            if not (first and l == 0):
                                pe.wait_ge(acc_done, gg - 1)
                            for c in range(2):
                                for j in range(JB):
                                    n = (base_s + 4 * half + j // 2) % NSLOT
                                    v = ring[:, n, (j % 2) * D + c * 512:(j % 2) * D + (c + 1) * 512]
                                    last = nc.tensor.matmul(PS[:, 2 * pr + c, :], ab[half][:, j, t * P:(t + 1) * P], v,
                                                            start=(j == 0), stop=(j == JB - 1))
                            last.then_inc(products, 1)

                value_pass(0)
                with pe.Fori(1, NBLK // 2) as i:
                    value_pass(i)
                state["n"] = base_n + NBLK * NT
                state["slice"] = base_s + 64
                slices.append(["V", l, base_n])

            def odd():
                modulated(2)
                w = take(a["w_dt"]).rearrange("p (k n) -> p k n", k=KD)
                for t in range(NT):
                    for k in range(KD):
                        last = nc.tensor.matmul(PS[:, 0, t * 64:(t + 1) * 64], hT[:, k, t * P:(t + 1) * P], w[:, k, 0:64],
                                                start=(k == 0), stop=(k == KD - 1))
                done(last, ("dt",))
                release(("dt",))
                pe.wait_ge(a_ready, 1)
                for t in range(NT):
                    for d in range(2):
                        c = (t * 2 + d) * H_C
                        nc.tensor.matmul(PS[:, 1, c:c + H_C], tri[:, d, :], av[:, t, d, :], start=True, stop=True)
                last = nc.tensor.matmul(PS[:, 2, 0:NT * 64], ones[:], av[:].rearrange("p t d h -> p (t d h)"), start=True, stop=True)
                done(last, ("acum",))
                pe.wait_ge(ac_ready, 1)
                for g in range(G_C):
                    for m in range(7):
                        q = g * 6 + m
                        if m < 6:
                            if m % 2 == 0:
                                w = take(a["w_xbc"][g, m // 2]).rearrange("p (k n) -> p k n", k=KD)
                            if q >= 2:
                                pe.wait_ge(pad_filled, q - 1)
                            b = 2 * (m % 2)
                            for k in range(KD):
                                nc.tensor.matmul(PS[:, b, 0:P], w[:, k, (m % 2) * P:(m % 2 + 1) * P], hT[:, k, 0:P],
                                                 start=(k == 0), stop=(k == KD - 1))
                            for k in range(KD):
                                last = nc.tensor.matmul(PS[:, b + 1, :], w[:, k, (m % 2) * P:(m % 2 + 1) * P], hT[:, k, P:T],
                                                        start=(k == 0), stop=(k == KD - 1))
                            done(last, ("xbc", g, m))
                            if m % 2 == 1:
                                release(("xbc", g, m))
                        mm = m - 1
                        if 0 <= mm < 5:
                            qq = g * 6 + mm
                            src = sx[:, mm % 2, :] if mm < 4 else BC[:, 0, :]
                            pe.wait_ge(act_done, qq + 1)
                            n = g * 5 + mm
                            if n >= 2:
                                pe.wait_ge(tr_evac, n - 1)
                            for t in range(NT):
                                b = 4 + 2 * (n % 2) + (t == NT - 1)
                                last = nc.tensor.transpose(PS[:, b, (t % 4) * P:(t % 4 + 1) * P], src[:, t * P:(t + 1) * P], ident[:])
                            done(last, ("xt", g, mm))
                    pe.wait_ge(act_done, g * 6 + 6)
                    pe.wait_ge(pad_filled, g * 6 + 6)
                    pe.wait_ge(tr_evac, g * 5 + 5)
                    for t in range(NT):
                        n = g * NT + t
                        if n >= 1:
                            pe.wait_ge(op_ready, 2 * n)
                        nc.tensor.matmul(PS[:, 4, 0:P], BC[:, 0, t * P:(t + 1) * P], BC[:, 1, t * P:(t + 1) * P], start=True, stop=True)
                        for d in range(2):
                            if 2 * n + d >= 1:
                                pe.wait_ge(oe_ready, 2 * n + d)
                            for j in range(J_C):
                                last = nc.tensor.matmul(PS[:, 5 + j // 4, (j % 4) * P:(j % 4 + 1) * P],
                                                        av[:, t, d, g * J_C + j:g * J_C + j + 1].broadcast_to([P, P]),
                                                        tri[:, d, :], start=True, stop=True)
                            done(last, ("seg", g, t, d))
                        pe.wait_ge(op_ready, 2 * n + 2)
                        if n >= 1:
                            pe.wait_ge(y_intra, n)
                        for j in range(J_C):
                            for d in range(2):
                                last = nc.tensor.matmul(PS[:, 7, j * P_C:(j + 1) * P_C], EP[:, d, j, :], xs[:, t, j * P_C:(j + 1) * P_C],
                                                        start=(d == 0), stop=(d == 1))
                        done(last, ("intra", g, t))
                    pe.wait_ge(y_intra, g * NT + NT)
                    pe.wait_ge(hst_loaded, 16 * (g + 1))
                    for s in range(NT):
                        for d in range(2):
                            t = tile_of(s, d)
                            n, nu = (g * 4 + s - 1) * 2 + d, (g * 4 + s) * 2 + d
                            if s > 0:
                                if n >= 1:
                                    pe.wait_ge(inter_done, n)
                                if s > 1:
                                    pe.wait_ge(upd_done, nu - 1)
                                last = nc.tensor.matmul(PS[:, n % 2, :], BC[:, 1, t * P:(t + 1) * P], hst[:, d, :], start=True, stop=True)
                                done(last, ("inter", g, s, d))
                            if s < NT - 1:
                                pe.wait_ge(xw_ready, nu + 1)
                                if nu >= 1:
                                    pe.wait_ge(upd_done, nu)
                                last = nc.tensor.matmul(PS[:, 2 + nu % 2, :], Btok[:, t, :], xw[:, :], start=True, stop=True)
                                done(last, ("upd", g, s, d))
                    pe.wait_ge(inter_done, (g + 1) * 8)
                    pe.wait_ge(upd_done, (g + 1) * 8)
                for s in range(D_INNER // SLICE):
                    w = take(a["w_z"][s]).rearrange("p (k n) -> p k n", k=KD)
                    for t in range(NT):
                        n = s * NT + t
                        if n >= 4:
                            pe.wait_ge(z_silu, n - 3)
                        for k in range(KD):
                            last = nc.tensor.matmul(PS[:, n % 4, 0:SLICE], hT[:, k, t * P:(t + 1) * P], w[:, k, :],
                                                    start=(k == 0), stop=(k == KD - 1))
                        done(last, ("z", s, t))
                    release(("z", s, NT - 1))
                pe.wait_ge(z_used, D_INNER // SLICE * NT)
                for k in range(2 * KD):
                    if k >= 4:
                        pe.wait_ge(yt_v, k - 3)
                        pe.wait_ge(yt_a, k - 3)
                    b = 2 * (k % 4)
                    for t in range(NT):
                        dst = PS[:, b, 0:P] if t == 0 else PS[:, b + 1, (t - 1) * P:t * P]
                        last = nc.tensor.transpose(dst, y[:, t, k * P:(k + 1) * P], ident[:])
                    done(last, ("yt", k))
                pe.wait_ge(yt_v, 2 * KD)
                pe.wait_ge(yt_a, 2 * KD)
                for s in range(KD):
                    w = take(a["w_oout"][s]).rearrange("p (k n) -> p k n", k=2 * KD)
                    for t in range(NT):
                        n = s * NT + t
                        if n >= 8:
                            pe.wait_ge(oo_evac, n - 7)
                        for k in range(2 * KD):
                            last = nc.tensor.matmul(PS[:, n % 8, 0:P], yT[:, k, t * P:(t + 1) * P], w[:, k, :],
                                                    start=(k == 0), stop=(k == 2 * KD - 1))
                        done(last, ("oo", s, t))
                    release(("oo", s, NT - 1))

            if "even" in run:
                even()
            if "peer0" in run:
                peer(0)
            if "odd" in run:
                odd()
            if "peer1" in run:
                peer(1)

        @block.vector
        def _(ve):
            V = nc.vector
            ch = Chain(ve, vec_chain)
            do, link, settle = ch.do, ch.link, ch.settle

            def bank(b):
                return PS[:, b, :]

            ve.wait_ge(x_loaded, 48)
            V.tensor_tensor(x[:, 1:NT, :], x[:, 1:NT, :], f[:, 0:NT - 1, :], ALU.add).then_inc(x_ready, 1)
            ve.wait_ge(small_loaded, 32)
            for l in range(DEPTH):
                if l:
                    ve.wait_ge(gates_stored, 32 * l)
                    ve.wait_ge(small_loaded, 32 + 16 * l)
                for s in range(NMOD // SLICE):
                    ve.wait_ge(products, at["mod", l, s])
                    c = slice(s * SLICE, (s + 1) * SLICE)
                    V.tensor_tensor(mrow[:, c], PS[0:2, (l * 24 + s) % 4, 0:SLICE], bmod[:, c], ALU.add).then_inc(mod_evac, 1)
                ve.wait_ge(mod_evac, (l + 1) * (NMOD // SLICE))
                do(V.tensor_scalar(mrow[:, D:2 * D], mrow[:, D:2 * D], 1.0, None, ALU.add))
                V.tensor_scalar(mrow[:, 4 * D:5 * D], mrow[:, 4 * D:5 * D], 1.0, None, ALU.add).then_inc(mod_rows, 1)
                ve.wait_ge(products, at["fold", l])
                V.tensor_copy(modT[:, l].rearrange("p a k g -> p (a k g)"), PS[:, 4, 0:64]).then_inc(mod_cols, 1)

            def modulated(n):
                l, kind = n // 2, 2 * (n % 2)
                ve.wait_ge(mod_cols, l + 1)
                for k in range(KD):
                    ve.wait_ge(products, at["h", n, k])
                    V.tensor_scalar(hT[:, k, P:T], PS[:, 2 * (k % 4) + 1, :], modT[:, l, kind + 1, k, 1:2], modT[:, l, kind, k, 1:2],
                                    ALU.mult, ALU.add).then_inc(h_evac_v, 1)

            def layer_norm(n, rows):
                ve.wait_ge(rows_loaded, 48 * (n + 1))
                settle()
                for t in range(NT):
                    do(V.tensor_tensor(f[:, t, :], f[:, t, :], rows[:, 2 + (t > 0), :], ALU.mult))
                settle()
                for t in range(NT):
                    do(V.scalar_tensor_tensor(x[:, t, :], x[:, t, :], ALPHA, f[:, t, :], ALU.mult, ALU.add))
                settle()
                for t in range(NT):
                    for c in range(2):
                        do(V.bn_stats(stat[:, 2 * t + c, :], x[:, t, c * 512:(c + 1) * 512]))
                settle()
                for t in range(NT):
                    last = V.bn_aggr(mv[:, t, :], stat[:, 2 * t:2 * t + 2, :])
                    if t < NT - 1:
                        do(last)
                last.then_inc(var_ready, 1)
                ve.wait_ge(dev_ready, at_dev[n])
                link(V.reciprocal(rstd[:, 0:NT], rstd[:, 0:NT]))
                for t in range(NT):
                    do(V.tensor_scalar(x[:, t, :], x[:, t, :], mv[:, t, 0:1], rstd[:, t:t + 1], ALU.subtract, ALU.mult))
                settle()
                for t in range(NT):
                    do(V.tensor_tensor(x[:, t, :], x[:, t, :], rows[:, 0, :], ALU.mult))
                settle()
                for t in range(NT):
                    last = V.tensor_tensor(x[:, t, :], x[:, t, :], rows[:, 1, :], ALU.add)
                    if t < NT - 1:
                        do(last)
                last.then_inc(x_ready, 1)
                ve.wait_ge(x_ready, n + 2)

            at_dev = {0: 3, 1: 4, 2: 5, 3: 6}

            def even():
                modulated(0)
                ve.wait_ge(even_loaded, 80)
                ve.wait_ge(ev_consts, 1)
                ve.wait_ge(products, at["gate",])
                L, F, t1, t2 = (grow[:, i] for i in range(4))
                wg_, wint_, col_, enm_ = L, F, t1, t2
                b, m = b_m[:, 0], b_m[:, 1]
                dst = [L[:, 0], L[:, 1], F[:, 0], F[:, 1]]
                for q in range(4):
                    last = V.tensor_copy(dst[q].rearrange("p (a t) -> p a t", a=2), PS[32 * q:32 * q + NH, 0:2, 0:HT])
                    if q < 3:
                        do(last)
                last.then_inc(proj_v, 1)
                ve.wait_ge(proj_v, 1)
                for q in range(4):
                    do(V.tensor_scalar(dst[q], dst[q], gbias[:, q:q + 1], None, ALU.add))
                settle()
                V.scalar_tensor_tensor(t1, F, -1.0, F, ALU.mult, ALU.max).then_inc(gate_exp, 1)
                ve.wait_ge(gate_act, 1)
                link(V.scalar_tensor_tensor(F, F, 0.0, t1, ALU.min, ALU.subtract))
                do(V.memset(t2[:, :, 0:P], 1.0))
                settle()
                for t in range(NT):
                    c = slice(t * P, (t + 1) * P)
                    do(V.tensor_tensor_scan(b[:, 0, c], t2[:, 0, 0:P], F[:, 0, c], 0.0, ALU.mult, ALU.add))
                    r = F[:, 1, c]
                    do(V.tensor_tensor_scan(b[:, 1, c][:, ::-1], t2[:, 1, 0:P], r[:, ::-1], 0.0, ALU.mult, ALU.add))
                for c, start in ((slice(0, P), None), (slice(P, T), m0)):
                    do(V.tensor_tensor_scan(m[:, 0, c], F[:, 0, c], L[:, 0, c], 0.0 if start is None else start[:, 0:1], ALU.add, ALU.max))
                    do(V.tensor_tensor_scan(m[:, 1, c][:, ::-1], F[:, 1, c][:, ::-1], L[:, 1, c][:, ::-1],
                                            0.0 if start is None else start[:, 1:2], ALU.add, ALU.max))
                settle()
                for src, dst_ in ((b, BE), (m, ML)):
                    do(V.tensor_copy(dst_[:, 0, :], src[:, 0, :].rearrange("p (n t) -> p n t", t=P)[:, :, P - 1]))
                    do(V.tensor_copy(dst_[:, 1, :], src[:, 1, :].rearrange("p (n t) -> p n t", t=P)[:, :, 0]))
                do(V.memset(MP[:, :, 0], 0.0))
                do(V.tensor_copy(MP[:, 0, 1:2], m0[:, 0:1]))
                do(V.tensor_copy(MP[:, 1, NT - 1:NT], m0[:, 1:2]))
                settle()
                do(V.tensor_copy(MP[:, 0, 2:NT], ML[:, 0, 1:NT - 1]))
                do(V.tensor_copy(MP[:, 1, 1:NT - 1], ML[:, 1, 2:NT]))
                do(V.tensor_tensor(row[:, :, :], b, m, ALU.subtract))
                do(V.tensor_tensor(col_, L, b, ALU.subtract))
                settle()
                do(V.tensor_tensor(BM, BE, ML, ALU.subtract))
                settle()
                chunked = lambda z: z.rearrange("p d (n t) -> p (d n) t", t=P)
                flat = lambda z: z.rearrange("p d n -> p (d n)")
                do(V.tensor_tensor(chunked(F), chunked(row[:, :, :]), bc(flat(MP), P), ALU.add))
                do(V.tensor_tensor(chunked(L), chunked(col_), bc(flat(BM), P), ALU.add))
                V.tensor_tensor(DEC_, BM, MP, ALU.add).then_inc(gate_exp, 1)
                do(V.memset(v1[:, :, :, DH:DH + 1], 1.0))

                for fam in range(2):
                    for s in range(2):
                        for t in range(NT):
                            ve.wait_ge(products, at["v", fam, (s, t)])
                            V.tensor_copy(v1[:, t, 2 * s:2 * s + 2, 0:DH],
                                          PS[:, 2 * (proj_count["v", fam, (s, t)][0] % 4), 0:SLICE].rearrange("p (h d) -> p h d", h=2)
                                          ).then_inc(proj_v, 1)
                    if fam == 0:
                        ve.wait_ge(products, at["cols",])
                        do(V.tensor_copy(cols[:].rearrange("p n k d h -> p (n k d h)"), PS[:, 7, 0:160]))
                        V.tensor_copy(decB[:].rearrange("p h d n -> p (h d n)"), PS[:, 7, 256:296]).then_inc(cols_ready, 1)
                        ve.wait_ge(cols_ready, 1)
                    else:
                        ve.wait_ge(diff_ready, 1)
                        link(V.tensor_scalar(lg[:].rearrange("p d h -> p (d h)"), lg[:].rearrange("p d h -> p (d h)"), -1.0, None, ALU.mult))
                        for kind in range(2):
                            for d in range(2):
                                do(V.tensor_scalar(xz[:, kind, d, :], lg[:, d, :], icol[:, 2 * kind + d:2 * kind + d + 1], None, ALU.mult))
                        V.tensor_scalar(xz[:, 2], lg[:], float(P), None, ALU.mult).then_inc(decay_ready, 1)
                        ve.wait_ge(ret_ready, 16)
                        ve.wait_ge(stored, 32)
                        ve.wait_ge(dm_ready, 1)
                    for t in range(NT):
                        ve.wait_ge(products, at["kt", fam, t])
                        if fam == 1 and t == 0:
                            ve.wait_ge(kw_ready, NU - 2 * NH)
                        V.tensor_copy(ktok[:, t].rearrange("p h d -> p (h d)"), PS[:, 2 * (proj_count["kt", fam, t][0] % 4), :]).then_inc(proj_v, 1)
                    for i in range(NU + 3):
                        if i < NU:
                            s, h, d = UNITS[i]
                            t = tile_of(s, d)
                            ve.wait_ge(products, at["S", fam, i])
                            if fam == 0:
                                if i >= 2:
                                    ve.wait_ge(p_ready, i - 1)
                                V.scalar_tensor_tensor(eb[:, i % 2, :], PS[:, i % 2, P:2 * P], cols[:, t, 2, d, h:h + 1], mask[:, d, :],
                                                       ALU.add, ALU.add).then_inc(e_ready, 1)
                        u = i - 1
                        if 0 <= u < NU:
                            s, h, d = UNITS[u]
                            if u >= 2:
                                ve.wait_ge(products, at["H", fam, u - 2])
                            if fam == 0:
                                ve.wait_ge(exp_ready, u + 1)
                                w = eb[:, u % 2, :]
                            else:
                                w = Dm[:, d, h, :]
                            V.tensor_tensor(pb[:, u % 2, :], w, PS[:, u % 2, 0:P], ALU.mult).then_inc(p_ready, 1)
                        u = i - 3
                        if u < 0:
                            continue
                        s, h, d = UNITS[u]
                        t = tile_of(s, d)
                        ve.wait_ge(products, at["H", fam, u])
                        width = DH + 1 if fam == 0 else DH
                        U = PS[:, 4 + u % 2, 0:width]
                        num, inter = PS[:, 2 + u % 2, 0:width], PS[:, 2 + u % 2, 256:256 + width]
                        ndu = nd[:, u % 2, :]
                        out = f[:, t, fam * W_A + h * DH:fam * W_A + (h + 1) * DH]
                        if s > 0:
                            w = cols[:, t, 1, d, h:h + 1] if fam == 0 else xz[:, 0, d, h:h + 1]
                            do(V.tensor_scalar(ndu[:, 0:width], inter, w, None, ALU.mult))
                        if s == 0:
                            V.tensor_copy(Cout[:, d, h, 0:width], U).then_inc(state_ready, 1)
                        elif s < NT - 1:
                            w = decB[:, h, d, t:t + 1] if fam == 0 else xz[:, 2, d, h:h + 1]
                            V.scalar_tensor_tensor(Cst[:, d, h, 0:width], Cst[:, d, h, 0:width], w, U, ALU.mult, ALU.add).then_inc(state_ready, 1)
                        settle()
                        if s > 0:
                            link(V.tensor_tensor(ndu[:, 0:width], ndu[:, 0:width], num, ALU.add))
                        else:
                            link(V.tensor_copy(ndu[:, 0:width], num))
                        if fam == 0:
                            link(V.scalar_tensor_tensor(ndu[:, DH + 1:DH + 2], ndu[:, DH:DH + 1], -1.0, ndu[:, DH:DH + 1], ALU.mult, ALU.max))
                            link(V.tensor_scalar(ndu[:, DH + 1:DH + 2], ndu[:, DH + 1:DH + 2], cols[:, t, 3, d, h:h + 1], None, ALU.max))
                            link(V.reciprocal(ndu[:, DH + 1:DH + 2], ndu[:, DH + 1:DH + 2]))
                            if first_on(s, d):
                                V.tensor_scalar(out, ndu[:, 0:DH], ndu[:, DH + 1:DH + 2], None, ALU.mult).then_inc(h_done, 1)
                            else:
                                V.scalar_tensor_tensor(out, ndu[:, 0:DH], ndu[:, DH + 1:DH + 2], out, ALU.mult, ALU.add).then_inc(h_done, 1)
                        elif first_on(s, d):
                            V.tensor_copy(out, ndu[:, 0:DH]).then_inc(h_done, 1)
                        else:
                            V.tensor_tensor(out, ndu[:, 0:DH], out, ALU.add).then_inc(h_done, 1)
                        ve.wait_ge(h_done, fam * NU + u + 1)
                    hv = lambda t, h: f[:, t, fam * W_A + h * DH:fam * W_A + (h + 1) * DH]
                    for t in range(NT):
                        for h in range(NH):
                            do(V.bn_stats(stat[:, t * NH + h, :], hv(t, h)))
                    settle()
                    for i in range(NT * NH):
                        last = V.bn_aggr(mv[:, i, :], stat[:, i:i + 1, :])
                        if i < NT * NH - 1:
                            do(last)
                    last.then_inc(var_ready, 1)
                    ve.wait_ge(dev_ready, fam + 1)
                    link(V.reciprocal(rstd[:], rstd[:]))
                    for t in range(NT):
                        for h in range(NH):
                            i = t * NH + h
                            do(V.tensor_scalar(hv(t, h), hv(t, h), mv[:, i, 0:1], rstd[:, i:i + 1], ALU.subtract, ALU.mult))
                    settle()
                    ve.wait_ge(og_ready, fam + 1)
                    V.tensor_tensor(f[:, :, fam * W_A:(fam + 1) * W_A], f[:, :, fam * W_A:(fam + 1) * W_A], og, ALU.mult).then_inc(norm_done, 1)
                    ve.wait_ge(norm_done, fam + 1)
                for k in range(KD):
                    ve.wait_ge(products, at["h", 4, k])
                    V.tensor_copy(hT[:, k, P:T], PS[:, 2 * (k % 4) + 1, :]).then_inc(h_evac_v, 1)
                ve.wait_ge(out_evac, D // SLICE * NT)
                layer_norm(0, rowsB)

            def peer(l):
                modulated(2 * l + 1)
                ve.wait_ge(iota_ready, l + 1)
                for m in range(2 * H_P):
                    for t in range(NT):
                        if t == 0:
                            ve.wait_ge(products, at["ps", l, m])
                        sc_ = PS[:, 4 + 2 * (m % 2) + (t == NT - 1), (t % 4) * P:(t % 4 + 1) * P]
                        v_, i_ = sv[:, t, m // 2, m % 2, :], si[:, t, m // 2, m % 2, :]
                        link(V.max(v_[:, 0:8], sc_))
                        do(V.max_index(i_[:, 0:8], v_[:, 0:8], sc_))
                        V.match_replace(swork[:], v_[:, 0:8], sc_, NEG).then_inc(s_used, 1)
                        ve.wait_ge(s_used, NT * (l * 2 * H_P + m) + t + 1)
                        link(V.max(v_[:, 8:16], swork[:]))
                        link(V.max_index(i_[:, 8:16], v_[:, 8:16], swork[:]))
                for t in range(NT):
                    hk = hkt[:, t]
                    bt = best[:, t]
                    for h in range(H_P):
                        cd = cand[:, 0, :].rearrange("p (a b) -> p a b", b=TOPK)
                        link(V.tensor_tensor(cd, bc(sv[:, t, h, 0, :], TOPK), sv[:, t, h, 1, :].unsqueeze(1).broadcast_to([P, TOPK, TOPK]), ALU.add))
                        link(V.max(bt[:, h, 0:8], cand[:, 0, :]))
                        do(V.max_index(pos[:, h, 0:8], bt[:, h, 0:8], cand[:, 0, :]))
                        link(V.match_replace(cand[:, 1, :], bt[:, h, 0:8], cand[:, 0, :], NEG))
                        link(V.max(bt[:, h, 8:16], cand[:, 1, :]))
                        link(V.max_index(pos[:, h, 8:16], bt[:, h, 8:16], cand[:, 1, :]))
                    link(V.tensor_copy(ssum[:, t, :], bt[:, :, 0]))
                    link(V.tensor_tensor(bt, bt, bc(ssum[:, t, :], TOPK), ALU.subtract))
                    pf = pos[:].rearrange("p h k -> p (h k)")
                    do(V.tensor_scalar(posi[:, 0, :], pf, 4, None, ALU.logical_shift_right))
                    do(V.tensor_scalar(posi[:, 1, :], pf, 15, None, ALU.bitwise_and))
                    do(V.tensor_copy(sif[:].rearrange("p h c k -> p (h c k)"), si[:, t].rearrange("p h c k -> p (h c k)")))
                    settle()
                    link(V.tensor_copy(posf[:], posi[:]))
                    for c in range(2):
                        link(V.tensor_tensor(eqb, bc(posf[:, c, :], TOPK), iota[:, 0:TOPK].unsqueeze(1).broadcast_to([P, HK, TOPK]), ALU.is_equal))
                        link(V.tensor_tensor(eqc.rearrange("p (h k) b -> p h k b", h=H_P), eqb.rearrange("p (h k) b -> p h k b", h=H_P),
                                             sif[:, :, c, :].unsqueeze(2).broadcast_to([P, H_P, TOPK, TOPK]), ALU.mult))
                        link(V.tensor_reduce(hk[:, c, :], eqc, AX, ALU.add))
                V.tensor_copy(ssum[:, 0, 0:1], best[:, 0, 0, 0:1]).then_inc(sm_sub, 1)
                ve.wait_ge(sm_exp, l + 1)
                link(V.tensor_reduce(ssum[:], best[:], AX, ALU.add))
                link(V.reciprocal(ssum[:], ssum[:]))
                for t in range(NT):
                    last = V.tensor_tensor(hkt[:, t, 2, :].rearrange("p (h k) -> p h k", h=H_P), best[:, t], bc(ssum[:, t, :], TOPK), ALU.mult)
                    if t < NT - 1:
                        do(last)
                last.then_inc(hk_ready, 1)
                for t in range(NT):
                    ve.wait_ge(products, at["hk", l, t])
                    V.tensor_copy(hkT[:, :, t * P:(t + 1) * P], PS[:, 4 + t % 2, 0:3 * P].rearrange("p (c t) -> p c t", c=3)).then_inc(hk_evac, 1)
                ve.wait_ge(hk_evac, l * NT + NT)

                def hots(it):
                    for half in range(2):
                        q = 2 * it + half
                        gq = l * 80 + q
                        if not (isinstance(it, int)):
                            pe_n = at["ub", l] + 4 * (it - 1) + 2 * half + 2
                            ve.wait_ge(products, pe_n)
                        for tk in range(8):
                            col = 8 * q + tk if isinstance(it, int) else bass.ds(16 * it + 8 * half + tk, 1)
                            if isinstance(it, int):
                                ci, cj, cg = (hkT[:, c, col:col + 1] for c in range(3))
                            else:
                                ci, cj, cg = (hkT[:, c, col] for c in range(3))
                            do(V.tensor_scalar(hot[:, half, 0, tk, :], iota[:], ci, None, ALU.is_equal))
                            last = V.tensor_scalar(hot[:, half, 1, tk, :], iota[:], cj, cg, ALU.is_equal, ALU.mult)
                            if tk < 7:
                                do(last)
                        last.then_inc(hot_ready, 1)

                hots(0)
                n0 = ch.n
                with ve.Fori(1, 40) as it:
                    hots(it)
                ch.n = n0 + 39 * 30
                settle()
                ve.wait_ge(hot_ready, 80 * (l + 1))
                ve.wait_ge(products, at["v", l])
                for half in range(2):
                    ve.wait_ge(g_stored[half], 16 * 20 * (l + 1))
                for t in range(NT):
                    do(V.memset(f[:, t, :], 0.0))
                settle()
                n1 = l * NBLK * NT

                def blocks(i):
                    for half in range(2):
                        blk = 2 * i + half
                        ve.wait_ge(ag_loaded[half], 32 * (l * NBLK // 2 + i + 1))
                        for j in range(JB):
                            A_ = ab[half][:, j, :].rearrange("p (n t) -> p n t", t=16)
                            last = V.tensor_tensor(A_, A_, gb[:, half, :, j, :], ALU.mult)
                            if j < JB - 1:
                                do(last)
                        last.then_inc(w_ready, 1)
                        for t in range(NT):
                            g = half * NT + t
                            pr = g % 2
                            gg = l * NBLK * NT + blk * NT + t
                            ve.wait_ge(products, at["v", l] + blk * NT + t + 1)
                            if not (isinstance(i, int) and half == 0 and t == 0 and l == 0):
                                ve.wait_ge(acc_done, gg)
                            V.tensor_tensor(f[:, t, :].rearrange("p (c d) -> p c d", c=2), f[:, t, :].rearrange("p (c d) -> p c d", c=2),
                                            PS[:, 2 * pr:2 * pr + 2, :], ALU.add).then_inc(acc_done, 1)

                n0 = ch.n
                blocks(0)
                with ve.Fori(1, NBLK // 2) as i:
                    blocks(i)
                ch.n = n0 + NBLK // 2 * 2 * (JB - 1)
                settle()
                ve.wait_ge(acc_done, (l + 1) * NBLK * NT)
                layer_norm(2 * l + 1, rowsP)

            def odd():
                modulated(2)
                ve.wait_ge(alog_exp, 1)
                ve.wait_ge(od_consts, 1)
                fl = lambda z: z[:].rearrange("p t d h -> p (t d h)")
                ve.wait_ge(products, at["dt",])
                link(V.tensor_tensor(dtc[:].rearrange("p t d h -> p t (d h)"), PS[:, 0, 0:NT * 64].rearrange("p (t n) -> p t n", t=NT),
                                     brow[:, 0, :].unsqueeze(1).broadcast_to([P, NT, 64]), ALU.add))
                V.scalar_tensor_tensor(fl(av), fl(dtc), -1.0, fl(dtc), ALU.mult, ALU.max).then_inc(dt_abs, 1)
                ve.wait_ge(dt_sp, 1)
                link(V.scalar_tensor_tensor(fl(dtc), fl(dtc), 0.0, fl(av), ALU.max, ALU.add))
                V.scalar_tensor_tensor(av[:].rearrange("p t d h -> p t (d h)"), dtc[:].rearrange("p t d h -> p t (d h)"), -1.0,
                                       brow[:, 1, :].unsqueeze(1).broadcast_to([P, NT, 64]), ALU.mult, ALU.mult).then_inc(a_ready, 1)
                ve.wait_ge(products, at["acum",])
                ac = PS[:, 1, 0:NT * 64]
                do(V.tensor_scalar(fl(nac), ac, -1.0, None, ALU.mult))
                do(V.tensor_copy(fl(win), ac))
                do(V.tensor_copy(fl(dcy), PS[:, 2, 0:NT * 64]))
                settle()
                link(V.tensor_tensor(fl(wup), fl(dcy), fl(nac), ALU.add))
                V.tensor_copy(otmp[:, 0:1], nac[:, 0, 0, 0:1]).then_inc(ac_ready, 1)
                ve.wait_ge(seg_exp, 1)
                link(V.tensor_tensor(fl(wup), fl(wup), fl(dtc), ALU.mult))
                for g in range(G_C):
                    hs = slice(g * J_C, (g + 1) * J_C)
                    for m in range(7):
                        if m < 6:
                            q = g * 6 + m
                            ve.wait_ge(pad_filled, q + 1)
                            if q >= 2:
                                ve.wait_ge(act_done, q - 1)
                            acc = cacc[:, q % 2, :]
                            w0 = g * 6 + m
                            link(V.tensor_scalar(acc, cpad[:, q % 2, 0:T + 2], cw[:, w0, 0:1], None, ALU.mult))
                            for j in range(1, D_CONV):
                                ins = V.scalar_tensor_tensor(acc, cpad[:, q % 2, j:j + T + 2], cw[:, w0, j:j + 1], acc, ALU.mult, ALU.add)
                                if j < D_CONV - 1:
                                    link(ins)
                            ins.then_inc(conv_done, 1)
                        mm = m - 1
                        if 0 <= mm < 5:
                            n = g * 5 + mm
                            ve.wait_ge(products, at["xt", g, mm])
                            dst = xs[:, :, mm * P:(mm + 1) * P] if mm < 4 else Btok[:, :, :]
                            b = 4 + 2 * (n % 2)
                            do(V.tensor_copy(dst[:, 0:4, :], PS[:, b, :].rearrange("p (t c) -> p t c", t=4)))
                            V.tensor_copy(dst[:, 4, :], PS[:, b + 1, 0:P]).then_inc(tr_evac, 1)
                    ve.wait_ge(tr_evac, g * 5 + 5)
                    for t in range(NT):
                        n = g * NT + t
                        for d in range(2):
                            ve.wait_ge(products, at["seg", g, t, d])
                            if n >= 1:
                                ve.wait_ge(products, at["intra", (g * NT + t - 1) // NT, (t - 1) % NT])
                            for j in range(J_C):
                                last = V.scalar_tensor_tensor(EP[:, d, j, :], PS[:, 5 + j // 4, (j % 4) * P:(j % 4 + 1) * P],
                                                              nac[:, t, d, g * J_C + j:g * J_C + j + 1], maskO[:, d, :], ALU.add, ALU.add)
                                if j < J_C - 1:
                                    do(last)
                            last.then_inc(oe_ready, 1)
                        for d in range(2):
                            ve.wait_ge(oexp_ready, 2 * n + d + 1)
                            for j in range(J_C):
                                last = V.scalar_tensor_tensor(EP[:, d, j, :], EP[:, d, j, :], dtc[:, t, d, g * J_C + j:g * J_C + j + 1],
                                                              PS[:, 4, 0:P], ALU.mult, ALU.mult)
                                if j < J_C - 1:
                                    do(last)
                            last.then_inc(op_ready, 1)
                        yt = y[:, t, g * GC:(g + 1) * GC]
                        link(V.tensor_tensor(yt.rearrange("p (j c) -> p j c", j=J_C), xs[:, t, :].rearrange("p (j c) -> p j c", j=J_C),
                                             bc(brow[:, 2, hs], P_C), ALU.mult))
                        ve.wait_ge(products, at["intra", g, t])
                        V.tensor_tensor(yt, yt, PS[:, 7, :], ALU.add).then_inc(y_intra, 1)
                    ve.wait_ge(y_intra, g * NT + NT)
                    for s in range(NT):
                        for d in range(2):
                            t = tile_of(s, d)
                            n, nu = (g * 4 + s - 1) * 2 + d, (g * 4 + s) * 2 + d
                            yt = y[:, t, g * GC:(g + 1) * GC]
                            if s > 0:
                                ve.wait_ge(products, at["inter", g, s, d])
                                link(V.tensor_tensor(otmp[:].rearrange("p (j c) -> p j c", j=J_C), PS[:, n % 2, :].rearrange("p (j c) -> p j c", j=J_C),
                                                     bc(win[:, t, d, hs], P_C), ALU.mult))
                                V.tensor_tensor(yt, yt, otmp[:], ALU.add).then_inc(inter_done, 1)
                                ve.wait_ge(inter_done, n + 1)
                            if s < NT - 1:
                                ve.wait_ge(products, at["upd", g, s, d])
                                if s == 0:
                                    if g >= 1:
                                        ve.wait_ge(hst_stored, 16 * g)
                                    V.tensor_copy(hout[:, d, :], PS[:, 2 + nu % 2, :]).then_inc(upd_done, 1)
                                else:
                                    hv = hst[:, d, :].rearrange("p (j c) -> p j c", j=J_C)
                                    link(V.tensor_tensor(hv, hv, bc(dcy[:, t, d, hs], P_C), ALU.mult))
                                    V.tensor_tensor(hst[:, d, :], hst[:, d, :], PS[:, 2 + nu % 2, :], ALU.add).then_inc(upd_done, 1)
                                ve.wait_ge(upd_done, nu + 1)
                for s in range(D_INNER // SLICE):
                    for t in range(NT):
                        n = s * NT + t
                        ve.wait_ge(z_silu, n + 1)
                        yt = y[:, t, s * SLICE:(s + 1) * SLICE]
                        V.tensor_tensor(yt, yt, zt[:, n % 2, :], ALU.mult).then_inc(z_used, 1)
                ve.wait_ge(nw_loaded, 16)
                for k in range(2 * KD):
                    ve.wait_ge(products, at["yt", k])
                    V.tensor_scalar(yT[:, k, P:T], PS[:, 2 * (k % 4) + 1, :], nw[:, k:k + 1], None, ALU.mult).then_inc(yt_v, 1)
                ve.wait_ge(ssq_done, 1)
                V.reciprocal(ssq[:], ssq[:]).then_inc(rr_ready, 1)
                ve.wait_ge(oo_evac, KD * NT)
                layer_norm(2, rowsO)

            if "even" in run:
                even()
            if "peer0" in run:
                peer(0)
            if "odd" in run:
                odd()
            if "peer1" in run:
                peer(1)

        @block.scalar
        def _(act):
            S = nc.scalar
            ch = Chain(act, act_chain)
            do, link, settle = ch.do, ch.link, ch.settle

            act.dma_start(cT[:], a["c"]).then_inc(small_loaded, 16)
            act.dma_start(bmod, a["b_mod"][:, 0]).then_inc(small_loaded, 16)
            act.dma_start(x[:, 0, :], a["x_prompt"]).then_inc(x_loaded, 16)
            act.dma_start(x[:, 1:NT, :], a["x_sample"]).then_inc(x_loaded, 16)
            act.dma_start(f[:, 0:NT - 1, :], a["pos"]).then_inc(x_loaded, 16)
            act.wait_ge(small_loaded, 32)
            S.activation(cT[:], cT[:], ACT.Silu).then_inc(c_ready, 1)
            for l in range(DEPTH):
                act.wait_ge(mod_rows, l + 1)
                if l + 1 < DEPTH:
                    act.dma_start(bmod, a["b_mod"][:, l + 1]).then_inc(small_loaded, 16)
                act.dma_start(gdram[l, 0], mrow[:, 2 * D:3 * D]).then_inc(gates_stored, 16)
                act.dma_start(gdram[l, 1], mrow[:, 5 * D:6 * D]).then_inc(gates_stored, 16)
            act.wait_ge(mod_cols, DEPTH)
            act.wait_ge(gates_stored, 32 * DEPTH)

            def modulated(n):
                l, kind = n // 2, 2 * (n % 2)
                for k in range(KD):
                    act.wait_ge(products, at["h", n, k])
                    S.activation(hT[:, k, 0:P], PS[:, 2 * (k % 4), 0:P], ACT.Identity, bias=modT[:, l, kind, k, 0:1],
                                 scale=modT[:, l, kind + 1, k, 0:1]).then_inc(h_evac_a, 1)

            def layer_norm(n, rows):
                l, second = n // 2, n % 2
                act.dma_start(rows[:, 0, :], a["ln_g"][n].partition_broadcast(P)).then_inc(rows_loaded, 16)
                act.dma_start(rows[:, 1, :], a["ln_b"][n].partition_broadcast(P)).then_inc(rows_loaded, 16)
                act.dma_start(rows[:, 2:4, :].rearrange("p a d -> p (a d)"),
                              gdram[l, second].rearrange("a d -> (a d)").partition_broadcast(P)).then_inc(rows_loaded, 16)

            def deviation(n_var, n):
                act.wait_ge(var_ready, n_var)
                S.activation(rstd[:, 0:n], mv[:, 0:n, 1], ACT.Sqrt, bias=eps[:, 0:1]).then_inc(dev_ready, 1)

            def even():
                modulated(0)
                for dst, name in ((m0[:], "m0"), (gbias[:], "gate_bias"), (gn[:].rearrange("p a d -> p (a d)"), "gn"),
                                  (lg[:].rearrange("p d h -> p (d h)"), "log_decay"), (Cst[:], "Cn0")):
                    src = a[name].partition_broadcast(P) if name in ("gn", "log_decay") else a[name]
                    act.dma_start(dst, src).then_inc(even_loaded, 16)
                L, F, t1, t2 = (grow[:, i] for i in range(4))
                for fam in range(2):
                    def pair_out(kind, i, dst, scale):
                        act.wait_ge(products, at[kind, fam, i])
                        pr = proj_count[kind, fam, i][0] % 4
                        S.activation(dst.rearrange("p (a t) -> p a t", a=2), PS[:, 2 * pr:2 * pr + 2, 0:HT], ACT.Copy,
                                     scale=scale).then_inc(proj_a, 1)
                    for i in range(NH):
                        pair_out("q", i, qT[:, i, :], 1.0 if fam == 0 else DH ** -0.5)
                    if fam == 0:
                        act.wait_ge(gate_exp, 1)
                        link(S.activation(t1, t1, ACT.Exp, scale=-1.0))
                        S.activation(t1, t1, ACT.Ln, bias=1.0).then_inc(gate_act, 1)
                    for i in range(NH):
                        pair_out("k", i, kT[:, i, :], DH ** -0.5 if fam == 0 else 1.0)
                    if fam == 0:
                        act.wait_ge(gate_exp, 2)
                        do(S.activation(L, L, ACT.Exp))
                        do(S.activation(F, F, ACT.Exp))
                        do(S.activation(t2, b_m[:, 1], ACT.Exp, scale=-1.0))
                        S.activation(DEC_, DEC_, ACT.Exp).then_inc(gates_done, 1)
                        act.dma_start(o["new_m"], ML[:, :, 0], allow_slow_non_contiguous=True).then_inc(stored, 16)
                    else:
                        act.wait_ge(even_loaded, 80)
                        S.activation(lg[:], lg[:], ACT.Exp).then_inc(diff_ready, 1)
                        act.wait_ge(norm_done, 1)
                    for s in range(2):
                        for t in range(NT):
                            act.wait_ge(products, at["o", fam, (s, t)])
                            pr = proj_count["o", fam, (s, t)][0] % 4
                            S.activation(og[:, t, s * SLICE:(s + 1) * SLICE], PS[:, 2 * pr, 0:SLICE],
                                         ACT.Sigmoid if fam == 0 else ACT.Silu).then_inc(proj_a, 1)
                    if fam == 0:
                        for u in range(NU):
                            act.wait_ge(e_ready, u + 1)
                            S.activation(eb[:, u % 2, :], eb[:, u % 2, :], ACT.Exp).then_inc(exp_ready, 1)
                            if u == 2 * NH + 4:
                                act.wait_ge(state_ready, 2 * NH)
                                act.dma_start(o["new_Cn"], Cout[:]).then_inc(stored, 16)
                        act.wait_ge(h_done, NU)
                        act.dma_start(Cst[:, :, :, 0:DH], a["S0"]).then_inc(ret_ready, 16)
                    else:
                        act.wait_ge(decay_ready, 1)
                        do(S.activation(xz[:], xz[:], ACT.Exp))
                        for d in range(2):
                            for h in range(NH):
                                last = S.activation(Dm[:, d, h, :], diff[:, d, :], ACT.Exp, scale=lg[:, d, h:h + 1])
                                if (d, h) != (1, NH - 1):
                                    do(last)
                        last.then_inc(decay_exp, 1)
                        act.wait_ge(state_ready, NU - 2 * NH + 2 * NH)
                        act.dma_start(o["new_ret"], Cout[:, :, :, 0:DH]).then_inc(stored, 16)
                    deviation(fam + 1, NT * NH)
                act.wait_ge(products, at["H", 1, NU - 1])
                layer_norm(0, rowsB)
                for k in range(KD):
                    act.wait_ge(products, at["h", 4, k])
                    S.activation(hT[:, k, 0:P], PS[:, 2 * (k % 4), 0:P], ACT.Copy).then_inc(h_evac_a, 1)
                for s in range(D // SLICE):
                    for t in range(NT):
                        act.wait_ge(products, at["eo", s, t])
                        S.activation(f[:, t, s * SLICE:(s + 1) * SLICE], PS[:, (s * NT + t) % 8, 0:SLICE], ACT.Copy).then_inc(out_evac, 1)
                deviation(3, NT)

            def peer(l):
                act.wait_ge(x_ready, 2 * l + 2)
                act.dma_start(keys, a["keys"][l]).then_inc(keys_loaded, 16)
                modulated(2 * l + 1)
                for m in range(2 * H_P):
                    act.wait_ge(products, at["pq", l, m])
                    if m >= 2:
                        act.wait_ge(products, at["ps", l, m - 2])
                    S.activation(qb[:, m % 2, :].rearrange("p (a t) -> p a t", a=2), PS[:, 2 * (m % 2):2 * (m % 2) + 2, 0:HT],
                                 ACT.Copy).then_inc(q_evac, 1)

                def gelus(i, build):
                    static = isinstance(i, int)
                    for jj in range(16):
                        gj = l * N_KEYS + i * 16 + jj
                        pr, half = jj // 2, jj % 2
                        n = at["ub", l] + (i - 3) * 32 + 2 * jj + 1 if build else at["u", l] + i * 16 + jj + 1
                        act.wait_ge(products, n)
                        if half == 0 and not (static and i == 0 and l == 0 and pr < 2):
                            act.wait_ge(a_stored[pr % 2], 16 * (l * 32 + i * 4 + pr // 2))
                        S.activation(abuf[:, pr % 2, half, :].rearrange("p (a t) -> p a t", a=2), PS[:, 2 * half:2 * half + 2, 0:HT],
                                     ACT.Gelu).then_inc(act_gelu, 1)
                        if half == 1:
                            act.wait_ge(act_gelu, gj + 1)
                            act.dma_start(Ad[2 * i + pr // 4, :, 2 * (pr % 4):2 * (pr % 4) + 2, :], abuf[:, pr % 2]).then_inc(a_stored[pr % 2], 16)
                        if build:
                            act.wait_ge(products, n + 1)
                            if half == 0 and not (static and l == 0 and pr < 2):
                                act.wait_ge(g_stored[pr % 2], 16 * (l * 20 + (i - 3) * 4 + pr // 2))
                            S.activation(gst[:, pr % 2, :, half * 8:half * 8 + 8].rearrange("p j t -> p t j"),
                                         PS[:, 4 + 2 * half:6 + 2 * half, :].rearrange("p b (t j) -> p (b t) j", j=P), ACT.Copy).then_inc(g_evac, 1)
                            if half == 1:
                                act.wait_ge(g_evac, l * 80 + (i - 3) * 16 + jj + 1)
                                act.dma_start(Gd[:, :, (i - 3) * 8 + pr].rearrange("b p j t -> p b (j t)"),
                                              gst[:, pr % 2].rearrange("p (b j) t -> p b (j t)", j=JB)).then_inc(g_stored[pr % 2], 16)

                gelus(0, False)
                with act.Fori(1, 3) as i:
                    gelus(i, False)
                act.wait_ge(sm_sub, l + 1)
                S.activation(best[:], best[:], ACT.Exp).then_inc(sm_exp, 1)
                gelus(3, True)
                with act.Fori(4, 8) as i:
                    gelus(i, True)
                for half in range(2):
                    act.wait_ge(a_stored[half], 16 * 32 * (l + 1))
                    act.wait_ge(g_stored[half], 16 * 20 * (l + 1))
                act.wait_ge(products, at["v", l])
                act.wait_ge(hot_ready, 80 * (l + 1))
                layer_norm(2 * l + 1, rowsP)
                deviation(4 + 2 * l, NT)

            def odd():
                act.wait_ge(x_ready, 3)
                act.dma_start(brow[:].rearrange("p a n -> p (a n)"), a["odd_rows"].partition_broadcast(P)).then_inc(odd_loaded, 16)
                act.dma_start(cw[:], a["conv"]).then_inc(odd_loaded, 16)
                act.wait_ge(odd_loaded, 32)
                S.activation(brow[:, 1, :], brow[:, 1, :], ACT.Exp).then_inc(alog_exp, 1)
                modulated(2)
                fl = lambda z: z[:].rearrange("p t d h -> p (t d h)")
                act.wait_ge(dt_abs, 1)
                link(S.activation(fl(av), fl(av), ACT.Exp, scale=-1.0))
                S.activation(fl(av), fl(av), ACT.Ln, bias=1.0).then_inc(dt_sp, 1)
                act.wait_ge(ac_ready, 1)
                do(S.activation(fl(win), fl(win), ACT.Exp))
                do(S.activation(fl(dcy), fl(dcy), ACT.Exp))
                S.activation(fl(wup), fl(wup), ACT.Exp).then_inc(seg_exp, 1)
                for g in range(G_C):
                    if g:
                        act.wait_ge(products, at["inter", g - 1, NT - 1, 1])
                        act.wait_ge(upd_done, 8 * g)
                    act.dma_start(hst[:], a["h0"][g]).then_inc(hst_loaded, 16)
                    for m in range(7):
                        if m < 6:
                            q = g * 6 + m
                            act.wait_ge(products, at["xbc", g, m])
                            if q >= 2:
                                act.wait_ge(conv_done, q - 1)
                            do(S.activation(cpad[:, q % 2, 2:2 + P], PS[:, 2 * (m % 2), 0:P], ACT.Copy))
                            S.activation(cpad[:, q % 2, 4 + P:4 + T], PS[:, 2 * (m % 2) + 1, :], ACT.Copy).then_inc(pad_filled, 1)
                        mm = m - 1
                        if mm >= 0:
                            q = g * 6 + mm
                            act.wait_ge(conv_done, q + 1)
                            if mm < 4:
                                if mm >= 2:
                                    act.wait_ge(products, at["xt", g, mm - 2])
                                dst = sx[:, mm % 2, :]
                            else:
                                dst = BC[:, mm - 4, :]
                            do(S.activation(dst[:, 0:P], cacc[:, q % 2, 0:P], ACT.Silu, bias=cw[:, q, D_CONV:D_CONV + 1]))
                            S.activation(dst[:, P:T], cacc[:, q % 2, P + 2:T + 2], ACT.Silu, bias=cw[:, q, D_CONV:D_CONV + 1]).then_inc(act_done, 1)
                    for t in range(NT):
                        for d in range(2):
                            n = (g * NT + t) * 2 + d
                            act.wait_ge(oe_ready, n + 1)
                            S.activation(EP[:, d], EP[:, d], ACT.Exp).then_inc(oexp_ready, 1)
                    act.wait_ge(upd_done, 8 * g + 2)
                    act.dma_start(o["new_ssd"][g], hout[:]).then_inc(hst_stored, 16)
                act.wait_ge(products, at["inter", G_C - 1, NT - 1, 1])
                act.wait_ge(inter_done, 8 * G_C)
                act.wait_ge(hst_stored, 16 * G_C)
                act.dma_start(nw[:], a["norm_w"]).then_inc(nw_loaded, 16)
                layer_norm(2, rowsO)
                for s in range(D_INNER // SLICE):
                    for t in range(NT):
                        n = s * NT + t
                        act.wait_ge(products, at["z", s, t])
                        if n >= 2:
                            act.wait_ge(z_used, n - 1)
                        S.activation(zt[:, n % 2, :], PS[:, n % 4, 0:SLICE], ACT.Silu).then_inc(z_silu, 1)
                act.wait_ge(z_used, D_INNER // SLICE * NT)
                act.wait_ge(products, at["z", D_INNER // SLICE - 1, NT - 1])
                act.wait_ge(nw_loaded, 16)
                for k in range(2 * KD):
                    act.wait_ge(products, at["yt", k])
                    S.activation(yT[:, k, 0:P], PS[:, 2 * (k % 4), 0:P], ACT.Copy, scale=nw[:, k:k + 1]).then_inc(yt_a, 1)
                junk = hT[:, 0:4, 0:512]
                for t in range(NT):
                    link(S.activation(junk, y[:, t, :].rearrange("p (a b) -> p a b", a=4), ACT.Square, accum_out=ssq[:, t:t + 1]))
                S.activation(ssq[:], ssq[:], ACT.Sqrt, bias=eps[:, 0:1], scale=1.0 / D_INNER).then_inc(ssq_done, 1)
                act.wait_ge(rr_ready, 1)
                for s in range(KD):
                    for t in range(NT):
                        act.wait_ge(products, at["oo", s, t])
                        S.activation(f[:, t, s * P:(s + 1) * P], PS[:, (s * NT + t) % 8, 0:P], ACT.Copy, scale=ssq[:, t:t + 1]).then_inc(oo_evac, 1)
                deviation(5, NT)

            if "even" in run:
                even()
            if "peer0" in run:
                peer(0)
            if "odd" in run:
                odd()
            if "peer1" in run:
                peer(1)
            act.wait_ge(x_ready, len(run))
            act.dma_start(o["y_prompt"], x[:, 0, :]).then_inc(stored, 16)
            act.dma_start(o["y_sample"], x[:, 1:NT, :]).then_inc(stored, 16)
            act.wait_ge(stored, 32 + (48 if "even" in run else 0))

        @block.gpsimd
        def _(pool):
            G = nc.gpsimd
            ch = Chain(pool, pool_chain)
            do, link, settle = ch.do, ch.link, ch.settle
            do(G.memset(ident[:], 0.0))
            do(G.memset(eps[:], EPS))
            link(G.memset(ones[:], 1.0))
            G.affine_select(out=ident[:], in_=ident[:], compare_op=ALU.not_equal, fill=1.0, base=0,
                            pattern=[[-1, P]], channel_multiplier=1).then_inc(consts_ready, 1)

            def one_sided(dst, src, d, fill):
                sign = 1 if d == 0 else -1
                return G.affine_select(out=dst, in_=src, compare_op=ALU.is_ge, fill=fill, base=0,
                                       pattern=[[sign, P]], channel_multiplier=-sign)

            def even():
                pool.wait_ge(mod_cols, DEPTH)
                pool.wait_ge(gates_stored, 32 * DEPTH)
                do(G.memset(mask[:], 0.0))
                do(G.memset(sel4[:], 0.0))
                do(G.iota(diff[:, 0, :], [[1, P]], base=0, channel_multiplier=-1, allow_small_or_imprecise_dtypes=True))
                do(G.iota(diff[:, 1, :], [[-1, P]], base=0, channel_multiplier=1, allow_small_or_imprecise_dtypes=True))
                for i, (b, m) in enumerate(((1, 1), (P, -1), (P - 1, -1), (0, 1))):
                    do(G.iota(icol[:, i:i + 1], [[0, 1]], base=b, channel_multiplier=m, allow_small_or_imprecise_dtypes=True))
                settle()
                for d in range(2):
                    do(one_sided(mask[:, d, :], mask[:, d, :], d, NEG))
                do(G.tensor_scalar(diff[:], diff[:], 0.0, None, ALU.max))
                G.affine_select(out=sel4[:], in_=sel4[:], compare_op=ALU.not_equal, fill=1.0, base=0,
                                pattern=[[-1, NH], [0, P]], channel_multiplier=1).then_inc(ev_consts, 1)
                for fam in range(2):
                    if fam == 1:
                        pool.wait_ge(decay_exp, 1)
                        for d in range(2):
                            for h in range(NH):
                                last = one_sided(Dm[:, d, h, :], Dm[:, d, h, :], d, 0.0)
                                if (d, h) != (1, NH - 1):
                                    do(last)
                        last.then_inc(dm_ready, 1)
                    pool.wait_ge(proj_a, proj_count["o", fam, (1, NT - 1)][2])
                    pool.wait_ge(even_loaded, 80)
                    G.tensor_tensor(og, og, gn[:, fam, :].unsqueeze(1).broadcast_to([P, NT, W_A]), ALU.mult).then_inc(og_ready, 1)
                    pool.wait_ge(proj_v, proj_count["kt", fam, NT - 1][2])
                    pool.wait_ge(cols_ready, 1)
                    if fam == 1:
                        pool.wait_ge(dm_ready, 1)
                    for u in range(NU - 2 * NH):
                        s, h, d = UNITS[u]
                        t = tile_of(s, d)
                        if u >= 2:
                            pool.wait_ge(products, at["H", fam, u - 2])
                        w = cols[:, t, 0, d, h:h + 1] if fam == 0 else xz[:, 1, d, h:h + 1]
                        G.tensor_scalar(kw[:, u % 2, :], ktok[:, t, h, :], w, None, ALU.mult).then_inc(kw_ready, 1)

            def peer(l):
                pool.wait_ge(x_ready, 2 * l + 2)
                G.iota(iota[:], [[1, N_KEYS]], base=0, channel_multiplier=0, allow_small_or_imprecise_dtypes=True).then_inc(iota_ready, 1)

            def odd():
                pool.wait_ge(x_ready, 3)
                for i in range(2):
                    do(G.memset(cpad[:, i, :], 0.0))
                for d in range(2):
                    do(G.memset(maskO[:, d, :], 0.0))
                settle()
                for d in range(2):
                    do(one_sided(maskO[:, d, :], maskO[:, d, :], d, NEG))
                do(one_sided(tri[:, 0, :], ones[:], 0, 0.0))
                one_sided(tri[:, 1, :], ones[:], 1, 0.0).then_inc(od_consts, 1)
                for g in range(G_C):
                    pool.wait_ge(tr_evac, g * 5 + 5)
                    for s in range(NT - 1):
                        for d in range(2):
                            t = tile_of(s, d)
                            nu = (g * 4 + s) * 2 + d
                            if nu >= 1:
                                gg, ss = divmod((nu - 1) // 2, 4)
                                pool.wait_ge(products, at["upd", gg, ss, (nu - 1) % 2])
                            G.tensor_tensor(xw[:].rearrange("p (j c) -> p j c", j=J_C), xs[:, t, :].rearrange("p (j c) -> p j c", j=J_C),
                                            bc(wup[:, t, d, g * J_C:(g + 1) * J_C], P_C), ALU.mult).then_inc(xw_ready, 1)

            if "even" in run:
                even()
            if "peer0" in run:
                peer(0)
            if "odd" in run:
                odd()
            if "peer1" in run:
                peer(1)

        @block.sync
        def _(sp):
            freed = []

            def load(src, k, before=None):
                n = len(freed) if k is None else k
                if before is not None:
                    sp.wait_ge(products, before)
                elif n >= NSLOT:
                    sp.wait_ge(products, freed[n - NSLOT])
                w = src.shape[-1]
                sp.dma_start(ring[:, n % NSLOT, 0:w], src).then_inc(slot_full[n % NSLOT], 16)

            for entry in slices:
                src = entry[0]
                if src == "U":
                    l, n_u, n_b = entry[1:]
                    b = len(freed)
                    for k in range(8):
                        load(a["u"][l, k], b + k)
                        freed.append(None)
                    for k in range(8, 64):
                        freed.append(None)
                    for m in range(64):
                        freed[b + m] = n_u + 2 * m + 2 if m < 24 else n_b + 2 * (2 * m + 1 - 48) + 1
                    with sp.Fori(1, 4) as i:
                        for k in range(8):
                            load(a["u"][l, 8 * i + k], b + k, n_u + (i - 1) * 16 + 2 * k + 2)
                    with sp.Fori(4, 8) as i:
                        for k in range(8):
                            load(a["u"][l, 8 * i + k], b + k, n_b + (i - 4) * 32 + 2 * (2 * k + 1) + 1)
                elif src == "V":
                    l, n_v = entry[1:]
                    b = len(freed)
                    for half in range(2):
                        sp.wait_ge(a_stored[half], 16 * 32 * (l + 1))
                        sp.wait_ge(g_stored[half], 16 * 20 * (l + 1))
                    sp.wait_ge(products, n_v)

                    def block_loads(i, first):
                        for half in range(2):
                            if not first:
                                sp.wait_ge(products, n_v + (2 * i + half - 1) * NT)
                            sp.dma_start(ab[half], Ad[2 * i + half]).then_inc(ag_loaded[half], 16)
                            sp.dma_start(gb[:, half], Gd[2 * i + half]).then_inc(ag_loaded[half], 16)
                            for q in range(4):
                                k = 4 * half + q
                                if first:
                                    load(a["v"][l, 8 * i + k], b + k)
                                else:
                                    load(a["v"][l, 8 * i + k], b + k, n_v + (2 * i + half - 1) * NT)

                    block_loads(0, True)
                    with sp.Fori(1, NBLK // 2) as i:
                        block_loads(i, False)
                    for m in range(64):
                        freed.append(n_v + (m // 4 + 1) * NT)
                else:
                    load(src, None)
                    freed.append(at[entry[1]])


def kernel(**inputs):
    import numpy as _np
    import concourse.bacc as _bacc
    from concourse import mybir as _mybir
    from concourse.bass_utils import run_bass_kernel_spmd as _run
    return launch(inputs, _np, _bacc, _mybir, _run, None)


def layouts(i):
    c_ = np.ascontiguousarray

    def rows(w, ncol):
        lead, (K, N) = w.shape[:-2], w.shape[-2:]
        w = w.reshape(*lead, K // P, P, N // ncol, ncol)
        n = len(lead)
        w = w.transpose(*range(n), n + 2, n + 1, n, n + 3)
        return c_(w.reshape(*lead, N // ncol, P, K // P * ncol))

    r = {k: np.asarray(v) for k, v in i.items()}
    a = {}
    a["c"] = c_(np.stack([r["c_ctx"].reshape(KD, P), r["c"][0].reshape(KD, P)], -1).transpose(1, 0, 2))
    a["b_mod"] = c_(np.stack([r["b_mod"]] * 2, 0))
    a["x_prompt"] = c_(r["x_prompt"][0])
    a["x_sample"] = c_(r["x_sample"][0].reshape(NT - 1, P, D).transpose(1, 0, 2))
    a["w_mod"] = rows(r["w_mod"], SLICE)
    w = r["even_w_in"][0]
    sizes = [W_A] * 4 + [2 * NH] * 2 + [W_A] * 4
    at = np.cumsum([0] + sizes)
    part = [w[:, at[n]:at[n + 1]] for n in range(10)]
    a["w_even"] = np.stack([np.stack([rows(q, SLICE) for q in part[0:4]]), np.stack([rows(q, SLICE) for q in part[6:10]])])
    wg = np.zeros((D, P), np.float32)
    for q in range(4):
        src = part[4 + q // 2]
        wg[:, 32 * q:32 * q + NH] = src[:, (q % 2) * NH:(q % 2 + 1) * NH]
    a["w_gate"] = rows(wg, P)[0]
    a["gate_bias"] = c_(np.concatenate([r["mlstm_i_bias"][0], r["mlstm_f_bias"][0]], 0).T)
    a["m0"] = c_(r["state_mlstm_m"][0, 0].T)
    a["gn"] = c_(np.stack([r["even_gn_a"][0], r["even_gn_b"][0]]).reshape(-1))
    a["log_decay"] = c_(r["ret_log_decay"][0].reshape(-1))
    a["Cn0"] = c_(np.concatenate([r["state_mlstm_C"][0, 0], r["state_mlstm_n"][0, 0][..., None]], -1).transpose(2, 0, 1, 3))
    a["S0"] = c_(r["state_ret"][0, 0].transpose(2, 0, 1, 3))
    a["w_eout"] = rows(r["even_w_out"][0], SLICE)
    a["ln_g"] = c_(np.stack([r["ln1_g"][0], r["ln2_g"][0], r["ln1_g"][1], r["ln2_g"][1]]))
    a["ln_b"] = c_(np.stack([r["ln1_b"][0], r["ln2_b"][0], r["ln1_b"][1], r["ln2_b"][1]]))
    w = r["odd_w_in"][0]
    a["w_z"] = rows(w[:, 0:D_INNER], SLICE)
    xbc = w[:, D_INNER:D_INNER + CONV_DIM]
    order = []
    for g in range(G_C):
        order += list(range(g * GC, (g + 1) * GC))
        order += list(range(D_INNER + g * N_C, D_INNER + (g + 1) * N_C))
        order += list(range(D_INNER + G_C * N_C + g * N_C, D_INNER + G_C * N_C + (g + 1) * N_C))
    a["w_xbc"] = c_(rows(xbc[:, order], SLICE).reshape(G_C, 3, P, KD * SLICE))
    a["w_dt"] = rows(w[:, D_INNER + CONV_DIM:], 64)[0]
    cw_ = np.concatenate([r["odd_conv_w"][0], r["odd_conv_b"]], 0)[:, order]
    a["conv"] = c_(cw_.reshape(D_CONV + 1, 24, P).transpose(2, 1, 0))
    a["odd_rows"] = c_(np.concatenate([r["odd_dt_bias"].reshape(-1), r["odd_a_log"].reshape(-1), r["odd_d"].reshape(-1), r["odd_d"].reshape(-1)]))
    a["h0"] = c_(r["state_ssd"][0, 0].reshape(2, G_C, GC, N_C).transpose(1, 3, 0, 2))
    a["norm_w"] = c_(r["odd_norm_w"][0].reshape(2 * KD, P).T)
    a["w_oout"] = rows(r["odd_w_out"][0], P)
    a["w_pq"] = rows(r["peer_w_q"], SLICE)
    a["keys"] = c_(r["peer_sub_keys"].transpose(0, 4, 1, 2, 3).reshape(DEPTH, P, 2 * H_P, N_KEYS))
    u = r["peer_u"].reshape(DEPTH, N_KEYS, N_KEYS // 2, 2, KD, P)
    a["u"] = c_(u.transpose(0, 2, 5, 4, 3, 1)).reshape(DEPTH, N_KEYS // 2, P, KD * SLICE)
    v = r["peer_v"].reshape(DEPTH, N_KEYS, N_KEYS // 2, 2, D)
    a["v"] = c_(v.transpose(0, 2, 1, 3, 4)).reshape(DEPTH, N_KEYS // 2, P, 2 * D)
    rr = np.repeat(np.arange(DEC // GRID_W, dtype=np.float32), GRID_W)
    cc = np.tile(np.arange(GRID_W, dtype=np.float32), DEC // GRID_W)
    fr = (1.0 / (10000.0 ** (np.arange(D // 4, dtype=np.float32) / (D // 4)))).astype(np.float32)
    er, ec = rr[:, None] * fr, cc[:, None] * fr
    pos_ = np.concatenate([np.sin(er), np.cos(er), np.sin(ec), np.cos(ec)], -1).astype(np.float32)
    a["pos"] = c_(pos_.reshape(NT - 1, P, D).transpose(1, 0, 2))
    return a


OUTS = {"y_prompt": [P, D], "y_sample": [P, NT - 1, D], "new_Cn": [P, 2, NH, DH + 1], "new_m": [NH, 2],
        "new_ret": [P, 2, NH, DH], "new_ssd": [G_C, P, 2, GC]}


def program(nc, arrays, mybir_, upto):
    f32 = mybir_.dt.float32
    a = {n: nc.dram_tensor(f"in_{n}", list(v.shape), f32, kind="ExternalInput").ap() for n, v in arrays.items()}
    o = {n: nc.dram_tensor(f"out_{n}", s, f32, kind="ExternalOutput").ap() for n, s in OUTS.items()}
    trunk(nc, a, o, upto)


def launch(inputs, np_, bacc, mybir_, run, upto):
    arrays = layouts(inputs)
    nc = bacc.Bacc("TRN2", target_bir_lowering=False, num_devices=1)
    program(nc, arrays, mybir_, upto)
    r = run(nc, [{f"in_{n}": v for n, v in arrays.items()}], core_ids=[0]).results[0]
    got = {n: r[f"out_{n}"] for n in OUTS}
    c_ = np_.ascontiguousarray
    Cn = got["new_Cn"].transpose(1, 2, 0, 3)
    return (
        got["y_prompt"][None],
        c_(got["y_sample"].transpose(1, 0, 2)).reshape(1, DEC, D),
        c_(Cn[..., 0:DH])[None, None],
        c_(Cn[..., DH])[None, None],
        c_(got["new_m"].T)[None, None],
        c_(got["new_ret"].transpose(1, 2, 0, 3))[None, None],
        c_(got["new_ssd"].transpose(2, 0, 3, 1)).reshape(1, 1, 2, H_C, P_C, N_C),
    )
```

```python
import numpy as np
import concourse.bass as bass
from concourse import mybir
from contextlib import ExitStack

D = 1024
P = 128
SEQ, DEC = 128, 512
T = SEQ + DEC
NT = T // P
KD = D // P
DEPTH = 2
GRID_W = 64
ALPHA = (2.0 * DEPTH) ** 0.25
EPS = 1e-5
NH = 4
DH = 128
W_A = NH * DH
D_INNER = 2 * D
P_C, N_C, G_C, J_C = 64, 128, 4, 8
H_C = G_C * J_C
D_CONV = 5
CONV_DIM = D_INNER + 2 * G_C * N_C
GC = J_C * P_C
N_KEYS, H_P, TOPK = 128, 8, 16
HK = H_P * TOPK
NMOD = 6 * D
SLICE = 256
NSLOT = 8
NRAW = 4
NSPLIT = 2
NVRAW = 2
NVSPLIT = 4
NB = 8 + 64 + 64
JB = 8
JV = 4
NBLK = N_KEYS // JB
HT = T // 2
NEG = -1.0e30


class Chain:

    def __init__(self, eng, sem):
        self.eng, self.sem, self.n = eng, sem, 0

    def do(self, ins):
        ins.then_inc(self.sem, 1)
        self.n = self.n + 1

    def settle(self):
        self.eng.wait_ge(self.sem, self.n)

    def link(self, ins):
        self.do(ins)
        self.settle()


def trunk(nc, a, o, upto):
    f32 = mybir.dt.float32
    f32r = mybir.dt.float32r
    u32 = mybir.dt.uint32
    ALU = mybir.AluOpType
    ACT = mybir.ActivationFunctionType
    AX = mybir.AxisListType.X

    stages = ["mod", "even", "peer0", "odd", "peer1"]
    run = stages[: stages.index(upto) + 1] if upto else stages

    ctx = ExitStack()

    def sb(name, shape, dt=f32, scope=None):
        return (scope or ctx).enter_context(nc.sbuf_tensor(name, shape, dt))

    def sem(name):
        return ctx.enter_context(nc.semaphore(name))

    x = sb("x", [P, NT, D])
    wsc = ExitStack()
    wideR = sb("wideR", [P, 2 * NT * D], f32r, scope=wsc)
    wsc.close()
    wide = sb("wide", [P, 2 * NT * D])
    f = wide[:, 0:NT * D].rearrange("p (n d) -> p n d", n=NT)
    hi = wide[:, NT * D:2 * NT * D]
    ident = sb("ident", [P, P])
    ones = sb("ones", [P, P])
    modT = sb("modT", [P, DEPTH, 4, KD, 2])
    cT = sb("cT", [P, KD, 2])
    stat = sb("stat", [P, 20, 6])
    mv = sb("mv", [P, 20, 2])
    rstd = sb("rstd", [P, 20])
    eps = sb("eps", [P, 1])
    PS = ctx.enter_context(nc.psum_tensor("PS", [P, 8, 512], f32))

    gdram = nc.dram_tensor("gate_rows", [DEPTH, 2, 2, D], f32, kind="Internal").ap()
    Ad = nc.dram_tensor("expert_acts", [NBLK, P, JB, T], f32, kind="Internal").ap()
    Gd = nc.dram_tensor("expert_gates", [NBLK, P, T // 16, JB, 16], f32, kind="Internal").ap()

    mx = ExitStack()
    ring = sb("ring", [P, NSLOT, KD * SLICE], scope=mx)
    hT = sb("hT", [P, KD, T], scope=mx)
    base = ExitStack()
    mrow = sb("mrow", [2, NMOD], scope=base)
    bmod = wide[0:2, 4 * D:4 * D + NMOD]
    base.close()

    ev = ExitStack()
    qT = sb("qT", [P, NH, T], scope=ev)
    kT = sb("kT", [P, NH, T], scope=ev)
    v1 = sb("v1", [P, NT, NH, DH + 1], scope=ev)
    ktok = hi[:, 0:NT * W_A].rearrange("p (n h d) -> p n h d", n=NT, h=NH)
    og = hi[:, NT * W_A:2 * NT * W_A].rearrange("p (n d) -> p n d", n=NT)
    row = sb("row", [NH, 2, T], scope=ev)
    small = sb("gate_small", [NH, 6, 2, NT], scope=ev)
    BE, ML, MP, DEC_, BM = (small[:, i] for i in range(5))
    m0 = sb("m0", [NH, 2], scope=ev)
    gbias = sb("gbias", [NH, 4], scope=ev)
    sel4 = sb("sel4", [NH, NH, P], scope=ev)
    cols = sb("cols", [P, NT, 4, 2, NH], scope=ev)
    decB = sb("decB", [P, NH, 2, NT], scope=ev)
    Cst = sb("Cst", [P, 2, NH, DH + 1], scope=ev)
    Cout = sb("Cout", [P, 2, NH, DH + 1], scope=ev)
    mask = sb("mask", [P, 2, P], scope=ev)
    Dm = sb("Dm", [P, 2, NH, P], scope=ev)
    diff = sb("diff", [P, 2, P], scope=ev)
    icol = sb("icol", [P, 4], scope=ev)
    lg = sb("lg", [P, 2, NH], scope=ev)
    xz = sb("xz", [P, 3, 2, NH], scope=ev)
    gn = sb("gn", [P, 2, W_A], scope=ev)
    eb = sb("eb", [P, 2, P], scope=ev)
    pb = sb("pb", [P, 2, P], scope=ev)
    kw = sb("kw", [P, 2, P], scope=ev)
    nd = sb("nd", [P, 2, DH + 2], scope=ev)
    ev.close()
    grow = wide[0:NH, 0:4 * 2 * T].rearrange("p (k d t) -> p k d t", k=4, d=2)
    b_m = hi[0:NH, 0:4 * T].rearrange("p (k d t) -> p k d t", k=2, d=2)

    ln = ExitStack()
    rowsB = sb("rowsB", [P, 4, D], scope=ln)
    ln.close()

    od = ExitStack()
    xs = sb("xs", [P, NT, GC], scope=od)
    BC = sb("BC", [P, 2, T], scope=od)
    Btok = sb("Btok", [P, NT, N_C], scope=od)
    hst = sb("hst", [P, 2, GC], scope=od)
    hout = sb("hout", [P, 2, GC], scope=od)
    EP = sb("EP", [P, 2, J_C, P], scope=od)
    cpad = sb("cpad", [P, 2, T + 8], scope=od)
    cacc = sb("cacc", [P, 2, T + 2], scope=od)
    sx = EP[:].rearrange("p a j t -> p a (j t)")[:, :, 0:T]
    dtc = sb("dtc", [P, NT, 2, H_C], scope=od)
    av = sb("av", [P, NT, 2, H_C], scope=od)
    nac = sb("nac", [P, NT, 2, H_C], scope=od)
    wup = sb("wup", [P, NT, 2, H_C], scope=od)
    win = sb("win", [P, NT, 2, H_C], scope=od)
    dcy = sb("dcy", [P, NT, 2, H_C], scope=od)
    tri = sb("tri", [P, 2, P], scope=od)
    maskO = sb("maskO", [P, 2, P], scope=od)
    brow = sb("brow", [P, 3, 2 * H_C], scope=od)
    cw = sb("cw", [P, 24, D_CONV + 1], scope=od)
    otmp = sb("otmp", [P, GC], scope=od)
    xw = sb("xw", [P, GC], scope=od)
    od.close()
    oz = ExitStack()
    yT = sb("yT", [P, 2 * KD, T], scope=oz)
    zt = sb("zt", [P, 2, SLICE], scope=oz)
    nw = sb("nw", [P, 2 * KD], scope=oz)
    ssq = sb("ssq", [P, NT], scope=oz)
    rowsO = sb("rowsO", [P, 4, D], scope=oz)
    oz.close()
    y = wide[:, :].rearrange("p (n d) -> p n d", n=NT)

    mx.close()

    pu = ExitStack()
    hH = sb("hH", [P, KD, T], f32r, scope=pu)
    hL = sb("hL", [P, KD, T], f32r, scope=pu)
    raw = sb("raw", [P, NRAW, KD * SLICE], scope=pu)
    wH = sb("wH", [P, NSPLIT, KD * SLICE], f32r, scope=pu)
    wL = sb("wL", [P, NSPLIT, KD * SLICE], f32r, scope=pu)
    hkT = sb("hkT", [P, 3, T], scope=pu)
    abuf = sb("abuf", [P, 2, 2, T], scope=pu)
    iota = sb("iota", [P, N_KEYS], scope=pu)
    ps_ = ExitStack()
    sv = sb("sv", [P, NT, H_P, 2, TOPK], scope=ps_)
    si = sb("si", [P, NT, H_P, 2, TOPK], u32, scope=ps_)
    qb = sb("qb", [P, 2, T], scope=ps_)
    swork = sb("swork", [P, N_KEYS], scope=ps_)
    sif = sb("sif", [P, H_P, 2, TOPK], scope=ps_)
    best = sb("best", [P, NT, H_P, TOPK], scope=ps_)
    pos = sb("pos", [P, H_P, TOPK], u32, scope=ps_)
    posi = sb("posi", [P, 2, HK], u32, scope=ps_)
    posf = sb("posf", [P, 2, HK], scope=ps_)
    ssum = sb("ssum", [P, NT, H_P], scope=ps_)
    ps_.close()
    gH = sb("gH", [P, T], f32r, scope=pu)
    gL = sb("gL", [P, T], scope=pu)
    pu.close()
    htmp = wide[:, 0:2 * T].rearrange("p (s t) -> p s t", s=2)
    eqb = wide[:, 0:TOPK * HK].rearrange("p (a b) -> p a b", b=TOPK)
    eqc = wide[:, TOPK * HK:2 * TOPK * HK].rearrange("p (a b) -> p a b", b=TOPK)
    gst = wide[:, 0:4096].rearrange("p (s j t) -> p s j t", s=2, j=P)
    hot = wideR[:, 4096:10240].rearrange("p (s c t i) -> p s c t i", s=2, c=3, t=8)
    cand = wide[:, 4096:4096 + 2 * TOPK * TOPK].rearrange("p (s n) -> p s n", s=2)
    hkt = wide[:, 6144:8064].rearrange("p (t c k) -> p t c k", t=NT, c=3)
    keys = wide[:, 8192:10240].rearrange("p (c n) -> p c n", c=2 * H_P)

    pv = ExitStack()
    wHv = sb("wHv", [P, NVSPLIT, 2 * D], f32r, scope=pv)
    wLv = sb("wLv", [P, NVSPLIT, 2 * D], f32r, scope=pv)
    rawV = sb("rawV", [P, NVRAW, 2 * D], scope=pv)
    WH = sb("WH", [P, 2, JV, T], f32r, scope=pv)
    WL = sb("WL", [P, 2, JV, T], f32r, scope=pv)
    rows_scope = ExitStack()
    rowsP = sb("rowsP", [P, 4, D], scope=rows_scope)
    rows_scope.close()
    gb = sb("gb", [P, T // 16, JB, 16], scope=pv)
    pv.close()
    ab = hi.rearrange("p (j t) -> p j t", j=JB)

    products = sem("products")
    slot_full = [sem(f"slot_full{i}") for i in range(NSLOT)]
    vec_chain, act_chain, pool_chain = sem("vec_chain"), sem("act_chain"), sem("pool_chain")
    consts_ready, small_loaded = sem("consts_ready"), sem("small_loaded")
    c_ready, mod_evac, mod_rows, mod_cols = sem("c_ready"), sem("mod_evac"), sem("mod_rows"), sem("mod_cols")
    gates_stored, x_loaded, x_ready = sem("gates_stored"), sem("x_loaded"), sem("x_ready")
    h_evac_v, h_evac_a = sem("h_evac_v"), sem("h_evac_a")
    rows_loaded, var_ready, dev_ready, f_ready = sem("rows_loaded"), sem("var_ready"), sem("dev_ready"), sem("f_ready")
    stored = sem("stored")
    even_loaded, proj_a, proj_v = sem("even_loaded"), sem("proj_a"), sem("proj_v")
    gate_exp, gate_act, gates_done, cols_ready = sem("gate_exp"), sem("gate_act"), sem("gates_done"), sem("cols_ready")
    e_ready, exp_ready, p_ready, kw_ready = sem("e_ready"), sem("exp_ready"), sem("p_ready"), sem("kw_ready")
    h_done, state_ready, ret_ready = sem("h_done"), sem("state_ready"), sem("ret_ready")
    diff_ready, decay_ready, norm_done, og_ready = sem("diff_ready"), sem("decay_ready"), sem("norm_done"), sem("og_ready")
    out_evac = sem("out_evac")
    odd_loaded, dt_abs, dt_sp, a_ready, ac_ready, seg_exp = (sem(n) for n in
        ("odd_loaded", "dt_abs", "dt_sp", "a_ready", "ac_ready", "seg_exp"))
    pad_filled, conv_done, act_done, tr_evac, oe_ready, oexp_ready, op_ready, skip_ready, y_intra = (sem(n) for n in
        ("pad_filled", "conv_done", "act_done", "tr_evac", "oe_ready", "oexp_ready", "op_ready", "skip_ready", "y_intra"))
    inter_done, xw_ready, upd_done, hst_loaded, hst_stored, z_silu, z_used, ssq_done, yt_v, yt_a, oo_evac = (sem(n) for n in
        ("inter_done", "xw_ready", "upd_done", "hst_loaded", "hst_stored", "z_silu", "z_used", "ssq_done", "yt_v", "yt_a", "oo_evac"))
    keys_loaded, q_evac, s_used, hk_ready, hk_evac, sm_exp, sm_sub = (sem(n) for n in
        ("keys_loaded", "q_evac", "s_used", "hk_ready", "hk_evac", "sm_exp", "sm_sub"))
    act_gelu, a_stored, hot_ready, g_evac, g_stored, ag_loaded, w_ready, acc_done, iota_ready = (sem(n) for n in
        ("act_gelu", "a_stored", "hot_ready", "g_evac", "g_stored", "ag_loaded0", "w_ready", "acc_done", "iota_ready"))
    ag_loaded, a_stored, g_stored = [ag_loaded, sem("ag_loaded1")], [a_stored, sem("a_stored1")], [g_stored, sem("g_stored1")]
    ev_consts, od_consts, dm_ready, decay_exp, alog_exp, nw_loaded, rr_ready = (sem(n) for n in
        ("ev_consts", "od_consts", "dm_ready", "decay_exp", "alog_exp", "nw_loaded", "rr_ready"))

    raw_full = [sem(f"raw_full{i}") for i in range(NRAW)]
    vraw_full = [sem(f"vraw_full{i}") for i in range(NVRAW)]
    hi_ready, lo_ready, hh_ready, hl_ready, wf_ready, wh_ready, ag_full = (sem(n) for n in
        ("hi_ready", "lo_ready", "hh_ready", "hl_ready", "wf_ready", "wh_ready", "ag_full"))

    at = {}
    slices = []
    UNITS = [(s, h, d) for s in range(NT) for h in range(NH) for d in range(2)]
    NU = len(UNITS)

    def tile_of(step, d):
        return step if d == 0 or step == 0 else NT - step

    def first_on(step, d):
        t = tile_of(step, d)
        other = t if d == 1 else (NT - t if t else 0)
        return step < other or (step == other and d == 0)

    def bc(v, n):
        return v.unsqueeze(len(v.shape)).broadcast_to(list(v.shape) + [n])

    at_h = {0: 0, 4: KD, 1: 2 * KD, 2: 3 * KD, 3: 4 * KD}

    proj = []
    for fam in range(2):
        if fam == 0:
            proj.append(("gate", 0, 0, "v"))
        proj += [("q", fam, i, "a") for i in range(NH)] + [("k", fam, i, "a") for i in range(NH)]
        proj += [("v", fam, (s, t), "v") for s in range(2) for t in range(NT)]
        proj += [("o", fam, (s, t), "a") for s in range(2) for t in range(NT)]
        proj += [("kt", fam, t, "v") for t in range(NT)]
    proj_count, n_a, n_v = {}, 0, 0
    for i, (kind, fam, m, e) in enumerate(proj):
        n_a, n_v = n_a + (e == "a"), n_v + (e == "v")
        proj_count[kind, fam, m] = (i, e, n_a if e == "a" else n_v)

    with ctx, nc.Block() as block:

        @block.tensor
        def _(pe):
            state = {"n": 0, "slice": 0}

            def done(ins, label):
                ins.then_inc(products, 1)
                state["n"] = state["n"] + 1
                at[label] = state["n"]

            def take(src):
                n = state["slice"]
                state["slice"] += 1
                pe.wait_ge(slot_full[n % NSLOT], 16 * (n // NSLOT + 1))
                slices.append([src, None])
                return ring[:, n % NSLOT, 0:src.shape[-1]]

            def release(label):
                slices[-1][1] = label

            def evacuated(kind, fam, m):
                _, e, n = proj_count[kind, fam, m]
                pe.wait_ge(proj_a if e == "a" else proj_v, n)

            pe.wait_ge(consts_ready, 1)
            pe.wait_ge(c_ready, 1)
            for l in range(DEPTH):
                for s in range(NMOD // SLICE):
                    g = l * (NMOD // SLICE) + s
                    w = take(a["w_mod"][l, s]).rearrange("p (k n) -> p k n", k=KD)
                    if g >= 4:
                        pe.wait_ge(mod_evac, g - 3)
                    for k in range(KD):
                        last = nc.tensor.matmul(PS[0:2, g % 4, 0:SLICE], cT[:, k, :], w[:, k, :],
                                                start=(k == 0), stop=(k == KD - 1))
                    done(last, ("mod", l, s))
                    release(("mod", l, s))
                pe.wait_ge(mod_rows, l + 1)
                if l:
                    pe.wait_ge(mod_cols, l)
                for i, kind in enumerate((0, 1, 3, 4)):
                    for k in range(KD):
                        c = (i * KD + k) * 2
                        last = nc.tensor.matmul(PS[:, 4, c:c + 2], mrow[0:2, kind * D + k * P:kind * D + (k + 1) * P],
                                                ident[0:2, 0:2], start=True, stop=True)
                done(last, ("fold", l))

            def modulated(n):
                pe.wait_ge(x_ready, n + 1)
                pe.wait_ge(mod_cols, DEPTH)
                for k in range(KD):
                    if k >= 4:
                        pe.wait_ge(h_evac_v, at_h[n] + k - 3)
                        pe.wait_ge(h_evac_a, at_h[n] + k - 3)
                    b = 2 * (k % 4)
                    for t in range(NT):
                        dst = PS[:, b, 0:P] if t == 0 else PS[:, b + 1, (t - 1) * P:t * P]
                        last = nc.tensor.transpose(dst, x[:, t, k * P:(k + 1) * P], ident[:])
                    done(last, ("h", n, k))
                pe.wait_ge(h_evac_v, at_h[n] + KD)
                pe.wait_ge(h_evac_a, at_h[n] + KD)

            def feature_major(w, m, pair):
                for half in range(2):
                    for k in range(KD):
                        last = nc.tensor.matmul(PS[:, 2 * pair + half, 0:HT], w[:, k, m * P:(m + 1) * P],
                                                hT[:, k, half * HT:(half + 1) * HT], start=(k == 0), stop=(k == KD - 1))
                return last

            def even():
                modulated(0)
                pe.wait_ge(ev_consts, 1)

                def pair_of(kind, fam, m):
                    i = proj_count[kind, fam, m][0]
                    if i >= 4:
                        evacuated(*proj[i - 4][:3])
                    return i % 4

                for fam in range(2):
                    if fam == 0:
                        w = take(a["w_gate"]).rearrange("p (k n) -> p k n", k=KD)
                        done(feature_major(w, 0, pair_of("gate", 0, 0)), ("gate",))
                        release(("gate",))
                    else:
                        pe.wait_ge(h_done, NU)
                        pe.wait_ge(state_ready, NU - 2 * NH)
                    for kind in ("q", "k"):
                        for i in range(NH):
                            if i % 2 == 0:
                                w = take(a["w_even"][fam, {"q": 0, "k": 1}[kind], i // 2]).rearrange("p (k n) -> p k n", k=KD)
                            done(feature_major(w, i % 2, pair_of(kind, fam, i)), (kind, fam, i))
                            release((kind, fam, i))
                    for kind in ("v", "o"):
                        for s in range(2):
                            w = take(a["w_even"][fam, {"v": 2, "o": 3}[kind], s]).rearrange("p (k n) -> p k n", k=KD)
                            for t in range(NT):
                                pr = pair_of(kind, fam, (s, t))
                                for k in range(KD):
                                    last = nc.tensor.matmul(PS[:, 2 * pr, 0:SLICE], hT[:, k, t * P:(t + 1) * P], w[:, k, :],
                                                            start=(k == 0), stop=(k == KD - 1))
                                done(last, (kind, fam, (s, t)))
                            release((kind, fam, (s, NT - 1)))
                    if fam == 0:
                        pe.wait_ge(gates_done, 1)
                        evacuated("o", 0, (1, NT - 1))
                        evacuated("v", 0, (1, NT - 1))
                        for t in range(NT):
                            for kind in range(4):
                                for d in range(2):
                                    c = ((t * 4 + kind) * 2 + d) * NH
                                    last = nc.tensor.matmul(PS[:, 7, c:c + NH], grow[:, kind, d, t * P:(t + 1) * P],
                                                            ident[0:NH, 0:NH], start=True, stop=True)
                        for h in range(NH):
                            last = nc.tensor.matmul(PS[:, 7, 256 + h * 2 * NT:256 + (h + 1) * 2 * NT], sel4[:, h, :],
                                                    DEC_.rearrange("p d t -> p (d t)"), start=True, stop=True)
                        done(last, ("cols",))
                        pe.wait_ge(cols_ready, 1)
                    evacuated("k", fam, NH - 1)
                    for t in range(NT):
                        pr = pair_of("kt", fam, t)
                        for h in range(NH):
                            last = nc.tensor.transpose(PS[:, 2 * pr, h * P:(h + 1) * P], kT[:, h, t * P:(t + 1) * P], ident[:])
                        done(last, ("kt", fam, t))
                    evacuated("kt", fam, NT - 1)
                    evacuated("o", fam, (1, NT - 1))
                    evacuated("v", fam, (1, NT - 1))
                    width = DH + 1 if fam == 0 else DH
                    for i in range(NU + 2):
                        if i < NU:
                            s, h, d = UNITS[i]
                            t = tile_of(s, d)
                            if i >= 2:
                                pe.wait_ge(p_ready, fam * NU + i - 1)
                            last = nc.tensor.matmul(PS[:, i % 2, 0:P], kT[:, h, t * P:(t + 1) * P], qT[:, h, t * P:(t + 1) * P],
                                                    start=True, stop=True)
                            if fam == 0:
                                last = nc.tensor.matmul(PS[:, i % 2, P:2 * P], sel4[:, h, :], row[:, d, t * P:(t + 1) * P],
                                                        start=True, stop=True)
                            done(last, ("S", fam, i))
                        u = i - 2
                        if u >= 0:
                            s, h, d = UNITS[u]
                            t = tile_of(s, d)
                            pe.wait_ge(p_ready, fam * NU + u + 1)
                            if u >= 2:
                                pe.wait_ge(h_done, fam * NU + u - 1)
                            if s < NT - 1:
                                pe.wait_ge(kw_ready, fam * (NU - 2 * NH) + u + 1)
                                last = nc.tensor.matmul(PS[:, 4 + u % 2, 0:width], kw[:, u % 2, :], v1[:, t, h, 0:width],
                                                        start=True, stop=True)
                            if s > 0:
                                pe.wait_ge(even_loaded, 80)
                                if fam == 1:
                                    pe.wait_ge(ret_ready, 16)
                                if s > 1:
                                    pe.wait_ge(state_ready, fam * (NU - 2 * NH) + u - 2 * NH + 1)
                                nc.tensor.matmul(PS[:, 2 + u % 2, 256:256 + width], qT[:, h, t * P:(t + 1) * P],
                                                 Cst[:, d, h, 0:width], start=True, stop=True)
                            last = nc.tensor.matmul(PS[:, 2 + u % 2, 0:width], pb[:, u % 2, :], v1[:, t, h, 0:width],
                                                    start=True, stop=True)
                            done(last, ("H", fam, u))
                pe.wait_ge(norm_done, 2)
                for k in range(KD):
                    if k >= 4:
                        pe.wait_ge(h_evac_v, at_h[4] + k - 3)
                        pe.wait_ge(h_evac_a, at_h[4] + k - 3)
                    b = 2 * (k % 4)
                    for t in range(NT):
                        dst = PS[:, b, 0:P] if t == 0 else PS[:, b + 1, (t - 1) * P:t * P]
                        last = nc.tensor.transpose(dst, f[:, t, k * P:(k + 1) * P], ident[:])
                    done(last, ("h", 4, k))
                pe.wait_ge(h_evac_v, at_h[4] + KD)
                pe.wait_ge(h_evac_a, at_h[4] + KD)
                g = 0
                for s in range(D // SLICE):
                    w = take(a["w_eout"][s]).rearrange("p (k n) -> p k n", k=KD)
                    for t in range(NT):
                        if g >= 8:
                            pe.wait_ge(out_evac, g - 7)
                        for k in range(KD):
                            last = nc.tensor.matmul(PS[:, g % 8, 0:SLICE], hT[:, k, t * P:(t + 1) * P], w[:, k, :],
                                                    start=(k == 0), stop=(k == KD - 1))
                        done(last, ("eo", s, t))
                        g += 1
                    release(("eo", s, NT - 1))

            def split_products(out, lhsH, lhsL, rhsH, rhsL, start, stop):
                nc.tensor.matmul(out, lhsH, rhsH, start=start, stop=False)
                nc.tensor.matmul(out, lhsH, rhsL, start=False, stop=False)
                return nc.tensor.matmul(out, lhsL, rhsH, start=False, stop=stop)

            def feature_major_split(slot, m, pair):
                for half in range(2):
                    c = slice(half * HT, (half + 1) * HT)
                    for k in range(KD):
                        w = slice(k * SLICE + m * P, k * SLICE + (m + 1) * P)
                        last = split_products(PS[:, 2 * pair + half, 0:HT], wH[:, slot, w], wL[:, slot, w], hH[:, k, c], hL[:, k, c],
                                              k == 0, k == KD - 1)
                return last

            def peer(l):
                modulated(2 * l + 1)
                pe.wait_ge(hl_ready, KD * (l + 1))
                for m in range(2 * H_P):
                    g = l * 2 * H_P + m
                    if m % 2 == 0:
                        pe.wait_ge(lo_ready, l * NB + m // 2 + 1)
                    if m >= 2:
                        pe.wait_ge(q_evac, g - 1)
                    done(feature_major_split(m // 2 % NSPLIT, m % 2, m % 2), ("pq", l, m))
                    if m == 0:
                        pe.wait_ge(keys_loaded, 16 * (l + 1))
                    pe.wait_ge(q_evac, g + 1)
                    if m >= 2:
                        pe.wait_ge(s_used, NT * (g - 1))
                    for t in range(NT):
                        b = 4 + 2 * (m % 2) + (t == NT - 1)
                        last = nc.tensor.matmul(PS[:, b, (t % 4) * P:(t % 4 + 1) * P], qb[:, m % 2, t * P:(t + 1) * P],
                                                keys[:, m, :], start=True, stop=True)
                    done(last, ("ps", l, m))
                base_n = state["n"]

                def act_pass(i, build):
                    for jj in range(16):
                        gj = l * N_KEYS + i * 16 + jj
                        if jj % 2 == 0:
                            pe.wait_ge(lo_ready, l * NB + 8 + 8 * i + jj // 2 + 1)
                        if not (isinstance(i, int) and i == 0 and jj < 2 and l == 0):
                            pe.wait_ge(act_gelu, gj - 1)
                        feature_major_split(jj // 2 % NSPLIT, jj % 2, jj % 2).then_inc(products, 1)
                        if build:
                            gq = l * 80 + (i - 3) * 16 + jj
                            pe.wait_ge(hot_ready, gq + 1)
                            if not (isinstance(i, int) and l == 0 and i == 3 and jj < 2):
                                pe.wait_ge(g_evac, gq - 1)
                            for tk in range(8):
                                b = 4 + 2 * (jj % 2) + tk // 4
                                dst = PS[:, b, (tk % 4) * P:(tk % 4 + 1) * P]
                                nc.tensor.matmul(dst, hot[:, jj % 2, 0, tk, :], hot[:, jj % 2, 1, tk, :], start=True, stop=False)
                                last = nc.tensor.matmul(dst, hot[:, jj % 2, 0, tk, :], hot[:, jj % 2, 2, tk, :], start=False, stop=True)
                            last.then_inc(products, 1)

                act_pass(0, False)
                with pe.Fori(1, 3) as i:
                    act_pass(i, False)
                n_tr = base_n + 3 * 16
                for t in range(NT):
                    if t == 0:
                        pe.wait_ge(hk_ready, l + 1)
                    if t >= 2:
                        pe.wait_ge(hk_evac, l * NT + t - 1)
                    for c in range(3):
                        last = nc.tensor.transpose(PS[:, 4 + t % 2, c * P:(c + 1) * P], hkt[:, t, c, :], ident[:])
                    last.then_inc(products, 1)
                    at["hk", l, t] = n_tr + t + 1
                pe.wait_ge(hk_evac, l * NT + NT)
                n_b = n_tr + NT
                at["u", l], at["ub", l] = base_n, n_b
                act_pass(3, True)
                with pe.Fori(4, 8) as i:
                    act_pass(i, True)
                state["n"] = n_b + 5 * 32
                base_n = state["n"]
                at["v", l] = base_n
                slices.append(["peer", l])

                def value_pass(i):
                    for q in range(4):
                        blk = 4 * i + q
                        pe.wait_ge(lo_ready, l * NB + 72 + 2 * blk + 2)
                        pe.wait_ge(w_ready, l * 32 + blk + 1)
                        for t in range(NT):
                            pr = (q * NT + t) % 4
                            gg = (l * 32 + blk) * NT + t
                            if not (isinstance(i, int) and q * NT + t < 4 and l == 0):
                                pe.wait_ge(acc_done, gg - 3)
                            for c in range(2):
                                for j in range(JV):
                                    slot, v = 2 * (q % 2) + j // 2, slice((j % 2) * D + c * 512, (j % 2) * D + (c + 1) * 512)
                                    tt = slice(t * P, (t + 1) * P)
                                    last = split_products(PS[:, 2 * pr + c, :], WH[:, q % 2, j, tt], WL[:, q % 2, j, tt],
                                                          wHv[:, slot, v], wLv[:, slot, v], j == 0, j == JV - 1)
                            last.then_inc(products, 1)

                value_pass(0)
                with pe.Fori(1, 8) as i:
                    value_pass(i)
                state["n"] = base_n + 32 * NT
                at["v_end", l] = state["n"]

            def odd():
                modulated(2)
                w = take(a["w_dt"]).rearrange("p (k n) -> p k n", k=KD)
                for t in range(NT):
                    for k in range(KD):
                        last = nc.tensor.matmul(PS[:, 0, t * 64:(t + 1) * 64], hT[:, k, t * P:(t + 1) * P], w[:, k, 0:64],
                                                start=(k == 0), stop=(k == KD - 1))
                done(last, ("dt",))
                release(("dt",))
                pe.wait_ge(a_ready, 1)
                for t in range(NT):
                    for d in range(2):
                        c = (t * 2 + d) * H_C
                        nc.tensor.matmul(PS[:, 1, c:c + H_C], tri[:, d, :], av[:, t, d, :], start=True, stop=True)
                last = nc.tensor.matmul(PS[:, 2, 0:NT * 64], ones[:], av[:].rearrange("p t d h -> p (t d h)"), start=True, stop=True)
                done(last, ("acum",))
                pe.wait_ge(ac_ready, 1)
                for g in range(G_C):
                    for m in range(7):
                        q = g * 6 + m
                        if m < 6:
                            if m % 2 == 0:
                                w = take(a["w_xbc"][g, m // 2]).rearrange("p (k n) -> p k n", k=KD)
                            if q >= 2:
                                pe.wait_ge(pad_filled, q - 1)
                            b = 2 * (m % 2)
                            for k in range(KD):
                                nc.tensor.matmul(PS[:, b, 0:P], w[:, k, (m % 2) * P:(m % 2 + 1) * P], hT[:, k, 0:P],
                                                 start=(k == 0), stop=(k == KD - 1))
                            for k in range(KD):
                                last = nc.tensor.matmul(PS[:, b + 1, :], w[:, k, (m % 2) * P:(m % 2 + 1) * P], hT[:, k, P:T],
                                                        start=(k == 0), stop=(k == KD - 1))
                            done(last, ("xbc", g, m))
                            if m % 2 == 1:
                                release(("xbc", g, m))
                        mm = m - 1
                        if 0 <= mm < 5:
                            qq = g * 6 + mm
                            src = sx[:, mm % 2, :] if mm < 4 else BC[:, 0, :]
                            pe.wait_ge(act_done, qq + 1)
                            n = g * 5 + mm
                            if n >= 2:
                                pe.wait_ge(tr_evac, n - 1)
                            for t in range(NT):
                                b = 4 + 2 * (n % 2) + (t == NT - 1)
                                last = nc.tensor.transpose(PS[:, b, (t % 4) * P:(t % 4 + 1) * P], src[:, t * P:(t + 1) * P], ident[:])
                            done(last, ("xt", g, mm))
                    pe.wait_ge(act_done, g * 6 + 6)
                    pe.wait_ge(pad_filled, g * 6 + 6)
                    pe.wait_ge(tr_evac, g * 5 + 5)
                    for t in range(NT):
                        n = g * NT + t
                        if n >= 1:
                            pe.wait_ge(op_ready, 2 * n)
                        nc.tensor.matmul(PS[:, 4, 0:P], BC[:, 0, t * P:(t + 1) * P], BC[:, 1, t * P:(t + 1) * P], start=True, stop=True)
                        for d in range(2):
                            if 2 * n + d >= 1:
                                pe.wait_ge(oe_ready, 2 * n + d)
                            for j in range(J_C):
                                last = nc.tensor.matmul(PS[:, 5 + j // 4, (j % 4) * P:(j % 4 + 1) * P],
                                                        av[:, t, d, g * J_C + j:g * J_C + j + 1].broadcast_to([P, P]),
                                                        tri[:, d, :], start=True, stop=True)
                            done(last, ("seg", g, t, d))
                        pe.wait_ge(op_ready, 2 * n + 2)
                        if n >= 1:
                            pe.wait_ge(y_intra, n)
                        for j in range(J_C):
                            for d in range(2):
                                last = nc.tensor.matmul(PS[:, 7, j * P_C:(j + 1) * P_C], EP[:, d, j, :], xs[:, t, j * P_C:(j + 1) * P_C],
                                                        start=(d == 0), stop=(d == 1))
                        done(last, ("intra", g, t))
                    pe.wait_ge(y_intra, g * NT + NT)
                    pe.wait_ge(hst_loaded, 16 * (g + 1))
                    for s in range(NT):
                        for d in range(2):
                            t = tile_of(s, d)
                            n, nu = (g * 4 + s - 1) * 2 + d, (g * 4 + s) * 2 + d
                            if s > 0:
                                if n >= 1:
                                    pe.wait_ge(inter_done, n)
                                if s > 1:
                                    pe.wait_ge(upd_done, nu - 1)
                                last = nc.tensor.matmul(PS[:, n % 2, :], BC[:, 1, t * P:(t + 1) * P], hst[:, d, :], start=True, stop=True)
                                done(last, ("inter", g, s, d))
                            if s < NT - 1:
                                pe.wait_ge(xw_ready, nu + 1)
                                if nu >= 1:
                                    pe.wait_ge(upd_done, nu)
                                last = nc.tensor.matmul(PS[:, 2 + nu % 2, :], Btok[:, t, :], xw[:, :], start=True, stop=True)
                                done(last, ("upd", g, s, d))
                    pe.wait_ge(inter_done, (g + 1) * 8)
                    pe.wait_ge(upd_done, (g + 1) * 8)
                for s in range(D_INNER // SLICE):
                    w = take(a["w_z"][s]).rearrange("p (k n) -> p k n", k=KD)
                    for t in range(NT):
                        n = s * NT + t
                        if n >= 4:
                            pe.wait_ge(z_silu, n - 3)
                        for k in range(KD):
                            last = nc.tensor.matmul(PS[:, n % 4, 0:SLICE], hT[:, k, t * P:(t + 1) * P], w[:, k, :],
                                                    start=(k == 0), stop=(k == KD - 1))
                        done(last, ("z", s, t))
                    release(("z", s, NT - 1))
                pe.wait_ge(z_used, D_INNER // SLICE * NT)
                for k in range(2 * KD):
                    if k >= 4:
                        pe.wait_ge(yt_v, k - 3)
                        pe.wait_ge(yt_a, k - 3)
                    b = 2 * (k % 4)
                    for t in range(NT):
                        dst = PS[:, b, 0:P] if t == 0 else PS[:, b + 1, (t - 1) * P:t * P]
                        last = nc.tensor.transpose(dst, y[:, t, k * P:(k + 1) * P], ident[:])
                    done(last, ("yt", k))
                pe.wait_ge(yt_v, 2 * KD)
                pe.wait_ge(yt_a, 2 * KD)
                for s in range(KD):
                    w = take(a["w_oout"][s]).rearrange("p (k n) -> p k n", k=2 * KD)
                    for t in range(NT):
                        n = s * NT + t
                        if n >= 8:
                            pe.wait_ge(oo_evac, n - 7)
                        for k in range(2 * KD):
                            last = nc.tensor.matmul(PS[:, n % 8, 0:P], yT[:, k, t * P:(t + 1) * P], w[:, k, :],
                                                    start=(k == 0), stop=(k == 2 * KD - 1))
                        done(last, ("oo", s, t))
                    release(("oo", s, NT - 1))

            if "even" in run:
                even()
            if "peer0" in run:
                peer(0)
            if "odd" in run:
                odd()
            if "peer1" in run:
                peer(1)

        @block.vector
        def _(ve):
            V = nc.vector
            ch = Chain(ve, vec_chain)
            do, link, settle = ch.do, ch.link, ch.settle

            def bank(b):
                return PS[:, b, :]

            ve.wait_ge(x_loaded, 48)
            V.tensor_tensor(x[:, 1:NT, :], x[:, 1:NT, :], f[:, 0:NT - 1, :], ALU.add).then_inc(x_ready, 1)
            ve.wait_ge(small_loaded, 32)
            for l in range(DEPTH):
                if l:
                    ve.wait_ge(gates_stored, 32 * l)
                    ve.wait_ge(small_loaded, 32 + 16 * l)
                for s in range(NMOD // SLICE):
                    ve.wait_ge(products, at["mod", l, s])
                    c = slice(s * SLICE, (s + 1) * SLICE)
                    V.tensor_tensor(mrow[:, c], PS[0:2, (l * 24 + s) % 4, 0:SLICE], bmod[:, c], ALU.add).then_inc(mod_evac, 1)
                ve.wait_ge(mod_evac, (l + 1) * (NMOD // SLICE))
                do(V.tensor_scalar(mrow[:, D:2 * D], mrow[:, D:2 * D], 1.0, None, ALU.add))
                V.tensor_scalar(mrow[:, 4 * D:5 * D], mrow[:, 4 * D:5 * D], 1.0, None, ALU.add).then_inc(mod_rows, 1)
                ve.wait_ge(products, at["fold", l])
                V.tensor_copy(modT[:, l].rearrange("p a k g -> p (a k g)"), PS[:, 4, 0:64]).then_inc(mod_cols, 1)

            def modulated(n):
                l, kind = n // 2, 2 * (n % 2)
                ve.wait_ge(mod_cols, l + 1)
                for k in range(KD):
                    ve.wait_ge(products, at["h", n, k])
                    V.tensor_scalar(hT[:, k, P:T], PS[:, 2 * (k % 4) + 1, :], modT[:, l, kind + 1, k, 1:2], modT[:, l, kind, k, 1:2],
                                    ALU.mult, ALU.add).then_inc(h_evac_v, 1)

            def layer_norm(n, rows):
                ve.wait_ge(rows_loaded, 48 * (n + 1))
                settle()
                for t in range(NT):
                    do(V.tensor_tensor(f[:, t, :], f[:, t, :], rows[:, 2 + (t > 0), :], ALU.mult))
                settle()
                for t in range(NT):
                    do(V.scalar_tensor_tensor(x[:, t, :], x[:, t, :], ALPHA, f[:, t, :], ALU.mult, ALU.add))
                settle()
                for t in range(NT):
                    for c in range(2):
                        do(V.bn_stats(stat[:, 2 * t + c, :], x[:, t, c * 512:(c + 1) * 512]))
                settle()
                for t in range(NT):
                    last = V.bn_aggr(mv[:, t, :], stat[:, 2 * t:2 * t + 2, :])
                    if t < NT - 1:
                        do(last)
                last.then_inc(var_ready, 1)
                ve.wait_ge(dev_ready, at_dev[n])
                link(V.reciprocal(rstd[:, 0:NT], rstd[:, 0:NT]))
                for t in range(NT):
                    do(V.tensor_scalar(x[:, t, :], x[:, t, :], mv[:, t, 0:1], rstd[:, t:t + 1], ALU.subtract, ALU.mult))
                settle()
                for t in range(NT):
                    do(V.tensor_tensor(x[:, t, :], x[:, t, :], rows[:, 0, :], ALU.mult))
                settle()
                for t in range(NT):
                    last = V.tensor_tensor(x[:, t, :], x[:, t, :], rows[:, 1, :], ALU.add)
                    if t < NT - 1:
                        do(last)
                last.then_inc(x_ready, 1)
                ve.wait_ge(x_ready, n + 2)

            at_dev = {0: 3, 1: 4, 2: 5, 3: 6}

            def even():
                modulated(0)
                ve.wait_ge(even_loaded, 80)
                ve.wait_ge(ev_consts, 1)
                ve.wait_ge(products, at["gate",])
                L, F, t1, t2 = (grow[:, i] for i in range(4))
                wg_, wint_, col_, enm_ = L, F, t1, t2
                b, m = b_m[:, 0], b_m[:, 1]
                dst = [L[:, 0], L[:, 1], F[:, 0], F[:, 1]]
                for q in range(4):
                    last = V.tensor_copy(dst[q].rearrange("p (a t) -> p a t", a=2), PS[32 * q:32 * q + NH, 0:2, 0:HT])
                    if q < 3:
                        do(last)
                last.then_inc(proj_v, 1)
                ve.wait_ge(proj_v, 1)
                for q in range(4):
                    do(V.tensor_scalar(dst[q], dst[q], gbias[:, q:q + 1], None, ALU.add))
                settle()
                V.scalar_tensor_tensor(t1, F, -1.0, F, ALU.mult, ALU.max).then_inc(gate_exp, 1)
                ve.wait_ge(gate_act, 1)
                link(V.scalar_tensor_tensor(F, F, 0.0, t1, ALU.min, ALU.subtract))
                do(V.memset(t2[:, :, 0:P], 1.0))
                settle()
                for t in range(NT):
                    c = slice(t * P, (t + 1) * P)
                    do(V.tensor_tensor_scan(b[:, 0, c], t2[:, 0, 0:P], F[:, 0, c], 0.0, ALU.mult, ALU.add))
                    r = F[:, 1, c]
                    do(V.tensor_tensor_scan(b[:, 1, c][:, ::-1], t2[:, 1, 0:P], r[:, ::-1], 0.0, ALU.mult, ALU.add))
                for c, start in ((slice(0, P), None), (slice(P, T), m0)):
                    do(V.tensor_tensor_scan(m[:, 0, c], F[:, 0, c], L[:, 0, c], 0.0 if start is None else start[:, 0:1], ALU.add, ALU.max))
                    do(V.tensor_tensor_scan(m[:, 1, c][:, ::-1], F[:, 1, c][:, ::-1], L[:, 1, c][:, ::-1],
                                            0.0 if start is None else start[:, 1:2], ALU.add, ALU.max))
                settle()
                for src, dst_ in ((b, BE), (m, ML)):
                    do(V.tensor_copy(dst_[:, 0, :], src[:, 0, :].rearrange("p (n t) -> p n t", t=P)[:, :, P - 1]))
                    do(V.tensor_copy(dst_[:, 1, :], src[:, 1, :].rearrange("p (n t) -> p n t", t=P)[:, :, 0]))
                do(V.memset(MP[:, :, 0], 0.0))
                do(V.tensor_copy(MP[:, 0, 1:2], m0[:, 0:1]))
                do(V.tensor_copy(MP[:, 1, NT - 1:NT], m0[:, 1:2]))
                settle()
                do(V.tensor_copy(MP[:, 0, 2:NT], ML[:, 0, 1:NT - 1]))
                do(V.tensor_copy(MP[:, 1, 1:NT - 1], ML[:, 1, 2:NT]))
                do(V.tensor_tensor(row[:, :, :], b, m, ALU.subtract))
                do(V.tensor_tensor(col_, L, b, ALU.subtract))
                settle()
                do(V.tensor_tensor(BM, BE, ML, ALU.subtract))
                settle()
                chunked = lambda z: z.rearrange("p d (n t) -> p (d n) t", t=P)
                flat = lambda z: z.rearrange("p d n -> p (d n)")
                do(V.tensor_tensor(chunked(F), chunked(row[:, :, :]), bc(flat(MP), P), ALU.add))
                do(V.tensor_tensor(chunked(L), chunked(col_), bc(flat(BM), P), ALU.add))
                V.tensor_tensor(DEC_, BM, MP, ALU.add).then_inc(gate_exp, 1)
                do(V.memset(v1[:, :, :, DH:DH + 1], 1.0))

                for fam in range(2):
                    for s in range(2):
                        for t in range(NT):
                            ve.wait_ge(products, at["v", fam, (s, t)])
                            V.tensor_copy(v1[:, t, 2 * s:2 * s + 2, 0:DH],
                                          PS[:, 2 * (proj_count["v", fam, (s, t)][0] % 4), 0:SLICE].rearrange("p (h d) -> p h d", h=2)
                                          ).then_inc(proj_v, 1)
                    if fam == 0:
                        ve.wait_ge(products, at["cols",])
                        do(V.tensor_copy(cols[:].rearrange("p n k d h -> p (n k d h)"), PS[:, 7, 0:160]))
                        V.tensor_copy(decB[:].rearrange("p h d n -> p (h d n)"), PS[:, 7, 256:296]).then_inc(cols_ready, 1)
                        ve.wait_ge(cols_ready, 1)
                    else:
                        ve.wait_ge(diff_ready, 1)
                        link(V.tensor_scalar(lg[:].rearrange("p d h -> p (d h)"), lg[:].rearrange("p d h -> p (d h)"), -1.0, None, ALU.mult))
                        for kind in range(2):
                            for d in range(2):
                                do(V.tensor_scalar(xz[:, kind, d, :], lg[:, d, :], icol[:, 2 * kind + d:2 * kind + d + 1], None, ALU.mult))
                        V.tensor_scalar(xz[:, 2], lg[:], float(P), None, ALU.mult).then_inc(decay_ready, 1)
                        ve.wait_ge(ret_ready, 16)
                        ve.wait_ge(stored, 32)
                        ve.wait_ge(dm_ready, 1)
                    for t in range(NT):
                        ve.wait_ge(products, at["kt", fam, t])
                        if fam == 1 and t == 0:
                            ve.wait_ge(kw_ready, NU - 2 * NH)
                        V.tensor_copy(ktok[:, t].rearrange("p h d -> p (h d)"), PS[:, 2 * (proj_count["kt", fam, t][0] % 4), :]).then_inc(proj_v, 1)
                    for i in range(NU + 3):
                        if i < NU:
                            s, h, d = UNITS[i]
                            t = tile_of(s, d)
                            ve.wait_ge(products, at["S", fam, i])
                            if fam == 0:
                                if i >= 2:
                                    ve.wait_ge(p_ready, i - 1)
                                V.scalar_tensor_tensor(eb[:, i % 2, :], PS[:, i % 2, P:2 * P], cols[:, t, 2, d, h:h + 1], mask[:, d, :],
                                                       ALU.add, ALU.add).then_inc(e_ready, 1)
                        u = i - 1
                        if 0 <= u < NU:
                            s, h, d = UNITS[u]
                            if u >= 2:
                                ve.wait_ge(products, at["H", fam, u - 2])
                            if fam == 0:
                                ve.wait_ge(exp_ready, u + 1)
                                w = eb[:, u % 2, :]
                            else:
                                w = Dm[:, d, h, :]
                            V.tensor_tensor(pb[:, u % 2, :], w, PS[:, u % 2, 0:P], ALU.mult).then_inc(p_ready, 1)
                        u = i - 3
                        if u < 0:
                            continue
                        s, h, d = UNITS[u]
                        t = tile_of(s, d)
                        ve.wait_ge(products, at["H", fam, u])
                        width = DH + 1 if fam == 0 else DH
                        U = PS[:, 4 + u % 2, 0:width]
                        num, inter = PS[:, 2 + u % 2, 0:width], PS[:, 2 + u % 2, 256:256 + width]
                        ndu = nd[:, u % 2, :]
                        out = f[:, t, fam * W_A + h * DH:fam * W_A + (h + 1) * DH]
                        if s > 0:
                            w = cols[:, t, 1, d, h:h + 1] if fam == 0 else xz[:, 0, d, h:h + 1]
                            do(V.tensor_scalar(ndu[:, 0:width], inter, w, None, ALU.mult))
                        if s == 0:
                            V.tensor_copy(Cout[:, d, h, 0:width], U).then_inc(state_ready, 1)
                        elif s < NT - 1:
                            w = decB[:, h, d, t:t + 1] if fam == 0 else xz[:, 2, d, h:h + 1]
                            V.scalar_tensor_tensor(Cst[:, d, h, 0:width], Cst[:, d, h, 0:width], w, U, ALU.mult, ALU.add).then_inc(state_ready, 1)
                        settle()
                        if s > 0:
                            link(V.tensor_tensor(ndu[:, 0:width], ndu[:, 0:width], num, ALU.add))
                        else:
                            link(V.tensor_copy(ndu[:, 0:width], num))
                        if fam == 0:
                            link(V.scalar_tensor_tensor(ndu[:, DH + 1:DH + 2], ndu[:, DH:DH + 1], -1.0, ndu[:, DH:DH + 1], ALU.mult, ALU.max))
                            link(V.tensor_scalar(ndu[:, DH + 1:DH + 2], ndu[:, DH + 1:DH + 2], cols[:, t, 3, d, h:h + 1], None, ALU.max))
                            link(V.reciprocal(ndu[:, DH + 1:DH + 2], ndu[:, DH + 1:DH + 2]))
                            if first_on(s, d):
                                V.tensor_scalar(out, ndu[:, 0:DH], ndu[:, DH + 1:DH + 2], None, ALU.mult).then_inc(h_done, 1)
                            else:
                                V.scalar_tensor_tensor(out, ndu[:, 0:DH], ndu[:, DH + 1:DH + 2], out, ALU.mult, ALU.add).then_inc(h_done, 1)
                        elif first_on(s, d):
                            V.tensor_copy(out, ndu[:, 0:DH]).then_inc(h_done, 1)
                        else:
                            V.tensor_tensor(out, ndu[:, 0:DH], out, ALU.add).then_inc(h_done, 1)
                        ve.wait_ge(h_done, fam * NU + u + 1)
                    hv = lambda t, h: f[:, t, fam * W_A + h * DH:fam * W_A + (h + 1) * DH]
                    for t in range(NT):
                        for h in range(NH):
                            do(V.bn_stats(stat[:, t * NH + h, :], hv(t, h)))
                    settle()
                    for i in range(NT * NH):
                        last = V.bn_aggr(mv[:, i, :], stat[:, i:i + 1, :])
                        if i < NT * NH - 1:
                            do(last)
                    last.then_inc(var_ready, 1)
                    ve.wait_ge(dev_ready, fam + 1)
                    link(V.reciprocal(rstd[:], rstd[:]))
                    for t in range(NT):
                        for h in range(NH):
                            i = t * NH + h
                            do(V.tensor_scalar(hv(t, h), hv(t, h), mv[:, i, 0:1], rstd[:, i:i + 1], ALU.subtract, ALU.mult))
                    settle()
                    ve.wait_ge(og_ready, fam + 1)
                    V.tensor_tensor(f[:, :, fam * W_A:(fam + 1) * W_A], f[:, :, fam * W_A:(fam + 1) * W_A], og, ALU.mult).then_inc(norm_done, 1)
                    ve.wait_ge(norm_done, fam + 1)
                for k in range(KD):
                    ve.wait_ge(products, at["h", 4, k])
                    V.tensor_copy(hT[:, k, P:T], PS[:, 2 * (k % 4) + 1, :]).then_inc(h_evac_v, 1)
                ve.wait_ge(out_evac, D // SLICE * NT)
                layer_norm(0, rowsB)

            def peer(l):
                kind = 2
                for k in range(KD + 1):
                    if k < KD:
                        ve.wait_ge(products, at["h", 2 * l + 1, k])
                        settle()
                        if k >= 2:
                            ve.wait_ge(hh_ready, KD * l + k - 1)
                            ve.wait_ge(hl_ready, KD * l + k - 1)
                        V.tensor_scalar(htmp[:, k % 2, P:T], PS[:, 2 * (k % 4) + 1, :], modT[:, l, kind + 1, k, 1:2], modT[:, l, kind, k, 1:2],
                                        ALU.mult, ALU.add).then_inc(h_evac_v, 1)
                    if k >= 1:
                        ve.wait_ge(hh_ready, KD * l + k)
                        V.tensor_tensor(hL[:, k - 1, :], htmp[:, (k - 1) % 2, :], hH[:, k - 1, :].bitcast(f32), ALU.subtract).then_inc(hl_ready, 1)
                ve.wait_ge(hl_ready, KD * (l + 1))
                ve.wait_ge(iota_ready, l + 1)
                for m in range(2 * H_P):
                    for t in range(NT):
                        if t == 0:
                            ve.wait_ge(products, at["ps", l, m])
                        sc_ = PS[:, 4 + 2 * (m % 2) + (t == NT - 1), (t % 4) * P:(t % 4 + 1) * P]
                        v_, i_ = sv[:, t, m // 2, m % 2, :], si[:, t, m // 2, m % 2, :]
                        link(V.max(v_[:, 0:8], sc_))
                        do(V.max_index(i_[:, 0:8], v_[:, 0:8], sc_))
                        V.match_replace(swork[:], v_[:, 0:8], sc_, NEG).then_inc(s_used, 1)
                        ve.wait_ge(s_used, NT * (l * 2 * H_P + m) + t + 1)
                        link(V.max(v_[:, 8:16], swork[:]))
                        link(V.max_index(i_[:, 8:16], v_[:, 8:16], swork[:]))
                for t in range(NT):
                    hk = hkt[:, t]
                    bt = best[:, t]
                    for h in range(H_P):
                        cd = cand[:, 0, :].rearrange("p (a b) -> p a b", b=TOPK)
                        link(V.tensor_tensor(cd, bc(sv[:, t, h, 0, :], TOPK), sv[:, t, h, 1, :].unsqueeze(1).broadcast_to([P, TOPK, TOPK]), ALU.add))
                        link(V.max(bt[:, h, 0:8], cand[:, 0, :]))
                        do(V.max_index(pos[:, h, 0:8], bt[:, h, 0:8], cand[:, 0, :]))
                        link(V.match_replace(cand[:, 1, :], bt[:, h, 0:8], cand[:, 0, :], NEG))
                        link(V.max(bt[:, h, 8:16], cand[:, 1, :]))
                        link(V.max_index(pos[:, h, 8:16], bt[:, h, 8:16], cand[:, 1, :]))
                    link(V.tensor_copy(ssum[:, t, :], bt[:, :, 0]))
                    link(V.tensor_tensor(bt, bt, bc(ssum[:, t, :], TOPK), ALU.subtract))
                    pf = pos[:].rearrange("p h k -> p (h k)")
                    do(V.tensor_scalar(posi[:, 0, :], pf, 4, None, ALU.logical_shift_right))
                    do(V.tensor_scalar(posi[:, 1, :], pf, 15, None, ALU.bitwise_and))
                    do(V.tensor_copy(sif[:].rearrange("p h c k -> p (h c k)"), si[:, t].rearrange("p h c k -> p (h c k)")))
                    settle()
                    link(V.tensor_copy(posf[:], posi[:]))
                    for c in range(2):
                        link(V.tensor_tensor(eqb, bc(posf[:, c, :], TOPK), iota[:, 0:TOPK].unsqueeze(1).broadcast_to([P, HK, TOPK]), ALU.is_equal))
                        link(V.tensor_tensor(eqc.rearrange("p (h k) b -> p h k b", h=H_P), eqb.rearrange("p (h k) b -> p h k b", h=H_P),
                                             sif[:, :, c, :].unsqueeze(2).broadcast_to([P, H_P, TOPK, TOPK]), ALU.mult))
                        link(V.tensor_reduce(hk[:, c, :], eqc, AX, ALU.add))
                V.tensor_copy(ssum[:, 0, 0:1], best[:, 0, 0, 0:1]).then_inc(sm_sub, 1)
                ve.wait_ge(sm_exp, l + 1)
                link(V.tensor_reduce(ssum[:], best[:], AX, ALU.add))
                link(V.reciprocal(ssum[:], ssum[:]))
                for t in range(NT):
                    last = V.tensor_tensor(hkt[:, t, 2, :].rearrange("p (h k) -> p h k", h=H_P), best[:, t], bc(ssum[:, t, :], TOPK), ALU.mult)
                    if t < NT - 1:
                        do(last)
                last.then_inc(hk_ready, 1)
                for t in range(NT):
                    ve.wait_ge(products, at["hk", l, t])
                    V.tensor_copy(hkT[:, :, t * P:(t + 1) * P], PS[:, 4 + t % 2, 0:3 * P].rearrange("p (c t) -> p c t", c=3)).then_inc(hk_evac, 1)
                ve.wait_ge(hk_evac, l * NT + NT)

                link(V.tensor_copy(gH[:], hkT[:, 2, :]))
                link(V.tensor_tensor(gL[:], hkT[:, 2, :], gH[:].bitcast(f32), ALU.subtract))

                def hots(it):
                    for half in range(2):
                        q = 2 * it + half
                        if not (isinstance(it, int)):
                            ve.wait_ge(products, at["ub", l] + 4 * (it - 1) + 2 * half + 2)
                        for tk in range(8):
                            c = bass.ds(16 * it + 8 * half + tk, 1)
                            do(V.tensor_scalar(hot[:, half, 0, tk, :], iota[:], hkT[:, 0, c], None, ALU.is_equal))
                            do(V.tensor_scalar(hot[:, half, 1, tk, :], iota[:], hkT[:, 1, c], gH[:, c].bitcast(f32), ALU.is_equal, ALU.mult))
                            last = V.tensor_scalar(hot[:, half, 2, tk, :], iota[:], hkT[:, 1, c], gL[:, c], ALU.is_equal, ALU.mult)
                            if tk < 7:
                                do(last)
                        last.then_inc(hot_ready, 1)

                hots(0)
                n0 = ch.n
                with ve.Fori(1, 40) as it:
                    hots(it)
                ch.n = n0 + 39 * 46
                settle()
                ve.wait_ge(hot_ready, 80 * (l + 1))
                ve.wait_ge(products, at["v", l])
                for half in range(2):
                    ve.wait_ge(g_stored[half], 16 * 20 * (l + 1))
                for t in range(NT):
                    do(V.memset(f[:, t, :], 0.0))
                settle()

                def weigh(blk, q):
                    js = slice((q % 2) * JV, (q % 2 + 1) * JV)
                    if q % 2 == 0:
                        ve.wait_ge(ag_full, 32 * (l * NBLK + 1) + 16 * (blk if isinstance(blk, int) else blk))
                    a_ = ab[:, js, :]
                    for j in range(JV):
                        aj = a_[:, j, :].rearrange("p (n t) -> p n t", t=16)
                        last = V.tensor_tensor(aj, aj, gb[:, :, (q % 2) * JV + j, :], ALU.mult)
                        if j < JV - 1:
                            do(last)
                    last.then_inc(wf_ready, 1)
                    ve.wait_ge(wh_ready, l * 32 + blk + 1)
                    V.tensor_tensor(WL[:, q % 2], a_, WH[:, q % 2].bitcast(f32), ALU.subtract).then_inc(w_ready, 1)

                def gather(blk, q):
                    for t in range(NT):
                        pr = (q * NT + t) % 4
                        gg = (l * 32 + blk) * NT + t
                        ve.wait_ge(products, at["v", l] + blk * NT + t + 1)
                        ft = f[:, t, :].rearrange("p (c d) -> p c d", c=2)
                        if not (isinstance(blk, int) and gg < NT):
                            ve.wait_ge(acc_done, gg - NT + 1)
                        V.tensor_tensor(ft, ft, PS[:, 2 * pr:2 * pr + 2, :], ALU.add).then_inc(acc_done, 1)

                def blocks(i, last_pass):
                    for q in range(4):
                        blk = 4 * i + q
                        if not (last_pass and q == 3):
                            weigh(blk + 1, (q + 1) % 4)
                        gather(blk, q)

                weigh(0, 0)
                blocks(0, False)
                n0 = ch.n
                with ve.Fori(1, 7) as i:
                    blocks(i, False)
                ch.n = n0 + 6 * 4 * (JV - 1)
                blocks(7, True)
                settle()
                ve.wait_ge(acc_done, (l + 1) * 32 * NT)
                layer_norm(2 * l + 1, rowsP)

            def odd():
                modulated(2)
                ve.wait_ge(alog_exp, 1)
                ve.wait_ge(od_consts, 1)
                fl = lambda z: z[:].rearrange("p t d h -> p (t d h)")
                ve.wait_ge(products, at["dt",])
                link(V.tensor_tensor(dtc[:].rearrange("p t d h -> p t (d h)"), PS[:, 0, 0:NT * 64].rearrange("p (t n) -> p t n", t=NT),
                                     brow[:, 0, :].unsqueeze(1).broadcast_to([P, NT, 64]), ALU.add))
                V.scalar_tensor_tensor(fl(av), fl(dtc), -1.0, fl(dtc), ALU.mult, ALU.max).then_inc(dt_abs, 1)
                ve.wait_ge(dt_sp, 1)
                link(V.scalar_tensor_tensor(fl(dtc), fl(dtc), 0.0, fl(av), ALU.max, ALU.add))
                V.scalar_tensor_tensor(av[:].rearrange("p t d h -> p t (d h)"), dtc[:].rearrange("p t d h -> p t (d h)"), -1.0,
                                       brow[:, 1, :].unsqueeze(1).broadcast_to([P, NT, 64]), ALU.mult, ALU.mult).then_inc(a_ready, 1)
                ve.wait_ge(products, at["acum",])
                ac = PS[:, 1, 0:NT * 64]
                do(V.tensor_scalar(fl(nac), ac, -1.0, None, ALU.mult))
                do(V.tensor_copy(fl(win), ac))
                do(V.tensor_copy(fl(dcy), PS[:, 2, 0:NT * 64]))
                settle()
                link(V.tensor_tensor(fl(wup), fl(dcy), fl(nac), ALU.add))
                V.tensor_copy(otmp[:, 0:1], nac[:, 0, 0, 0:1]).then_inc(ac_ready, 1)
                ve.wait_ge(seg_exp, 1)
                link(V.tensor_tensor(fl(wup), fl(wup), fl(dtc), ALU.mult))
                for g in range(G_C):
                    hs = slice(g * J_C, (g + 1) * J_C)
                    for m in range(7):
                        if m < 6:
                            q = g * 6 + m
                            ve.wait_ge(pad_filled, q + 1)
                            if q >= 2:
                                ve.wait_ge(act_done, q - 1)
                            acc = cacc[:, q % 2, :]
                            w0 = g * 6 + m
                            link(V.tensor_scalar(acc, cpad[:, q % 2, 0:T + 2], cw[:, w0, 0:1], None, ALU.mult))
                            for j in range(1, D_CONV):
                                ins = V.scalar_tensor_tensor(acc, cpad[:, q % 2, j:j + T + 2], cw[:, w0, j:j + 1], acc, ALU.mult, ALU.add)
                                if j < D_CONV - 1:
                                    link(ins)
                            ins.then_inc(conv_done, 1)
                        mm = m - 1
                        if 0 <= mm < 5:
                            n = g * 5 + mm
                            ve.wait_ge(products, at["xt", g, mm])
                            dst = xs[:, :, mm * P:(mm + 1) * P] if mm < 4 else Btok[:, :, :]
                            b = 4 + 2 * (n % 2)
                            do(V.tensor_copy(dst[:, 0:4, :], PS[:, b, :].rearrange("p (t c) -> p t c", t=4)))
                            V.tensor_copy(dst[:, 4, :], PS[:, b + 1, 0:P]).then_inc(tr_evac, 1)
                    ve.wait_ge(tr_evac, g * 5 + 5)
                    for t in range(NT):
                        n = g * NT + t
                        for d in range(2):
                            ve.wait_ge(products, at["seg", g, t, d])
                            if n >= 1:
                                ve.wait_ge(products, at["intra", (g * NT + t - 1) // NT, (t - 1) % NT])
                            for j in range(J_C):
                                last = V.scalar_tensor_tensor(EP[:, d, j, :], PS[:, 5 + j // 4, (j % 4) * P:(j % 4 + 1) * P],
                                                              nac[:, t, d, g * J_C + j:g * J_C + j + 1], maskO[:, d, :], ALU.add, ALU.add)
                                if j < J_C - 1:
                                    do(last)
                            last.then_inc(oe_ready, 1)
                        for d in range(2):
                            ve.wait_ge(oexp_ready, 2 * n + d + 1)
                            for j in range(J_C):
                                last = V.scalar_tensor_tensor(EP[:, d, j, :], EP[:, d, j, :], dtc[:, t, d, g * J_C + j:g * J_C + j + 1],
                                                              PS[:, 4, 0:P], ALU.mult, ALU.mult)
                                if j < J_C - 1:
                                    do(last)
                            last.then_inc(op_ready, 1)
                        yt = y[:, t, g * GC:(g + 1) * GC]
                        link(V.tensor_tensor(yt.rearrange("p (j c) -> p j c", j=J_C), xs[:, t, :].rearrange("p (j c) -> p j c", j=J_C),
                                             bc(brow[:, 2, hs], P_C), ALU.mult))
                        ve.wait_ge(products, at["intra", g, t])
                        V.tensor_tensor(yt, yt, PS[:, 7, :], ALU.add).then_inc(y_intra, 1)
                    ve.wait_ge(y_intra, g * NT + NT)
                    for s in range(NT):
                        for d in range(2):
                            t = tile_of(s, d)
                            n, nu = (g * 4 + s - 1) * 2 + d, (g * 4 + s) * 2 + d
                            yt = y[:, t, g * GC:(g + 1) * GC]
                            if s > 0:
                                ve.wait_ge(products, at["inter", g, s, d])
                                link(V.tensor_tensor(otmp[:].rearrange("p (j c) -> p j c", j=J_C), PS[:, n % 2, :].rearrange("p (j c) -> p j c", j=J_C),
                                                     bc(win[:, t, d, hs], P_C), ALU.mult))
                                V.tensor_tensor(yt, yt, otmp[:], ALU.add).then_inc(inter_done, 1)
                                ve.wait_ge(inter_done, n + 1)
                            if s < NT - 1:
                                ve.wait_ge(products, at["upd", g, s, d])
                                if s == 0:
                                    if g >= 1:
                                        ve.wait_ge(hst_stored, 16 * g)
                                    V.tensor_copy(hout[:, d, :], PS[:, 2 + nu % 2, :]).then_inc(upd_done, 1)
                                else:
                                    hv = hst[:, d, :].rearrange("p (j c) -> p j c", j=J_C)
                                    link(V.tensor_tensor(hv, hv, bc(dcy[:, t, d, hs], P_C), ALU.mult))
                                    V.tensor_tensor(hst[:, d, :], hst[:, d, :], PS[:, 2 + nu % 2, :], ALU.add).then_inc(upd_done, 1)
                                ve.wait_ge(upd_done, nu + 1)
                for s in range(D_INNER // SLICE):
                    for t in range(NT):
                        n = s * NT + t
                        ve.wait_ge(z_silu, n + 1)
                        yt = y[:, t, s * SLICE:(s + 1) * SLICE]
                        V.tensor_tensor(yt, yt, zt[:, n % 2, :], ALU.mult).then_inc(z_used, 1)
                ve.wait_ge(nw_loaded, 16)
                for k in range(2 * KD):
                    ve.wait_ge(products, at["yt", k])
                    V.tensor_scalar(yT[:, k, P:T], PS[:, 2 * (k % 4) + 1, :], nw[:, k:k + 1], None, ALU.mult).then_inc(yt_v, 1)
                ve.wait_ge(ssq_done, 1)
                V.reciprocal(ssq[:], ssq[:]).then_inc(rr_ready, 1)
                ve.wait_ge(oo_evac, KD * NT)
                layer_norm(2, rowsO)

            if "even" in run:
                even()
            if "peer0" in run:
                peer(0)
            if "odd" in run:
                odd()
            if "peer1" in run:
                peer(1)

        @block.scalar
        def _(act):
            S = nc.scalar
            ch = Chain(act, act_chain)
            do, link, settle = ch.do, ch.link, ch.settle

            act.dma_start(cT[:], a["c"]).then_inc(small_loaded, 16)
            act.dma_start(bmod, a["b_mod"][:, 0]).then_inc(small_loaded, 16)
            act.dma_start(x[:, 0, :], a["x_prompt"]).then_inc(x_loaded, 16)
            act.dma_start(x[:, 1:NT, :], a["x_sample"]).then_inc(x_loaded, 16)
            act.dma_start(f[:, 0:NT - 1, :], a["pos"]).then_inc(x_loaded, 16)
            act.wait_ge(small_loaded, 32)
            S.activation(cT[:], cT[:], ACT.Silu).then_inc(c_ready, 1)
            for l in range(DEPTH):
                act.wait_ge(mod_rows, l + 1)
                if l + 1 < DEPTH:
                    act.dma_start(bmod, a["b_mod"][:, l + 1]).then_inc(small_loaded, 16)
                act.dma_start(gdram[l, 0], mrow[:, 2 * D:3 * D]).then_inc(gates_stored, 16)
                act.dma_start(gdram[l, 1], mrow[:, 5 * D:6 * D]).then_inc(gates_stored, 16)
            act.wait_ge(mod_cols, DEPTH)
            act.wait_ge(gates_stored, 32 * DEPTH)

            def modulated(n):
                l, kind = n // 2, 2 * (n % 2)
                for k in range(KD):
                    act.wait_ge(products, at["h", n, k])
                    S.activation(hT[:, k, 0:P], PS[:, 2 * (k % 4), 0:P], ACT.Identity, bias=modT[:, l, kind, k, 0:1],
                                 scale=modT[:, l, kind + 1, k, 0:1]).then_inc(h_evac_a, 1)

            def layer_norm(n, rows):
                l, second = n // 2, n % 2
                act.dma_start(rows[:, 0, :], a["ln_g"][n].partition_broadcast(P)).then_inc(rows_loaded, 16)
                act.dma_start(rows[:, 1, :], a["ln_b"][n].partition_broadcast(P)).then_inc(rows_loaded, 16)
                act.dma_start(rows[:, 2:4, :].rearrange("p a d -> p (a d)"),
                              gdram[l, second].rearrange("a d -> (a d)").partition_broadcast(P)).then_inc(rows_loaded, 16)

            def deviation(n_var, n):
                act.wait_ge(var_ready, n_var)
                S.activation(rstd[:, 0:n], mv[:, 0:n, 1], ACT.Sqrt, bias=eps[:, 0:1]).then_inc(dev_ready, 1)

            def even():
                modulated(0)
                for dst, name in ((m0[:], "m0"), (gbias[:], "gate_bias"), (gn[:].rearrange("p a d -> p (a d)"), "gn"),
                                  (lg[:].rearrange("p d h -> p (d h)"), "log_decay"), (Cst[:], "Cn0")):
                    src = a[name].partition_broadcast(P) if name in ("gn", "log_decay") else a[name]
                    act.dma_start(dst, src).then_inc(even_loaded, 16)
                L, F, t1, t2 = (grow[:, i] for i in range(4))
                for fam in range(2):
                    def pair_out(kind, i, dst, scale):
                        act.wait_ge(products, at[kind, fam, i])
                        pr = proj_count[kind, fam, i][0] % 4
                        S.activation(dst.rearrange("p (a t) -> p a t", a=2), PS[:, 2 * pr:2 * pr + 2, 0:HT], ACT.Copy,
                                     scale=scale).then_inc(proj_a, 1)
                    for i in range(NH):
                        pair_out("q", i, qT[:, i, :], 1.0 if fam == 0 else DH ** -0.5)
                    if fam == 0:
                        act.wait_ge(gate_exp, 1)
                        link(S.activation(t1, t1, ACT.Exp, scale=-1.0))
                        S.activation(t1, t1, ACT.Ln, bias=1.0).then_inc(gate_act, 1)
                    for i in range(NH):
                        pair_out("k", i, kT[:, i, :], DH ** -0.5 if fam == 0 else 1.0)
                    if fam == 0:
                        act.wait_ge(gate_exp, 2)
                        do(S.activation(L, L, ACT.Exp))
                        do(S.activation(F, F, ACT.Exp))
                        do(S.activation(t2, b_m[:, 1], ACT.Exp, scale=-1.0))
                        S.activation(DEC_, DEC_, ACT.Exp).then_inc(gates_done, 1)
                        act.dma_start(o["new_m"], ML[:, :, 0], allow_slow_non_contiguous=True).then_inc(stored, 16)
                    else:
                        act.wait_ge(even_loaded, 80)
                        S.activation(lg[:], lg[:], ACT.Exp).then_inc(diff_ready, 1)
                        act.wait_ge(norm_done, 1)
                    for s in range(2):
                        for t in range(NT):
                            act.wait_ge(products, at["o", fam, (s, t)])
                            pr = proj_count["o", fam, (s, t)][0] % 4
                            S.activation(og[:, t, s * SLICE:(s + 1) * SLICE], PS[:, 2 * pr, 0:SLICE],
                                         ACT.Sigmoid if fam == 0 else ACT.Silu).then_inc(proj_a, 1)
                    if fam == 0:
                        for u in range(NU):
                            act.wait_ge(e_ready, u + 1)
                            S.activation(eb[:, u % 2, :], eb[:, u % 2, :], ACT.Exp).then_inc(exp_ready, 1)
                            if u == 2 * NH + 4:
                                act.wait_ge(state_ready, 2 * NH)
                                act.dma_start(o["new_Cn"], Cout[:]).then_inc(stored, 16)
                        act.wait_ge(h_done, NU)
                        act.dma_start(Cst[:, :, :, 0:DH], a["S0"]).then_inc(ret_ready, 16)
                    else:
                        act.wait_ge(decay_ready, 1)
                        do(S.activation(xz[:], xz[:], ACT.Exp))
                        for d in range(2):
                            for h in range(NH):
                                last = S.activation(Dm[:, d, h, :], diff[:, d, :], ACT.Exp, scale=lg[:, d, h:h + 1])
                                if (d, h) != (1, NH - 1):
                                    do(last)
                        last.then_inc(decay_exp, 1)
                        act.wait_ge(state_ready, NU - 2 * NH + 2 * NH)
                        act.dma_start(o["new_ret"], Cout[:, :, :, 0:DH]).then_inc(stored, 16)
                    deviation(fam + 1, NT * NH)
                act.wait_ge(products, at["H", 1, NU - 1])
                layer_norm(0, rowsB)
                for k in range(KD):
                    act.wait_ge(products, at["h", 4, k])
                    S.activation(hT[:, k, 0:P], PS[:, 2 * (k % 4), 0:P], ACT.Copy).then_inc(h_evac_a, 1)
                for s in range(D // SLICE):
                    for t in range(NT):
                        act.wait_ge(products, at["eo", s, t])
                        S.activation(f[:, t, s * SLICE:(s + 1) * SLICE], PS[:, (s * NT + t) % 8, 0:SLICE], ACT.Copy).then_inc(out_evac, 1)
                deviation(3, NT)

            def peer(l):
                act.wait_ge(x_ready, 2 * l + 2)
                act.dma_start(keys, a["keys"][l]).then_inc(keys_loaded, 16)

                def high(n, slot, freed):
                    act.wait_ge(raw_full[slot % NRAW], 16 * (l * 18 + 1) + 4 * (n - slot % NRAW))
                    if freed is not None:
                        act.wait_ge(products, freed)
                    S.activation(wH[:, slot % NSPLIT, :], raw[:, slot % NRAW, :], ACT.Copy).then_inc(hi_ready, 1)

                kind = 2
                for k in range(KD):
                    act.wait_ge(products, at["h", 2 * l + 1, k])
                    if k >= 2:
                        act.wait_ge(hl_ready, KD * l + k - 1)
                    S.activation(htmp[:, k % 2, 0:P], PS[:, 2 * (k % 4), 0:P], ACT.Identity, bias=modT[:, l, kind, k, 0:1],
                                 scale=modT[:, l, kind + 1, k, 0:1]).then_inc(h_evac_a, 1)
                    act.wait_ge(h_evac_v, at_h[2 * l + 1] + k + 1)
                    act.wait_ge(h_evac_a, at_h[2 * l + 1] + k + 1)
                    S.activation(hH[:, k, :], htmp[:, k % 2, :], ACT.Copy).then_inc(hh_ready, 1)
                    if k < NSPLIT:
                        high(k, k, None)
                for m in range(2 * H_P):
                    if m % 2 == 0 and m >= 2:
                        high(m // 2 + 1, m // 2 + 1, at["pq", l, m - 1])
                    act.wait_ge(products, at["pq", l, m])
                    if m >= 2:
                        act.wait_ge(products, at["ps", l, m - 2])
                    S.activation(qb[:, m % 2, :].rearrange("p (a t) -> p a t", a=2), PS[:, 2 * (m % 2):2 * (m % 2) + 2, 0:HT],
                                 ACT.Copy).then_inc(q_evac, 1)

                def product_of(i, jj, build):
                    return at["ub", l] + (i - 3) * 32 + 2 * jj + 1 if build else at["u", l] + i * 16 + jj + 1

                def gelus(i, build, final=False):
                    static = isinstance(i, int)
                    for jj in range(16):
                        gj = l * N_KEYS + i * 16 + jj
                        pr, half = jj // 2, jj % 2
                        n = product_of(i, jj, build)
                        if half == 0 and not (final and pr == 7):
                            if pr:
                                freed = product_of(i, jj - 1, build)
                            elif static and i == 0:
                                freed = at["pq", l, 2 * H_P - 1]
                            else:
                                freed = product_of(i - 1, 15, build and not (static and i == 3))
                            high(8 + 8 * i + pr + 1, pr + 1, freed)
                        act.wait_ge(products, n)
                        if half == 0 and not (static and i == 0 and l == 0 and pr < 2):
                            act.wait_ge(a_stored[pr % 2], 16 * (l * 32 + i * 4 + pr // 2))
                        S.activation(abuf[:, pr % 2, half, :].rearrange("p (a t) -> p a t", a=2), PS[:, 2 * half:2 * half + 2, 0:HT],
                                     ACT.Gelu).then_inc(act_gelu, 1)
                        if half == 1:
                            act.wait_ge(act_gelu, gj + 1)
                            act.dma_start(Ad[2 * i + pr // 4, :, 2 * (pr % 4):2 * (pr % 4) + 2, :], abuf[:, pr % 2]).then_inc(a_stored[pr % 2], 16)
                        if build:
                            act.wait_ge(products, n + 1)
                            if half == 0 and not (static and i == 3 and l == 0 and pr < 2):
                                act.wait_ge(g_stored[pr % 2], 16 * (l * 20 + (i - 3) * 4 + pr // 2))
                            S.activation(gst[:, pr % 2, :, half * 8:half * 8 + 8].rearrange("p j t -> p t j"),
                                         PS[:, 4 + 2 * half:6 + 2 * half, :].rearrange("p b (t j) -> p (b t) j", j=P), ACT.Copy).then_inc(g_evac, 1)
                            if half == 1:
                                act.wait_ge(g_evac, l * 80 + (i - 3) * 16 + jj + 1)
                                act.dma_start(Gd[:, :, (i - 3) * 8 + pr].rearrange("b p j t -> p b (j t)"),
                                              gst[:, pr % 2].rearrange("p (b j) t -> p b (j t)", j=JB)).then_inc(g_stored[pr % 2], 16)

                gelus(0, False)
                with act.Fori(1, 3) as i:
                    gelus(i, False)
                act.wait_ge(sm_sub, l + 1)
                S.activation(best[:], best[:], ACT.Exp).then_inc(sm_exp, 1)
                gelus(3, True)
                with act.Fori(4, 7) as i:
                    gelus(i, True)
                gelus(7, True, final=True)
                for half in range(2):
                    act.wait_ge(a_stored[half], 16 * 32 * (l + 1))
                    act.wait_ge(g_stored[half], 16 * 20 * (l + 1))
                act.wait_ge(products, at["v", l])
                act.wait_ge(hot_ready, 80 * (l + 1))

                def highs(blk, q):
                    for c in range(2):
                        act.wait_ge(vraw_full[c], 16 * (l * 32 + 1) + 16 * blk)
                        if not (isinstance(blk, int) and blk < 2):
                            act.wait_ge(products, at["v", l] + (blk - 1) * NT)
                        S.activation(wHv[:, 2 * (q % 2) + c, :], rawV[:, c, :], ACT.Copy).then_inc(hi_ready, 1)
                    act.wait_ge(wf_ready, l * 32 + blk + 1)
                    S.activation(WH[:, q % 2], ab[:, (q % 2) * JV:(q % 2 + 1) * JV, :], ACT.Copy).then_inc(wh_ready, 1)

                for q in range(4):
                    highs(q, q)
                with act.Fori(1, 8) as i:
                    for q in range(4):
                        highs(4 * i + q, q)
                act.wait_ge(w_ready, 32 * (l + 1))
                layer_norm(2 * l + 1, rowsP)
                deviation(4 + 2 * l, NT)

            def odd():
                act.wait_ge(x_ready, 3)
                act.dma_start(brow[:].rearrange("p a n -> p (a n)"), a["odd_rows"].partition_broadcast(P)).then_inc(odd_loaded, 16)
                act.dma_start(cw[:], a["conv"]).then_inc(odd_loaded, 16)
                act.wait_ge(odd_loaded, 32)
                S.activation(brow[:, 1, :], brow[:, 1, :], ACT.Exp).then_inc(alog_exp, 1)
                modulated(2)
                fl = lambda z: z[:].rearrange("p t d h -> p (t d h)")
                act.wait_ge(dt_abs, 1)
                link(S.activation(fl(av), fl(av), ACT.Exp, scale=-1.0))
                S.activation(fl(av), fl(av), ACT.Ln, bias=1.0).then_inc(dt_sp, 1)
                act.wait_ge(ac_ready, 1)
                do(S.activation(fl(win), fl(win), ACT.Exp))
                do(S.activation(fl(dcy), fl(dcy), ACT.Exp))
                S.activation(fl(wup), fl(wup), ACT.Exp).then_inc(seg_exp, 1)
                for g in range(G_C):
                    if g:
                        act.wait_ge(products, at["inter", g - 1, NT - 1, 1])
                        act.wait_ge(upd_done, 8 * g)
                    act.dma_start(hst[:], a["h0"][g]).then_inc(hst_loaded, 16)
                    for m in range(7):
                        if m < 6:
                            q = g * 6 + m
                            act.wait_ge(products, at["xbc", g, m])
                            if q >= 2:
                                act.wait_ge(conv_done, q - 1)
                            do(S.activation(cpad[:, q % 2, 2:2 + P], PS[:, 2 * (m % 2), 0:P], ACT.Copy))
                            S.activation(cpad[:, q % 2, 4 + P:4 + T], PS[:, 2 * (m % 2) + 1, :], ACT.Copy).then_inc(pad_filled, 1)
                        mm = m - 1
                        if mm >= 0:
                            q = g * 6 + mm
                            act.wait_ge(conv_done, q + 1)
                            if mm < 4:
                                if mm >= 2:
                                    act.wait_ge(products, at["xt", g, mm - 2])
                                dst = sx[:, mm % 2, :]
                            else:
                                dst = BC[:, mm - 4, :]
                            do(S.activation(dst[:, 0:P], cacc[:, q % 2, 0:P], ACT.Silu, bias=cw[:, q, D_CONV:D_CONV + 1]))
                            S.activation(dst[:, P:T], cacc[:, q % 2, P + 2:T + 2], ACT.Silu, bias=cw[:, q, D_CONV:D_CONV + 1]).then_inc(act_done, 1)
                    for t in range(NT):
                        for d in range(2):
                            n = (g * NT + t) * 2 + d
                            act.wait_ge(oe_ready, n + 1)
                            S.activation(EP[:, d], EP[:, d], ACT.Exp).then_inc(oexp_ready, 1)
                    act.wait_ge(upd_done, 8 * g + 2)
                    act.dma_start(o["new_ssd"][g], hout[:]).then_inc(hst_stored, 16)
                act.wait_ge(products, at["inter", G_C - 1, NT - 1, 1])
                act.wait_ge(inter_done, 8 * G_C)
                act.wait_ge(hst_stored, 16 * G_C)
                act.dma_start(nw[:], a["norm_w"]).then_inc(nw_loaded, 16)
                layer_norm(2, rowsO)
                for s in range(D_INNER // SLICE):
                    for t in range(NT):
                        n = s * NT + t
                        act.wait_ge(products, at["z", s, t])
                        if n >= 2:
                            act.wait_ge(z_used, n - 1)
                        S.activation(zt[:, n % 2, :], PS[:, n % 4, 0:SLICE], ACT.Silu).then_inc(z_silu, 1)
                act.wait_ge(z_used, D_INNER // SLICE * NT)
                act.wait_ge(products, at["z", D_INNER // SLICE - 1, NT - 1])
                act.wait_ge(nw_loaded, 16)
                for k in range(2 * KD):
                    act.wait_ge(products, at["yt", k])
                    S.activation(yT[:, k, 0:P], PS[:, 2 * (k % 4), 0:P], ACT.Copy, scale=nw[:, k:k + 1]).then_inc(yt_a, 1)
                junk = hT[:, 0:4, 0:512]
                for t in range(NT):
                    link(S.activation(junk, y[:, t, :].rearrange("p (a b) -> p a b", a=4), ACT.Square, accum_out=ssq[:, t:t + 1]))
                S.activation(ssq[:], ssq[:], ACT.Sqrt, bias=eps[:, 0:1], scale=1.0 / D_INNER).then_inc(ssq_done, 1)
                act.wait_ge(rr_ready, 1)
                for s in range(KD):
                    for t in range(NT):
                        act.wait_ge(products, at["oo", s, t])
                        S.activation(f[:, t, s * P:(s + 1) * P], PS[:, (s * NT + t) % 8, 0:P], ACT.Copy, scale=ssq[:, t:t + 1]).then_inc(oo_evac, 1)
                deviation(5, NT)

            if "even" in run:
                even()
            if "peer0" in run:
                peer(0)
            if "odd" in run:
                odd()
            if "peer1" in run:
                peer(1)
            act.wait_ge(x_ready, len(run))
            act.dma_start(o["y_prompt"], x[:, 0, :]).then_inc(stored, 16)
            act.dma_start(o["y_sample"], x[:, 1:NT, :]).then_inc(stored, 16)
            act.wait_ge(stored, 32 + (48 if "even" in run else 0))

        @block.gpsimd
        def _(pool):
            G = nc.gpsimd
            ch = Chain(pool, pool_chain)
            do, link, settle = ch.do, ch.link, ch.settle
            do(G.memset(ident[:], 0.0))
            do(G.memset(eps[:], EPS))
            link(G.memset(ones[:], 1.0))
            G.affine_select(out=ident[:], in_=ident[:], compare_op=ALU.not_equal, fill=1.0, base=0,
                            pattern=[[-1, P]], channel_multiplier=1).then_inc(consts_ready, 1)

            def one_sided(dst, src, d, fill):
                sign = 1 if d == 0 else -1
                return G.affine_select(out=dst, in_=src, compare_op=ALU.is_ge, fill=fill, base=0,
                                       pattern=[[sign, P]], channel_multiplier=-sign)

            def even():
                pool.wait_ge(mod_cols, DEPTH)
                pool.wait_ge(gates_stored, 32 * DEPTH)
                do(G.memset(mask[:], 0.0))
                do(G.memset(sel4[:], 0.0))
                do(G.iota(diff[:, 0, :], [[1, P]], base=0, channel_multiplier=-1, allow_small_or_imprecise_dtypes=True))
                do(G.iota(diff[:, 1, :], [[-1, P]], base=0, channel_multiplier=1, allow_small_or_imprecise_dtypes=True))
                for i, (b, m) in enumerate(((1, 1), (P, -1), (P - 1, -1), (0, 1))):
                    do(G.iota(icol[:, i:i + 1], [[0, 1]], base=b, channel_multiplier=m, allow_small_or_imprecise_dtypes=True))
                settle()
                for d in range(2):
                    do(one_sided(mask[:, d, :], mask[:, d, :], d, NEG))
                do(G.tensor_scalar(diff[:], diff[:], 0.0, None, ALU.max))
                G.affine_select(out=sel4[:], in_=sel4[:], compare_op=ALU.not_equal, fill=1.0, base=0,
                                pattern=[[-1, NH], [0, P]], channel_multiplier=1).then_inc(ev_consts, 1)
                for fam in range(2):
                    if fam == 1:
                        pool.wait_ge(decay_exp, 1)
                        for d in range(2):
                            for h in range(NH):
                                last = one_sided(Dm[:, d, h, :], Dm[:, d, h, :], d, 0.0)
                                if (d, h) != (1, NH - 1):
                                    do(last)
                        last.then_inc(dm_ready, 1)
                    pool.wait_ge(proj_a, proj_count["o", fam, (1, NT - 1)][2])
                    pool.wait_ge(even_loaded, 80)
                    G.tensor_tensor(og, og, gn[:, fam, :].unsqueeze(1).broadcast_to([P, NT, W_A]), ALU.mult).then_inc(og_ready, 1)
                    pool.wait_ge(proj_v, proj_count["kt", fam, NT - 1][2])
                    pool.wait_ge(cols_ready, 1)
                    if fam == 1:
                        pool.wait_ge(dm_ready, 1)
                    for u in range(NU - 2 * NH):
                        s, h, d = UNITS[u]
                        t = tile_of(s, d)
                        if u >= 2:
                            pool.wait_ge(products, at["H", fam, u - 2])
                        w = cols[:, t, 0, d, h:h + 1] if fam == 0 else xz[:, 1, d, h:h + 1]
                        G.tensor_scalar(kw[:, u % 2, :], ktok[:, t, h, :], w, None, ALU.mult).then_inc(kw_ready, 1)

            def peer(l):
                pool.wait_ge(x_ready, 2 * l + 2)
                G.iota(iota[:], [[1, N_KEYS]], base=0, channel_multiplier=0, allow_small_or_imprecise_dtypes=True).then_inc(iota_ready, 1)

                def low(n, k):
                    pool.wait_ge(hi_ready, l * NB + n + 1)
                    G.tensor_tensor(wL[:, k % NSPLIT, :], raw[:, k % NRAW, :], wH[:, k % NSPLIT, :].bitcast(f32), ALU.subtract).then_inc(lo_ready, 1)

                with pool.Fori(0, 9) as i:
                    for k in range(8):
                        low(8 * i + k, k)
                pool.wait_ge(products, at["v", l])
                with pool.Fori(0, 16) as i:
                    for k in range(4):
                        pool.wait_ge(hi_ready, l * NB + 72 + 4 * i + k + 1)
                        G.tensor_tensor(wLv[:, k, :], rawV[:, k % 2, :], wHv[:, k, :].bitcast(f32), ALU.subtract).then_inc(lo_ready, 1)

            def odd():
                pool.wait_ge(x_ready, 3)
                for i in range(2):
                    do(G.memset(cpad[:, i, :], 0.0))
                for d in range(2):
                    do(G.memset(maskO[:, d, :], 0.0))
                settle()
                for d in range(2):
                    do(one_sided(maskO[:, d, :], maskO[:, d, :], d, NEG))
                do(one_sided(tri[:, 0, :], ones[:], 0, 0.0))
                one_sided(tri[:, 1, :], ones[:], 1, 0.0).then_inc(od_consts, 1)
                for g in range(G_C):
                    pool.wait_ge(tr_evac, g * 5 + 5)
                    for s in range(NT - 1):
                        for d in range(2):
                            t = tile_of(s, d)
                            nu = (g * 4 + s) * 2 + d
                            if nu >= 1:
                                gg, ss = divmod((nu - 1) // 2, 4)
                                pool.wait_ge(products, at["upd", gg, ss, (nu - 1) % 2])
                            G.tensor_tensor(xw[:].rearrange("p (j c) -> p j c", j=J_C), xs[:, t, :].rearrange("p (j c) -> p j c", j=J_C),
                                            bc(wup[:, t, d, g * J_C:(g + 1) * J_C], P_C), ALU.mult).then_inc(xw_ready, 1)

            if "even" in run:
                even()
            if "peer0" in run:
                peer(0)
            if "odd" in run:
                odd()
            if "peer1" in run:
                peer(1)

        @block.sync
        def _(sp):
            freed = []

            def load(src, k, before=None):
                n = len(freed) if k is None else k
                if before is not None:
                    sp.wait_ge(products, before)
                elif n >= NSLOT:
                    sp.wait_ge(products, freed[n - NSLOT])
                w = src.shape[-1]
                sp.dma_start(ring[:, n % NSLOT, 0:w], src).then_inc(slot_full[n % NSLOT], 16)

            for entry in slices:
                src = entry[0]
                if src == "peer":
                    l = entry[1]
                    sp.wait_ge(x_ready, 2 * l + 2)
                    for n in range(8):
                        if n >= NRAW:
                            sp.wait_ge(lo_ready, l * NB + n - NRAW + 1)
                        sp.dma_start(raw[:, n % NRAW, :], a["w_pq"][l, n]).then_inc(raw_full[n % NRAW], 16)
                    with sp.Fori(0, 8) as i:
                        for k in range(8):
                            sp.wait_ge(lo_ready, l * NB + 8 + 8 * i + k - NRAW + 1)
                            sp.dma_start(raw[:, k % NRAW, :], a["u"][l, 8 * i + k]).then_inc(raw_full[k % NRAW], 16)
                    for half in range(2):
                        sp.wait_ge(a_stored[half], 16 * 32 * (l + 1))
                        sp.wait_ge(g_stored[half], 16 * 20 * (l + 1))
                    sp.wait_ge(products, at["v", l])

                    def value_loads(i, first):
                        if not first:
                            sp.wait_ge(w_ready, l * 32 + 2 * i)
                        sp.dma_start(ab, Ad[i]).then_inc(ag_full, 16)
                        sp.dma_start(gb[:], Gd[i]).then_inc(ag_full, 16)
                        for k in range(4):
                            if not (first and k < NVRAW):
                                sp.wait_ge(lo_ready, l * NB + 72 + 4 * i + k - NVRAW + 1)
                            sp.dma_start(rawV[:, k % NVRAW, :], a["v"][l, 4 * i + k]).then_inc(vraw_full[k % NVRAW], 16)

                    value_loads(0, True)
                    with sp.Fori(1, NBLK) as i:
                        value_loads(i, False)
                    sp.wait_ge(products, at["v_end", l])
                    sp.wait_ge(x_ready, 2 * l + 3)
                else:
                    load(src, None)
                    freed.append(at[entry[1]])


def kernel(**inputs):
    import numpy as _np
    import concourse.bacc as _bacc
    from concourse import mybir as _mybir
    from concourse.bass_utils import run_bass_kernel_spmd as _run
    return launch(inputs, _np, _bacc, _mybir, _run, None)


def layouts(i):
    c_ = np.ascontiguousarray

    def rows(w, ncol):
        lead, (K, N) = w.shape[:-2], w.shape[-2:]
        w = w.reshape(*lead, K // P, P, N // ncol, ncol)
        n = len(lead)
        w = w.transpose(*range(n), n + 2, n + 1, n, n + 3)
        return c_(w.reshape(*lead, N // ncol, P, K // P * ncol))

    r = {k: np.asarray(v) for k, v in i.items()}
    a = {}
    a["c"] = c_(np.stack([r["c_ctx"].reshape(KD, P), r["c"][0].reshape(KD, P)], -1).transpose(1, 0, 2))
    a["b_mod"] = c_(np.stack([r["b_mod"]] * 2, 0))
    a["x_prompt"] = c_(r["x_prompt"][0])
    a["x_sample"] = c_(r["x_sample"][0].reshape(NT - 1, P, D).transpose(1, 0, 2))
    a["w_mod"] = rows(r["w_mod"], SLICE)
    w = r["even_w_in"][0]
    sizes = [W_A] * 4 + [2 * NH] * 2 + [W_A] * 4
    at = np.cumsum([0] + sizes)
    part = [w[:, at[n]:at[n + 1]] for n in range(10)]
    a["w_even"] = np.stack([np.stack([rows(q, SLICE) for q in part[0:4]]), np.stack([rows(q, SLICE) for q in part[6:10]])])
    wg = np.zeros((D, P), np.float32)
    for q in range(4):
        src = part[4 + q // 2]
        wg[:, 32 * q:32 * q + NH] = src[:, (q % 2) * NH:(q % 2 + 1) * NH]
    a["w_gate"] = rows(wg, P)[0]
    a["gate_bias"] = c_(np.concatenate([r["mlstm_i_bias"][0], r["mlstm_f_bias"][0]], 0).T)
    a["m0"] = c_(r["state_mlstm_m"][0, 0].T)
    a["gn"] = c_(np.stack([r["even_gn_a"][0], r["even_gn_b"][0]]).reshape(-1))
    a["log_decay"] = c_(r["ret_log_decay"][0].reshape(-1))
    a["Cn0"] = c_(np.concatenate([r["state_mlstm_C"][0, 0], r["state_mlstm_n"][0, 0][..., None]], -1).transpose(2, 0, 1, 3))
    a["S0"] = c_(r["state_ret"][0, 0].transpose(2, 0, 1, 3))
    a["w_eout"] = rows(r["even_w_out"][0], SLICE)
    a["ln_g"] = c_(np.stack([r["ln1_g"][0], r["ln2_g"][0], r["ln1_g"][1], r["ln2_g"][1]]))
    a["ln_b"] = c_(np.stack([r["ln1_b"][0], r["ln2_b"][0], r["ln1_b"][1], r["ln2_b"][1]]))
    w = r["odd_w_in"][0]
    a["w_z"] = rows(w[:, 0:D_INNER], SLICE)
    xbc = w[:, D_INNER:D_INNER + CONV_DIM]
    order = []
    for g in range(G_C):
        order += list(range(g * GC, (g + 1) * GC))
        order += list(range(D_INNER + g * N_C, D_INNER + (g + 1) * N_C))
        order += list(range(D_INNER + G_C * N_C + g * N_C, D_INNER + G_C * N_C + (g + 1) * N_C))
    a["w_xbc"] = c_(rows(xbc[:, order], SLICE).reshape(G_C, 3, P, KD * SLICE))
    a["w_dt"] = rows(w[:, D_INNER + CONV_DIM:], 64)[0]
    cw_ = np.concatenate([r["odd_conv_w"][0], r["odd_conv_b"]], 0)[:, order]
    a["conv"] = c_(cw_.reshape(D_CONV + 1, 24, P).transpose(2, 1, 0))
    a["odd_rows"] = c_(np.concatenate([r["odd_dt_bias"].reshape(-1), r["odd_a_log"].reshape(-1), r["odd_d"].reshape(-1), r["odd_d"].reshape(-1)]))
    a["h0"] = c_(r["state_ssd"][0, 0].reshape(2, G_C, GC, N_C).transpose(1, 3, 0, 2))
    a["norm_w"] = c_(r["odd_norm_w"][0].reshape(2 * KD, P).T)
    a["w_oout"] = rows(r["odd_w_out"][0], P)
    a["w_pq"] = rows(r["peer_w_q"], SLICE)
    a["keys"] = c_(r["peer_sub_keys"].transpose(0, 4, 1, 2, 3).reshape(DEPTH, P, 2 * H_P, N_KEYS))
    u = r["peer_u"].reshape(DEPTH, N_KEYS, N_KEYS // 2, 2, KD, P)
    a["u"] = c_(u.transpose(0, 2, 5, 4, 3, 1)).reshape(DEPTH, N_KEYS // 2, P, KD * SLICE)
    v = r["peer_v"].reshape(DEPTH, N_KEYS, N_KEYS // 2, 2, D)
    a["v"] = c_(v.transpose(0, 2, 1, 3, 4)).reshape(DEPTH, N_KEYS // 2, P, 2 * D)
    rr = np.repeat(np.arange(DEC // GRID_W, dtype=np.float32), GRID_W)
    cc = np.tile(np.arange(GRID_W, dtype=np.float32), DEC // GRID_W)
    fr = (1.0 / (10000.0 ** (np.arange(D // 4, dtype=np.float32) / (D // 4)))).astype(np.float32)
    er, ec = rr[:, None] * fr, cc[:, None] * fr
    pos_ = np.concatenate([np.sin(er), np.cos(er), np.sin(ec), np.cos(ec)], -1).astype(np.float32)
    a["pos"] = c_(pos_.reshape(NT - 1, P, D).transpose(1, 0, 2))
    return a


OUTS = {"y_prompt": [P, D], "y_sample": [P, NT - 1, D], "new_Cn": [P, 2, NH, DH + 1], "new_m": [NH, 2],
        "new_ret": [P, 2, NH, DH], "new_ssd": [G_C, P, 2, GC]}


def program(nc, arrays, mybir_, upto):
    f32 = mybir_.dt.float32
    a = {n: nc.dram_tensor(f"in_{n}", list(v.shape), f32, kind="ExternalInput").ap() for n, v in arrays.items()}
    o = {n: nc.dram_tensor(f"out_{n}", s, f32, kind="ExternalOutput").ap() for n, s in OUTS.items()}
    trunk(nc, a, o, upto)


def launch(inputs, np_, bacc, mybir_, run, upto):
    arrays = layouts(inputs)
    nc = bacc.Bacc("TRN2", target_bir_lowering=False, num_devices=1)
    program(nc, arrays, mybir_, upto)
    r = run(nc, [{f"in_{n}": v for n, v in arrays.items()}], core_ids=[0]).results[0]
    got = {n: r[f"out_{n}"] for n in OUTS}
    c_ = np_.ascontiguousarray
    Cn = got["new_Cn"].transpose(1, 2, 0, 3)
    return (
        got["y_prompt"][None],
        c_(got["y_sample"].transpose(1, 0, 2)).reshape(1, DEC, D),
        c_(Cn[..., 0:DH])[None, None],
        c_(Cn[..., DH])[None, None],
        c_(got["new_m"].T)[None, None],
        c_(got["new_ret"].transpose(1, 2, 0, 3))[None, None],
        c_(got["new_ssd"].transpose(2, 0, 3, 1)).reshape(1, 1, 2, H_C, P_C, N_C),
    )
```

```python
import numpy as np
import concourse.bass as bass
from concourse import mybir
from contextlib import ExitStack

D = 1024
P = 128
SEQ, DEC = 128, 512
T = SEQ + DEC
NT = T // P
KD = D // P
DEPTH = 2
GRID_W = 64
ALPHA = (2.0 * DEPTH) ** 0.25
EPS = 1e-5
NH = 4
DH = 128
W_A = NH * DH
D_INNER = 2 * D
P_C, N_C, G_C, J_C = 64, 128, 4, 8
H_C = G_C * J_C
D_CONV = 5
CONV_DIM = D_INNER + 2 * G_C * N_C
GC = J_C * P_C
N_KEYS, H_P, TOPK = 128, 8, 16
HK = H_P * TOPK
NMOD = 6 * D
SLICE = 256
NSLOT = 8
NRAW = 4
NSPLIT = 2
NVRAW = 2
NVSPLIT = 4
NB = 8 + 64 + 64
JB = 8
JV = 4
NBLK = N_KEYS // JB
HT = T // 2
NEG = -1.0e30


class Chain:

    def __init__(self, eng, sem):
        self.eng, self.sem, self.n = eng, sem, 0

    def do(self, ins):
        ins.then_inc(self.sem, 1)
        self.n = self.n + 1

    def settle(self):
        self.eng.wait_ge(self.sem, self.n)

    def link(self, ins):
        self.do(ins)
        self.settle()


def trunk(nc, a, o, upto):
    f32 = mybir.dt.float32
    f32r = mybir.dt.float32r
    bf16 = mybir.dt.bfloat16
    u32 = mybir.dt.uint32
    ALU = mybir.AluOpType
    ACT = mybir.ActivationFunctionType
    AX = mybir.AxisListType.X

    stages = ["mod", "even", "peer0", "odd", "peer1"]
    run = stages[: stages.index(upto) + 1] if upto else stages

    ctx = ExitStack()

    def sb(name, shape, dt=f32, scope=None):
        return (scope or ctx).enter_context(nc.sbuf_tensor(name, shape, dt))

    def sem(name):
        return ctx.enter_context(nc.semaphore(name))

    x = sb("x", [P, NT, D])
    wsc = ExitStack()
    wideR = sb("wideR", [P, 2 * NT * D], f32r, scope=wsc)
    wsc.close()
    wide = sb("wide", [P, 2 * NT * D])
    f = wide[:, 0:NT * D].rearrange("p (n d) -> p n d", n=NT)
    hi = wide[:, NT * D:2 * NT * D]
    ident = sb("ident", [P, P])
    ones = sb("ones", [P, P])
    modT = sb("modT", [P, DEPTH, 4, KD, 2])
    cT = sb("cT", [P, KD, 2])
    stat = sb("stat", [P, 20, 6])
    mv = sb("mv", [P, 20, 2])
    rstd = sb("rstd", [P, 20])
    nmr = sb("nmr", [P, NT])
    eps = sb("eps", [P, 1])
    PS = ctx.enter_context(nc.psum_tensor("PS", [P, 8, 512], f32))

    gdram = nc.dram_tensor("gate_rows", [DEPTH, 2, 2, D], f32, kind="Internal").ap()
    Ad = nc.dram_tensor("expert_acts", [NBLK, P, JB, T], f32, kind="Internal").ap()
    Gd = nc.dram_tensor("expert_gates", [NBLK, P, T // 16, JB, 16], f32, kind="Internal").ap()

    mx = ExitStack()
    ring = sb("ring", [P, NSLOT, KD * SLICE], scope=mx)
    hT = sb("hT", [P, KD, T], scope=mx)
    base = ExitStack()
    mrow = sb("mrow", [2, NMOD], scope=base)
    bmod = wide[0:2, 4 * D:4 * D + NMOD]
    base.close()

    ev = ExitStack()
    qT = sb("qT", [P, NH, T], scope=ev)
    kT = sb("kT", [P, NH, T], scope=ev)
    v1 = sb("v1", [P, NT, NH, DH + 1], scope=ev)
    ktok = hi[:, 0:NT * W_A].rearrange("p (n h d) -> p n h d", n=NT, h=NH)
    og = hi[:, NT * W_A:2 * NT * W_A].rearrange("p (n d) -> p n d", n=NT)
    row = sb("row", [NH, 2, T], scope=ev)
    small = sb("gate_small", [NH, 6, 2, NT], scope=ev)
    BE, ML, MP, DEC_, BM = (small[:, i] for i in range(5))
    m0 = sb("m0", [NH, 2], scope=ev)
    gbias = sb("gbias", [NH, 4], scope=ev)
    sel4 = sb("sel4", [NH, NH, P], scope=ev)
    cols = sb("cols", [P, NT, 4, 2, NH], scope=ev)
    decB = sb("decB", [P, NH, 2, NT], scope=ev)
    Cst = sb("Cst", [P, 2, NH, DH + 1], scope=ev)
    Cout = sb("Cout", [P, 2, NH, DH + 1], scope=ev)
    mask = sb("mask", [P, 2, P], scope=ev)
    Dm = sb("Dm", [P, 2, NH, P], scope=ev)
    diff = sb("diff", [P, 2, P], scope=ev)
    icol = sb("icol", [P, 4], scope=ev)
    lg = sb("lg", [P, 2, NH], scope=ev)
    xz = sb("xz", [P, 3, 2, NH], scope=ev)
    gn = sb("gn", [P, 2, W_A], scope=ev)
    eb = sb("eb", [P, 2, P], scope=ev)
    pb = sb("pb", [P, 2, P], scope=ev)
    kw = sb("kw", [P, 2, P], scope=ev)
    nd = sb("nd", [P, 2, DH + 2], scope=ev)
    gcol = Dm[0:8 * NH].rearrange("p d h t -> p (d h t)")[:, 0:T]
    ev.close()
    grow = wide[0:NH, 0:4 * 2 * T].rearrange("p (k d t) -> p k d t", k=4, d=2)
    b_m = hi[0:NH, 0:4 * T].rearrange("p (k d t) -> p k d t", k=2, d=2)

    ln = ExitStack()
    rowsB = sb("rowsB", [P, 4, D], scope=ln)
    ln.close()

    od = ExitStack()
    xs = sb("xs", [P, NT, GC], scope=od)
    BC = sb("BC", [P, 2, T], scope=od)
    Btok = sb("Btok", [P, NT, N_C], scope=od)
    hst = sb("hst", [P, 2, GC], scope=od)
    hout = sb("hout", [P, 2, GC], scope=od)
    EP = sb("EP", [P, 2, J_C, P], scope=od)
    cpad = sb("cpad", [P, 2, T + 8], scope=od)
    cacc = sb("cacc", [P, 2, T + 2], scope=od)
    sx = EP[:].rearrange("p a j t -> p a (j t)")[:, :, 0:T]
    dtc = sb("dtc", [P, NT, 2, H_C], scope=od)
    av = sb("av", [P, NT, 2, H_C], scope=od)
    nac = sb("nac", [P, NT, 2, H_C], scope=od)
    wup = sb("wup", [P, NT, 2, H_C], scope=od)
    win = sb("win", [P, NT, 2, H_C], scope=od)
    dcy = sb("dcy", [P, NT, 2, H_C], scope=od)
    tri = sb("tri", [P, 2, P], scope=od)
    maskB = sb("maskB", [P, 2, P], bf16, scope=od)
    identB = sb("identB", [P, P], bf16, scope=od)
    brow = sb("brow", [P, 3, 2 * H_C], scope=od)
    cw = sb("cw", [P, 24, D_CONV + 1], scope=od)
    otmp = sb("otmp", [P, GC], scope=od)
    xw = sb("xw", [P, GC], scope=od)
    od.close()
    oz = ExitStack()
    yT = sb("yT", [P, 2 * KD, T], scope=oz)
    zt = sb("zt", [P, 2, SLICE], scope=oz)
    nw = sb("nw", [P, 2 * KD], scope=oz)
    ssq = sb("ssq", [P, NT], scope=oz)
    rowsO = sb("rowsO", [P, 4, D], scope=oz)
    oz.close()
    y = wide[:, :].rearrange("p (n d) -> p n d", n=NT)

    mx.close()

    pu = ExitStack()
    hH = sb("hH", [P, KD, T], f32r, scope=pu)
    hL = sb("hL", [P, KD, T], f32r, scope=pu)
    raw = sb("raw", [P, NRAW, KD * SLICE], scope=pu)
    wH = sb("wH", [P, NSPLIT, KD * SLICE], f32r, scope=pu)
    wL = sb("wL", [P, NSPLIT, KD * SLICE], f32r, scope=pu)
    hkT = sb("hkT", [P, 3, T], scope=pu)
    abuf = sb("abuf", [P, 2, 2, T], scope=pu)
    iota = sb("iota", [P, N_KEYS], scope=pu)
    ps_ = ExitStack()
    sv = sb("sv", [P, NT, H_P, 2, TOPK], scope=ps_)
    si = sb("si", [P, NT, H_P, 2, TOPK], u32, scope=ps_)
    qb = sb("qb", [P, 2, T], scope=ps_)
    swork = sb("swork", [P, N_KEYS], scope=ps_)
    sif = sb("sif", [P, H_P, 2, TOPK], scope=ps_)
    best = sb("best", [P, NT, H_P, TOPK], scope=ps_)
    pos = sb("pos", [P, H_P, TOPK], u32, scope=ps_)
    posi = sb("posi", [P, 2, HK], u32, scope=ps_)
    posf = sb("posf", [P, 2, HK], scope=ps_)
    ssum = sb("ssum", [P, NT, H_P], scope=ps_)
    ps_.close()
    gH = sb("gH", [P, T], f32r, scope=pu)
    gL = sb("gL", [P, T], scope=pu)
    pu.close()
    eqb = wide[:, 0:TOPK * HK].rearrange("p (a b) -> p a b", b=TOPK)
    eqc = wide[:, TOPK * HK:2 * TOPK * HK].rearrange("p (a b) -> p a b", b=TOPK)
    gst = wide[:, 0:4096].rearrange("p (s j t) -> p s j t", s=2, j=P)
    hot = wideR[:, 4096:10240].rearrange("p (s c t i) -> p s c t i", s=2, c=3, t=8)
    cand = wide[:, 4096:4096 + 2 * TOPK * TOPK].rearrange("p (s n) -> p s n", s=2)
    def gate_halves(c):
        v_ = PS[:, 4 + 2 * c:6 + 2 * c, :].rearrange("p b (t c j) -> p c (b t) j", t=2, c=2)
        return v_[:, 0], v_[:, 1]

    hkt = wide[:, 6144:8064].rearrange("p (t c k) -> p t c k", t=NT, c=3)
    keys = wide[:, 8192:10240].rearrange("p (c n) -> p c n", c=2 * H_P)

    pv = ExitStack()
    wHv = sb("wHv", [P, NVSPLIT, 2 * D], f32r, scope=pv)
    wLv = sb("wLv", [P, NVSPLIT, 2 * D], f32r, scope=pv)
    rawV = sb("rawV", [P, NVRAW, 2 * D], scope=pv)
    WH = sb("WH", [P, 2, JV, T], f32r, scope=pv)
    WL = sb("WL", [P, 2, JV, T], f32r, scope=pv)
    rows_scope = ExitStack()
    rowsP = sb("rowsP", [P, 4, D], scope=rows_scope)
    rows_scope.close()
    gb = sb("gb", [P, T // 16, JB, 16], scope=pv)
    pv.close()
    htmp = [f[:, t, :].rearrange("p (k c) -> p k c", k=KD) for t in range(NT)]
    ab = hi.rearrange("p (j t) -> p j t", j=JB)

    products = sem("products")
    slot_full = [sem(f"slot_full{i}") for i in range(NSLOT)]
    vec_chain, act_chain, pool_chain = sem("vec_chain"), sem("act_chain"), sem("pool_chain")
    consts_ready, small_loaded = sem("consts_ready"), sem("small_loaded")
    c_ready, mod_evac, mod_rows, mod_cols = sem("c_ready"), sem("mod_evac"), sem("mod_rows"), sem("mod_cols")
    gates_stored, x_loaded, x_ready = sem("gates_stored"), sem("x_loaded"), sem("x_ready")
    h_evac_v, h_evac_a = sem("h_evac_v"), sem("h_evac_a")
    rows_loaded, var_ready, dev_ready = sem("rows_loaded"), sem("var_ready"), sem("dev_ready")
    stored = sem("stored")
    even_loaded, proj_a, proj_v = sem("even_loaded"), sem("proj_a"), sem("proj_v")
    gate_exp, gate_act, gates_done, cols_ready = sem("gate_exp"), sem("gate_act"), sem("gates_done"), sem("cols_ready")
    e_ready, exp_ready, p_ready, kw_ready = sem("e_ready"), sem("exp_ready"), sem("p_ready"), sem("kw_ready")
    h_done, state_ready, ret_ready = sem("h_done"), sem("state_ready"), sem("ret_ready")
    diff_ready, decay_ready, norm_done, og_ready = sem("diff_ready"), sem("decay_ready"), sem("norm_done"), sem("og_ready")
    out_evac = sem("out_evac")
    odd_loaded, dt_abs, dt_sp, a_ready, ac_ready, seg_exp = (sem(n) for n in
        ("odd_loaded", "dt_abs", "dt_sp", "a_ready", "ac_ready", "seg_exp"))
    pad_filled, conv_done, act_done, tr_evac, oexp_ready, op_ready, skip_ready, y_intra = (sem(n) for n in
        ("pad_filled", "conv_done", "act_done", "tr_evac", "oexp_ready", "op_ready", "skip_ready", "y_intra"))
    inter_done, xw_ready, upd_done, hst_loaded, hst_stored, z_silu, z_used, ssq_done, yt_v, yt_a, oo_evac = (sem(n) for n in
        ("inter_done", "xw_ready", "upd_done", "hst_loaded", "hst_stored", "z_silu", "z_used", "ssq_done", "yt_v", "yt_a", "oo_evac"))
    keys_loaded, q_evac, s_used, hk_ready, hk_evac, sm_exp, sm_sub = (sem(n) for n in
        ("keys_loaded", "q_evac", "s_used", "hk_ready", "hk_evac", "sm_exp", "sm_sub"))
    act_gelu, a_stored, hot_ready, g_evac, g_stored, w_ready, acc_done, iota_ready = (sem(n) for n in
        ("act_gelu", "a_stored", "hot_ready", "g_evac", "g_stored", "w_ready", "acc_done", "iota_ready"))
    a_stored, g_stored = [a_stored, sem("a_stored1")], [g_stored, sem("g_stored1")]
    ev_consts, od_consts, dm_ready, decay_exp, alog_exp, nw_loaded, rr_ready = (sem(n) for n in
        ("ev_consts", "od_consts", "dm_ready", "decay_exp", "alog_exp", "nw_loaded", "rr_ready"))

    ln_stats, ln_factors, ln_normed, x_scaled, x_tile = (sem(n) for n in ("ln_stats", "ln_factors", "ln_normed", "x_scaled", "x_tile"))
    g_high, ag_first, rows_moved = sem("g_high"), sem("ag_first"), sem("rows_moved")
    raw_full = [sem(f"raw_full{i}") for i in range(NRAW)]
    vraw_full = [sem(f"vraw_full{i}") for i in range(NVRAW)]
    hi_ready, lo_ready, hh_ready, hl_ready, wf_ready, wh_ready, ag_full = (sem(n) for n in
        ("hi_ready", "lo_ready", "hh_ready", "hl_ready", "wf_ready", "wh_ready", "ag_full"))

    at = {}
    slices = []
    UNITS = [(s, h, d) for s in range(NT) for h in range(NH) for d in range(2)]
    NU = len(UNITS)

    seg_bank = [5, 0]

    def tile_of(step, d):
        return step if d == 0 or step == 0 else NT - step

    def first_on(step, d):
        t = tile_of(step, d)
        other = t if d == 1 else (NT - t if t else 0)
        return step < other or (step == other and d == 0)

    def bc(v, n):
        return v.unsqueeze(len(v.shape)).broadcast_to(list(v.shape) + [n])

    at_h = {0: 0, 4: NT, 1: NT + KD, 2: 2 * NT + KD, 3: 3 * NT + KD}

    pair_h = {0: 0, 1: 1, 2: 0, 3: 1}

    proj = []
    for fam in range(2):
        if fam == 0:
            proj.append(("gate", 0, 0, "v"))
        proj += [("q", fam, i, "a") for i in range(NH)] + [("k", fam, i, "a") for i in range(NH)]
        proj += [("v", fam, (s, t), "v") for s in range(2) for t in range(NT)]
        proj += [("o", fam, (s, t), "a") for s in range(2) for t in range(NT)]
        proj += [("kt", fam, t, "v") for t in range(NT)]
    proj_count, n_a, n_v = {}, 0, 0
    for i, (kind, fam, m, e) in enumerate(proj):
        n_a, n_v = n_a + (e == "a"), n_v + (e == "v")
        proj_count[kind, fam, m] = (i, e, n_a if e == "a" else n_v)

    with ctx, nc.Block() as block:

        @block.tensor
        def _(pe):
            state = {"n": 0, "slice": 0}

            def done(ins, label):
                ins.then_inc(products, 1)
                state["n"] = state["n"] + 1
                at[label] = state["n"]

            def take(src):
                n = state["slice"]
                state["slice"] += 1
                pe.wait_ge(slot_full[n % NSLOT], 16 * (n // NSLOT + 1))
                slices.append([src, None])
                return ring[:, n % NSLOT, 0:src.shape[-1]]

            def release(label):
                slices[-1][1] = label

            def evacuated(kind, fam, m):
                _, e, n = proj_count[kind, fam, m]
                pe.wait_ge(proj_a if e == "a" else proj_v, n)

            pe.wait_ge(consts_ready, 1)
            pe.wait_ge(c_ready, 1)
            for l in range(DEPTH):
                for s in range(NMOD // SLICE):
                    g = l * (NMOD // SLICE) + s
                    w = take(a["w_mod"][l, s]).rearrange("p (k n) -> p k n", k=KD)
                    if g >= 4:
                        pe.wait_ge(mod_evac, g - 3)
                    for k in range(KD):
                        last = nc.tensor.matmul(PS[0:2, g % 4, 0:SLICE], cT[:, k, :], w[:, k, :],
                                                start=(k == 0), stop=(k == KD - 1))
                    done(last, ("mod", l, s))
                    release(("mod", l, s))
                pe.wait_ge(mod_rows, l + 1)
                if l:
                    pe.wait_ge(mod_cols, l)
                for i, kind in enumerate((0, 1, 3, 4)):
                    for k in range(KD):
                        c = (i * KD + k) * 2
                        last = nc.tensor.matmul(PS[:, 4, c:c + 2], mrow[0:2, kind * D + k * P:kind * D + (k + 1) * P],
                                                ident[0:2, 0:2], start=True, stop=True)
                done(last, ("fold", l))

            def modulated(n):
                first = pair_h[n]
                for t in range(NT):
                    if n == 0 or t == NT - 1:
                        pe.wait_ge(x_ready, n + 1)
                    else:
                        pe.wait_ge(x_tile, (n - 1) * (NT - 1) + t + 1)
                    if n == 0:
                        pe.wait_ge(mod_cols, DEPTH)
                    else:
                        sem_, before = ((out_evac, 0), (acc_done, 31 * NT), (oo_evac, 0))[n - 1]
                        pe.wait_ge(sem_, before + min(t + 2, NT))
                    if t >= 4:
                        pe.wait_ge(h_evac_v, at_h[n] + t - 3)
                        pe.wait_ge(h_evac_a, at_h[n] + t - 3)
                    b = 2 * ((t + first) % 4)
                    for k in range(KD):
                        last = nc.tensor.transpose(PS[:, b + k // 4, (k % 4) * P:(k % 4 + 1) * P], x[:, t, k * P:(k + 1) * P], ident[:])
                    done(last, ("h", n, t))
                pe.wait_ge(h_evac_v, at_h[n] + NT)
                pe.wait_ge(h_evac_a, at_h[n] + NT)

            def feature_major(w, m, pair):
                for half in range(2):
                    for k in range(KD):
                        last = nc.tensor.matmul(PS[:, 2 * pair + half, 0:HT], w[:, k, m * P:(m + 1) * P],
                                                hT[:, k, half * HT:(half + 1) * HT], start=(k == 0), stop=(k == KD - 1))
                return last

            def even():
                modulated(0)
                pe.wait_ge(ev_consts, 1)

                def pair_of(kind, fam, m):
                    i = proj_count[kind, fam, m][0]
                    if i >= 4:
                        evacuated(*proj[i - 4][:3])
                    return i % 4

                for fam in range(2):
                    if fam == 0:
                        w = take(a["w_gate"]).rearrange("p (k n) -> p k n", k=KD)
                        done(feature_major(w, 0, pair_of("gate", 0, 0)), ("gate",))
                        release(("gate",))
                    else:
                        pe.wait_ge(h_done, NU)
                        pe.wait_ge(state_ready, NU - 2 * NH)
                    for kind in ("q", "k"):
                        for i in range(NH):
                            if i % 2 == 0:
                                w = take(a["w_even"][fam, {"q": 0, "k": 1}[kind], i // 2]).rearrange("p (k n) -> p k n", k=KD)
                            done(feature_major(w, i % 2, pair_of(kind, fam, i)), (kind, fam, i))
                            release((kind, fam, i))
                    for kind in ("v", "o"):
                        for s in range(2):
                            w = take(a["w_even"][fam, {"v": 2, "o": 3}[kind], s]).rearrange("p (k n) -> p k n", k=KD)
                            for t in range(NT):
                                pr = pair_of(kind, fam, (s, t))
                                for k in range(KD):
                                    last = nc.tensor.matmul(PS[:, 2 * pr, 0:SLICE], hT[:, k, t * P:(t + 1) * P], w[:, k, :],
                                                            start=(k == 0), stop=(k == KD - 1))
                                done(last, (kind, fam, (s, t)))
                            release((kind, fam, (s, NT - 1)))
                    if fam == 0:
                        pe.wait_ge(gates_done, 1)
                        evacuated("o", 0, (1, NT - 1))
                        evacuated("v", 0, (1, NT - 1))
                        pe.wait_ge(rows_moved, 8 * 16)
                        for t in range(NT):
                            nc.tensor.transpose(PS[:, 7, t * 8 * NH:(t + 1) * 8 * NH], gcol[:, t * P:(t + 1) * P], ident[0:8 * NH, 0:8 * NH])
                        for h in range(NH):
                            last = nc.tensor.matmul(PS[:, 7, 256 + h * 2 * NT:256 + (h + 1) * 2 * NT], sel4[:, h, :],
                                                    DEC_.rearrange("p d t -> p (d t)"), start=True, stop=True)
                        done(last, ("cols",))
                        pe.wait_ge(cols_ready, 1)
                    evacuated("k", fam, NH - 1)
                    for t in range(NT):
                        pr = pair_of("kt", fam, t)
                        for h in range(NH):
                            last = nc.tensor.transpose(PS[:, 2 * pr, h * P:(h + 1) * P], kT[:, h, t * P:(t + 1) * P], ident[:])
                        done(last, ("kt", fam, t))
                    evacuated("kt", fam, NT - 1)
                    evacuated("o", fam, (1, NT - 1))
                    evacuated("v", fam, (1, NT - 1))
                    width = DH + 1 if fam == 0 else DH
                    for i in range(NU + 2):
                        if i < NU:
                            s, h, d = UNITS[i]
                            t = tile_of(s, d)
                            if i >= 2:
                                pe.wait_ge(p_ready, fam * NU + i - 1)
                            last = nc.tensor.matmul(PS[:, i % 2, 0:P], kT[:, h, t * P:(t + 1) * P], qT[:, h, t * P:(t + 1) * P],
                                                    start=True, stop=True)
                            if fam == 0:
                                last = nc.tensor.matmul(PS[:, i % 2, P:2 * P], sel4[:, h, :], row[:, d, t * P:(t + 1) * P],
                                                        start=True, stop=True)
                            done(last, ("S", fam, i))
                        u = i - 2
                        if u >= 0:
                            s, h, d = UNITS[u]
                            t = tile_of(s, d)
                            pe.wait_ge(p_ready, fam * NU + u + 1)
                            if u >= 2:
                                pe.wait_ge(h_done, fam * NU + u - 1)
                            if s < NT - 1:
                                pe.wait_ge(kw_ready, fam * (NU - 2 * NH) + u + 1)
                                last = nc.tensor.matmul(PS[:, 4 + u % 2, 0:width], kw[:, u % 2, :], v1[:, t, h, 0:width],
                                                        start=True, stop=True)
                            if s > 0:
                                pe.wait_ge(even_loaded, 80)
                                if fam == 1:
                                    pe.wait_ge(ret_ready, 16)
                                if s > 1:
                                    pe.wait_ge(state_ready, fam * (NU - 2 * NH) + u - 2 * NH + 1)
                                nc.tensor.matmul(PS[:, 2 + u % 2, 256:256 + width], qT[:, h, t * P:(t + 1) * P],
                                                 Cst[:, d, h, 0:width], start=True, stop=True)
                            last = nc.tensor.matmul(PS[:, 2 + u % 2, 0:width], pb[:, u % 2, :], v1[:, t, h, 0:width],
                                                    start=True, stop=True)
                            done(last, ("H", fam, u))
                pe.wait_ge(norm_done, 1)
                pe.wait_ge(h_done, 2 * NU)
                for k in range(KD):
                    if k == KD // 2:
                        pe.wait_ge(norm_done, 2)
                    if k >= 4:
                        pe.wait_ge(h_evac_v, at_h[4] + k - 3)
                        pe.wait_ge(h_evac_a, at_h[4] + k - 3)
                    b = 2 * (k % 4)
                    for t in range(NT):
                        dst = PS[:, b, 0:P] if t == 0 else PS[:, b + 1, (t - 1) * P:t * P]
                        last = nc.tensor.transpose(dst, f[:, t, k * P:(k + 1) * P], ident[:])
                    done(last, ("h", 4, k))
                pe.wait_ge(h_evac_v, at_h[4] + KD)
                pe.wait_ge(h_evac_a, at_h[4] + KD)
                ws = [take(a["w_eout"][s]).rearrange("p (k n) -> p k n", k=KD) for s in range(D // SLICE)]
                for t in range(NT):
                    if t >= 4:
                        pe.wait_ge(out_evac, t - 3)
                    for s, w in enumerate(ws):
                        for k in range(KD):
                            last = nc.tensor.matmul(PS[:, 2 * (t % 4) + s // 2, (s % 2) * SLICE:(s % 2 + 1) * SLICE], hT[:, k, t * P:(t + 1) * P],
                                                    w[:, k, :], start=(k == 0), stop=(k == KD - 1))
                    done(last, ("eo", t))
                for s in range(D // SLICE):
                    slices[-1 - s][1] = ("eo", NT - 1)

            def split_products(out, lhsH, lhsL, rhsH, rhsL, start, stop):
                nc.tensor.matmul(out, lhsH, rhsH, start=start, stop=False)
                nc.tensor.matmul(out, lhsH, rhsL, start=False, stop=False)
                return nc.tensor.matmul(out, lhsL, rhsH, start=False, stop=stop)

            def feature_major_split(slot, m, pair):
                for half in range(2):
                    c = slice(half * HT, (half + 1) * HT)
                    for k in range(KD):
                        w = slice(k * SLICE + m * P, k * SLICE + (m + 1) * P)
                        last = split_products(PS[:, 2 * pair + half, 0:HT], wH[:, slot, w], wL[:, slot, w], hH[:, k, c], hL[:, k, c],
                                              k == 0, k == KD - 1)
                return last

            def peer(l):
                modulated(2 * l + 1)
                pe.wait_ge(hl_ready, NT * (l + 1))
                for m in range(2 * H_P):
                    g = l * 2 * H_P + m
                    if m % 2 == 0:
                        pe.wait_ge(lo_ready, l * NB + m // 2 + 1)
                    if m >= 2:
                        pe.wait_ge(q_evac, g - 1)
                    done(feature_major_split(m // 2 % NSPLIT, m % 2, m % 2), ("pq", l, m))
                    if m == 0:
                        pe.wait_ge(keys_loaded, 16 * (l + 1))
                    pe.wait_ge(q_evac, g + 1)
                    if m >= 2:
                        pe.wait_ge(s_used, NT * (g - 1))
                    for t in range(NT):
                        b = 4 + 2 * (m % 2) + (t == NT - 1)
                        last = nc.tensor.matmul(PS[:, b, (t % 4) * P:(t % 4 + 1) * P], qb[:, m % 2, t * P:(t + 1) * P],
                                                keys[:, m, :], start=True, stop=True)
                    done(last, ("ps", l, m))
                base_n = state["n"]

                def act_pass(i, build):
                    for jj in range(16):
                        gj = l * N_KEYS + i * 16 + jj
                        if jj % 2 == 0:
                            pe.wait_ge(lo_ready, l * NB + 8 + 8 * i + jj // 2 + 1)
                        if not (isinstance(i, int) and i == 0 and jj < 2 and l == 0):
                            pe.wait_ge(act_gelu, gj - 1)
                        feature_major_split(jj // 2 % NSPLIT, jj % 2, jj % 2).then_inc(products, 1)
                        if build:
                            gq = l * 80 + (i - 3) * 16 + jj
                            pe.wait_ge(hot_ready, gq + 1)
                            for c in range(2):
                                if not (isinstance(i, int) and l == 0 and i == 3 and jj == 0):
                                    pe.wait_ge(g_evac, 2 * gq + c - 1)
                                for tk in range(4 * c, 4 * c + 4):
                                    last = nc.tensor.matmul(PS[:, 4 + tk // 2, (tk % 2) * 2 * P:(tk % 2 + 1) * 2 * P].rearrange("p (c j) -> p c j", c=2),
                                                            hot[:, jj % 2, 0, tk, :], hot[:, jj % 2, 1:3, tk, :], start=True, stop=True)
                                last.then_inc(products, 1)

                act_pass(0, False)
                with pe.Fori(1, 3) as i:
                    act_pass(i, False)
                n_tr = base_n + 3 * 16
                for t in range(NT):
                    if t == 0:
                        pe.wait_ge(hk_ready, l + 1)
                    if t >= 2:
                        pe.wait_ge(hk_evac, l * NT + t - 1)
                    for c in range(3):
                        last = nc.tensor.transpose(PS[:, 4 + t % 2, c * P:(c + 1) * P], hkt[:, t, c, :], ident[:])
                    last.then_inc(products, 1)
                    at["hk", l, t] = n_tr + t + 1
                pe.wait_ge(hk_evac, l * NT + NT)
                n_b = n_tr + NT
                at["u", l], at["ub", l] = base_n, n_b
                act_pass(3, True)
                with pe.Fori(4, 8) as i:
                    act_pass(i, True)
                state["n"] = n_b + 5 * 48
                base_n = state["n"]
                at["v", l] = base_n
                slices.append(["peer", l])

                def value_pass(i):
                    for q in range(4):
                        blk = 4 * i + q
                        pe.wait_ge(lo_ready, l * NB + 72 + 2 * blk + 2)
                        pe.wait_ge(w_ready, l * 32 + blk + 1)
                        for t in range(NT):
                            pr = (q * NT + t) % 4
                            gg = (l * 32 + blk) * NT + t
                            if not (isinstance(i, int) and q * NT + t < 4 and l == 0):
                                pe.wait_ge(acc_done, gg - 3)
                            for c in range(2):
                                for j in range(JV):
                                    slot, v = 2 * (q % 2) + j // 2, slice((j % 2) * D + c * 512, (j % 2) * D + (c + 1) * 512)
                                    tt = slice(t * P, (t + 1) * P)
                                    last = split_products(PS[:, 2 * pr + c, :], WH[:, q % 2, j, tt], WL[:, q % 2, j, tt],
                                                          wHv[:, slot, v], wLv[:, slot, v], j == 0, j == JV - 1)
                            last.then_inc(products, 1)

                value_pass(0)
                with pe.Fori(1, 8) as i:
                    value_pass(i)
                state["n"] = base_n + 32 * NT
                at["v_end", l] = state["n"]

            def odd():
                modulated(2)
                w = take(a["w_dt"]).rearrange("p (k n) -> p k n", k=KD)
                for t in range(NT):
                    for k in range(KD):
                        last = nc.tensor.matmul(PS[:, 0, t * 64:(t + 1) * 64], hT[:, k, t * P:(t + 1) * P], w[:, k, 0:64],
                                                start=(k == 0), stop=(k == KD - 1))
                done(last, ("dt",))
                release(("dt",))
                pe.wait_ge(a_ready, 1)
                for t in range(NT):
                    for d in range(2):
                        c = (t * 2 + d) * H_C
                        nc.tensor.matmul(PS[:, 1, c:c + H_C], tri[:, d, :], av[:, t, d, :], start=True, stop=True)
                last = nc.tensor.matmul(PS[:, 2, 0:NT * 64], ones[:], av[:].rearrange("p t d h -> p (t d h)"), start=True, stop=True)
                done(last, ("acum",))
                pe.wait_ge(ac_ready, 1)
                for g in range(G_C):
                    for m in range(7):
                        q = g * 6 + m
                        if m < 6:
                            if m % 2 == 0:
                                w = take(a["w_xbc"][g, m // 2]).rearrange("p (k n) -> p k n", k=KD)
                            if q >= 2:
                                pe.wait_ge(pad_filled, q - 1)
                            b = 2 * (m % 2)
                            for k in range(KD):
                                nc.tensor.matmul(PS[:, b, 0:P], w[:, k, (m % 2) * P:(m % 2 + 1) * P], hT[:, k, 0:P],
                                                 start=(k == 0), stop=(k == KD - 1))
                            for k in range(KD):
                                last = nc.tensor.matmul(PS[:, b + 1, :], w[:, k, (m % 2) * P:(m % 2 + 1) * P], hT[:, k, P:T],
                                                        start=(k == 0), stop=(k == KD - 1))
                            done(last, ("xbc", g, m))
                            if m % 2 == 1:
                                release(("xbc", g, m))
                        mm = m - 1
                        if 0 <= mm < 5:
                            qq = g * 6 + mm
                            src = sx[:, mm % 2, :] if mm < 4 else BC[:, 0, :]
                            pe.wait_ge(act_done, qq + 1)
                            n = g * 5 + mm
                            if n >= 2:
                                pe.wait_ge(tr_evac, n - 1)
                            for t in range(NT):
                                b = 4 + 2 * (n % 2) + (t == NT - 1)
                                last = nc.tensor.transpose(PS[:, b, (t % 4) * P:(t % 4 + 1) * P], src[:, t * P:(t + 1) * P], ident[:])
                            done(last, ("xt", g, mm))
                    pe.wait_ge(act_done, g * 6 + 6)
                    pe.wait_ge(pad_filled, g * 6 + 6)
                    pe.wait_ge(tr_evac, g * 5 + 5)
                    def between(s, d):
                        t = tile_of(s, d)
                        n, nu = (g * 4 + s - 1) * 2 + d, (g * 4 + s) * 2 + d
                        if s > 0:
                            if n >= 1:
                                pe.wait_ge(inter_done, n)
                            if s > 1:
                                pe.wait_ge(upd_done, nu - 1)
                            done(nc.tensor.matmul(PS[:, 2, :], BC[:, 1, t * P:(t + 1) * P], hst[:, d, :], start=True, stop=True),
                                 ("inter", g, s, d))
                        if s < NT - 1:
                            pe.wait_ge(xw_ready, nu + 1)
                            if nu >= 1:
                                pe.wait_ge(upd_done, nu)
                            done(nc.tensor.matmul(PS[:, 3, :], Btok[:, t, :], xw[:, :], start=True, stop=True), ("upd", g, s, d))

                    def segment(t, d):
                        n = g * NT + t
                        if n >= 1:
                            pe.wait_ge(oexp_ready, 2 * (n - 1) + d + 1)
                        for j in range(J_C):
                            bank = seg_bank[d] + j // 4
                            if j % 4 == 0:
                                nc.tensor.matmul(PS[:, bank, :].rearrange("p (a t) -> p a t", a=4), identB[:],
                                                 maskB[:, d, :].unsqueeze(1).broadcast_to([P, 4, P]), start=True, stop=False)
                            last = nc.tensor.matmul(PS[:, bank, (j % 4) * P:(j % 4 + 1) * P],
                                                    av[:, t, d, g * J_C + j:g * J_C + j + 1].broadcast_to([P, P]),
                                                    tri[:, d, :], start=False, stop=(j % 4 == 3))
                        done(last, ("seg", g, t, d))

                    def scores(t):
                        nc.tensor.matmul(PS[:, 4, 0:P], BC[:, 0, t * P:(t + 1) * P], BC[:, 1, t * P:(t + 1) * P],
                                         start=True, stop=True).then_inc(products, 1)
                        state["n"] += 1
                        at["cb", g, t] = state["n"]

                    pe.wait_ge(hst_loaded, 16 * (g + 1))
                    segment(0, 0)
                    segment(0, 1)
                    scores(0)
                    for i in range(NT):
                        n = g * NT + i
                        between(i, 0)
                        if i < NT - 1:
                            segment(i + 1, 0)
                            segment(i + 1, 1)
                        between(i, 1)
                        pe.wait_ge(op_ready, 2 * n + 2)
                        if n >= 1:
                            pe.wait_ge(y_intra, n)
                        for j in range(J_C):
                            for d in range(2):
                                last = nc.tensor.matmul(PS[:, 7, j * P_C:(j + 1) * P_C], EP[:, d, j, :], xs[:, i, j * P_C:(j + 1) * P_C],
                                                        start=(d == 0), stop=(d == 1))
                        done(last, ("intra", g, i))
                        if i < NT - 1:
                            scores(i + 1)
                    pe.wait_ge(y_intra, g * NT + NT)
                    pe.wait_ge(inter_done, (g + 1) * 8)
                    pe.wait_ge(upd_done, (g + 1) * 8)
                for s in range(D_INNER // SLICE):
                    w = take(a["w_z"][s]).rearrange("p (k n) -> p k n", k=KD)
                    for t in range(NT):
                        n = s * NT + t
                        if n >= 4:
                            pe.wait_ge(z_silu, n - 3)
                        for k in range(KD):
                            last = nc.tensor.matmul(PS[:, n % 4, 0:SLICE], hT[:, k, t * P:(t + 1) * P], w[:, k, :],
                                                    start=(k == 0), stop=(k == KD - 1))
                        done(last, ("z", s, t))
                    release(("z", s, NT - 1))
                pe.wait_ge(z_used, D_INNER // SLICE * NT)
                for k in range(2 * KD):
                    if k >= 4:
                        pe.wait_ge(yt_v, k - 3)
                        pe.wait_ge(yt_a, k - 3)
                    b = 2 * (k % 4)
                    for t in range(NT):
                        dst = PS[:, b, 0:P] if t == 0 else PS[:, b + 1, (t - 1) * P:t * P]
                        last = nc.tensor.transpose(dst, y[:, t, k * P:(k + 1) * P], ident[:])
                    done(last, ("yt", k))
                pe.wait_ge(yt_v, 2 * KD)
                pe.wait_ge(yt_a, 2 * KD)
                ws = [take(a["w_oout"][s]).rearrange("p (k n) -> p k n", k=2 * KD) for s in range(KD)]
                for t in range(NT):
                    if t >= 4:
                        pe.wait_ge(oo_evac, t - 3)
                    for s, w in enumerate(ws):
                        for k in range(2 * KD):
                            last = nc.tensor.matmul(PS[:, 2 * (t % 4) + s // 4, (s % 4) * P:(s % 4 + 1) * P], yT[:, k, t * P:(t + 1) * P],
                                                    w[:, k, :], start=(k == 0), stop=(k == 2 * KD - 1))
                    done(last, ("oo", t))
                for s in range(KD):
                    slices[-1 - s][1] = ("oo", NT - 1)

            if "even" in run:
                even()
            if "peer0" in run:
                peer(0)
            if "odd" in run:
                odd()
            if "peer1" in run:
                peer(1)

        @block.vector
        def _(ve):
            V = nc.vector
            ch = Chain(ve, vec_chain)
            do, link, settle = ch.do, ch.link, ch.settle

            ve.wait_ge(x_loaded, 48)
            V.tensor_tensor(x[:, 1:NT, :], x[:, 1:NT, :], f[:, 0:NT - 1, :], ALU.add).then_inc(x_ready, 1)
            ve.wait_ge(small_loaded, 32)
            for l in range(DEPTH):
                if l:
                    ve.wait_ge(gates_stored, 32 * l)
                    ve.wait_ge(small_loaded, 32 + 16 * l)
                for s in range(NMOD // SLICE):
                    ve.wait_ge(products, at["mod", l, s])
                    c = slice(s * SLICE, (s + 1) * SLICE)
                    V.tensor_tensor(mrow[:, c], PS[0:2, (l * 24 + s) % 4, 0:SLICE], bmod[:, c], ALU.add).then_inc(mod_evac, 1)
                ve.wait_ge(mod_evac, (l + 1) * (NMOD // SLICE))
                do(V.tensor_scalar(mrow[:, D:2 * D], mrow[:, D:2 * D], 1.0, None, ALU.add))
                V.tensor_scalar(mrow[:, 4 * D:5 * D], mrow[:, 4 * D:5 * D], 1.0, None, ALU.add).then_inc(mod_rows, 1)
                ve.wait_ge(products, at["fold", l])
                V.tensor_copy(modT[:, l].rearrange("p a k g -> p (a k g)"), PS[:, 4, 0:64]).then_inc(mod_cols, 1)

            def modulated(n):
                l, kind = n // 2, 2 * (n % 2)
                ve.wait_ge(mod_cols, l + 1)
                for t in range(NT):
                    ve.wait_ge(products, at["h", n, t])
                    b, g = 2 * ((t + pair_h[n]) % 4) + 1, int(t > 0)
                    for k in range(4, KD):
                        last = V.tensor_scalar(hT[:, k, t * P:(t + 1) * P], PS[:, b, (k - 4) * P:(k - 3) * P], modT[:, l, kind + 1, k, g:g + 1],
                                               modT[:, l, kind, k, g:g + 1], ALU.mult, ALU.add)
                        if k < KD - 1:
                            do(last)
                    last.then_inc(h_evac_v, 1)

            def layer_norm(n, rows, gated):
                ve.wait_ge(rows_loaded, 48 * (n + 1))
                settle()
                for i in range(NT + 1):
                    if i < NT:
                        gated(i)
                        link(V.scalar_tensor_tensor(x[:, i, :], x[:, i, :], ALPHA, f[:, i, :], ALU.mult, ALU.add))
                        for c in range(2):
                            do(V.bn_stats(stat[:, 2 * i + c, :], x[:, i, c * 512:(c + 1) * 512]))
                        settle()
                        V.bn_aggr(mv[:, i, :], stat[:, 2 * i:2 * i + 2, :]).then_inc(ln_stats, 1)
                    t = i - 1
                    if t >= 0:
                        ve.wait_ge(ln_normed, n * NT + t + 1)
                        ins = V.tensor_tensor(x[:, t, :], x[:, t, :], rows[:, 0, :], ALU.mult)
                        if t < NT - 1:
                            ins.then_inc(x_scaled, 1)
                        else:
                            link(ins)
                            ve.wait_ge(x_tile, (n + 1) * (NT - 1))
                            V.tensor_tensor(x[:, t, :], x[:, t, :], rows[:, 1, :], ALU.add).then_inc(x_ready, 1)
                    if i < NT:
                        ve.wait_ge(dev_ready, 2 + n * NT + i + 1)
                        link(V.reciprocal(rstd[:, i:i + 1], rstd[:, i:i + 1]))
                        V.scalar_tensor_tensor(nmr[:, i:i + 1], mv[:, i, 0:1], -1.0, rstd[:, i:i + 1], ALU.mult, ALU.mult).then_inc(ln_factors, 1)
                ve.wait_ge(x_ready, n + 2)

            def even():
                modulated(0)
                ve.wait_ge(even_loaded, 80)
                ve.wait_ge(ev_consts, 1)
                ve.wait_ge(products, at["gate",])
                L, F, t1, t2 = (grow[:, i] for i in range(4))
                wg_, wint_, col_, enm_ = L, F, t1, t2
                b, m = b_m[:, 0], b_m[:, 1]
                dst = [L[:, 0], L[:, 1], F[:, 0], F[:, 1]]
                for q in range(4):
                    last = V.tensor_copy(dst[q].rearrange("p (a t) -> p a t", a=2), PS[32 * q:32 * q + NH, 0:2, 0:HT])
                    if q < 3:
                        do(last)
                last.then_inc(proj_v, 1)
                ve.wait_ge(proj_v, 1)
                for q in range(4):
                    do(V.tensor_scalar(dst[q], dst[q], gbias[:, q:q + 1], None, ALU.add))
                settle()
                V.scalar_tensor_tensor(t1, F, -1.0, F, ALU.mult, ALU.max).then_inc(gate_exp, 1)
                ve.wait_ge(gate_act, 1)
                link(V.scalar_tensor_tensor(F, F, 0.0, t1, ALU.min, ALU.subtract))
                do(V.memset(t2[:, :, 0:P], 1.0))
                settle()
                for t in range(NT):
                    c = slice(t * P, (t + 1) * P)
                    do(V.tensor_tensor_scan(b[:, 0, c], t2[:, 0, 0:P], F[:, 0, c], 0.0, ALU.mult, ALU.add))
                    r = F[:, 1, c]
                    do(V.tensor_tensor_scan(b[:, 1, c][:, ::-1], t2[:, 1, 0:P], r[:, ::-1], 0.0, ALU.mult, ALU.add))
                for c, start in ((slice(0, P), None), (slice(P, T), m0)):
                    do(V.tensor_tensor_scan(m[:, 0, c], F[:, 0, c], L[:, 0, c], 0.0 if start is None else start[:, 0:1], ALU.add, ALU.max))
                    do(V.tensor_tensor_scan(m[:, 1, c][:, ::-1], F[:, 1, c][:, ::-1], L[:, 1, c][:, ::-1],
                                            0.0 if start is None else start[:, 1:2], ALU.add, ALU.max))
                settle()
                for src, dst_ in ((b, BE), (m, ML)):
                    do(V.tensor_copy(dst_[:, 0, :], src[:, 0, :].rearrange("p (n t) -> p n t", t=P)[:, :, P - 1]))
                    do(V.tensor_copy(dst_[:, 1, :], src[:, 1, :].rearrange("p (n t) -> p n t", t=P)[:, :, 0]))
                do(V.memset(MP[:, :, 0], 0.0))
                do(V.tensor_copy(MP[:, 0, 1:2], m0[:, 0:1]))
                do(V.tensor_copy(MP[:, 1, NT - 1:NT], m0[:, 1:2]))
                settle()
                do(V.tensor_copy(MP[:, 0, 2:NT], ML[:, 0, 1:NT - 1]))
                do(V.tensor_copy(MP[:, 1, 1:NT - 1], ML[:, 1, 2:NT]))
                do(V.tensor_tensor(row[:, :, :], b, m, ALU.subtract))
                do(V.tensor_tensor(col_, L, b, ALU.subtract))
                settle()
                do(V.tensor_tensor(BM, BE, ML, ALU.subtract))
                settle()
                chunked = lambda z: z.rearrange("p d (n t) -> p (d n) t", t=P)
                flat = lambda z: z.rearrange("p d n -> p (d n)")
                do(V.tensor_tensor(chunked(F), chunked(row[:, :, :]), bc(flat(MP), P), ALU.add))
                do(V.tensor_tensor(chunked(L), chunked(col_), bc(flat(BM), P), ALU.add))
                V.tensor_tensor(DEC_, BM, MP, ALU.add).then_inc(gate_exp, 1)
                do(V.memset(v1[:, :, :, DH:DH + 1], 1.0))

                for fam in range(2):
                    for s in range(2):
                        for t in range(NT):
                            ve.wait_ge(products, at["v", fam, (s, t)])
                            V.tensor_copy(v1[:, t, 2 * s:2 * s + 2, 0:DH],
                                          PS[:, 2 * (proj_count["v", fam, (s, t)][0] % 4), 0:SLICE].rearrange("p (h d) -> p h d", h=2)
                                          ).then_inc(proj_v, 1)
                    if fam == 0:
                        ve.wait_ge(products, at["cols",])
                        do(V.tensor_copy(cols[:].rearrange("p n k d h -> p (n k d h)"), PS[:, 7, 0:160]))
                        V.tensor_copy(decB[:].rearrange("p h d n -> p (h d n)"), PS[:, 7, 256:296]).then_inc(cols_ready, 1)
                        ve.wait_ge(cols_ready, 1)
                    else:
                        ve.wait_ge(diff_ready, 1)
                        link(V.tensor_scalar(lg[:].rearrange("p d h -> p (d h)"), lg[:].rearrange("p d h -> p (d h)"), -1.0, None, ALU.mult))
                        for kind in range(2):
                            for d in range(2):
                                do(V.tensor_scalar(xz[:, kind, d, :], lg[:, d, :], icol[:, 2 * kind + d:2 * kind + d + 1], None, ALU.mult))
                        V.tensor_scalar(xz[:, 2], lg[:], float(P), None, ALU.mult).then_inc(decay_ready, 1)
                        ve.wait_ge(ret_ready, 16)
                        ve.wait_ge(stored, 32)
                        ve.wait_ge(dm_ready, 1)
                    for t in range(NT):
                        ve.wait_ge(products, at["kt", fam, t])
                        if fam == 1 and t == 0:
                            ve.wait_ge(kw_ready, NU - 2 * NH)
                        V.tensor_copy(ktok[:, t].rearrange("p h d -> p (h d)"), PS[:, 2 * (proj_count["kt", fam, t][0] % 4), :]).then_inc(proj_v, 1)
                    for i in range(NU + 3):
                        if i < NU:
                            s, h, d = UNITS[i]
                            t = tile_of(s, d)
                            ve.wait_ge(products, at["S", fam, i])
                            if fam == 0:
                                if i >= 2:
                                    ve.wait_ge(p_ready, i - 1)
                                V.scalar_tensor_tensor(eb[:, i % 2, :], PS[:, i % 2, P:2 * P], cols[:, t, 2, d, h:h + 1], mask[:, d, :],
                                                       ALU.add, ALU.add).then_inc(e_ready, 1)
                        u = i - 1
                        if 0 <= u < NU:
                            s, h, d = UNITS[u]
                            if u >= 2:
                                ve.wait_ge(products, at["H", fam, u - 2])
                            if fam == 0:
                                ve.wait_ge(exp_ready, u + 1)
                                w = eb[:, u % 2, :]
                            else:
                                w = Dm[:, d, h, :]
                            V.tensor_tensor(pb[:, u % 2, :], w, PS[:, u % 2, 0:P], ALU.mult).then_inc(p_ready, 1)
                        u = i - 3
                        if u < 0:
                            continue
                        s, h, d = UNITS[u]
                        t = tile_of(s, d)
                        ve.wait_ge(products, at["H", fam, u])
                        width = DH + 1 if fam == 0 else DH
                        U = PS[:, 4 + u % 2, 0:width]
                        num, inter = PS[:, 2 + u % 2, 0:width], PS[:, 2 + u % 2, 256:256 + width]
                        ndu = nd[:, u % 2, :]
                        out = f[:, t, fam * W_A + h * DH:fam * W_A + (h + 1) * DH]
                        if s > 0:
                            w = cols[:, t, 1, d, h:h + 1] if fam == 0 else xz[:, 0, d, h:h + 1]
                            do(V.tensor_scalar(ndu[:, 0:width], inter, w, None, ALU.mult))
                        if s == 0:
                            V.tensor_copy(Cout[:, d, h, 0:width], U).then_inc(state_ready, 1)
                        elif s < NT - 1:
                            w = decB[:, h, d, t:t + 1] if fam == 0 else xz[:, 2, d, h:h + 1]
                            V.scalar_tensor_tensor(Cst[:, d, h, 0:width], Cst[:, d, h, 0:width], w, U, ALU.mult, ALU.add).then_inc(state_ready, 1)
                        settle()
                        if s > 0:
                            link(V.tensor_tensor(ndu[:, 0:width], ndu[:, 0:width], num, ALU.add))
                        else:
                            link(V.tensor_copy(ndu[:, 0:width], num))
                        if fam == 0:
                            link(V.scalar_tensor_tensor(ndu[:, DH + 1:DH + 2], ndu[:, DH:DH + 1], -1.0, ndu[:, DH:DH + 1], ALU.mult, ALU.max))
                            link(V.tensor_scalar(ndu[:, DH + 1:DH + 2], ndu[:, DH + 1:DH + 2], cols[:, t, 3, d, h:h + 1], None, ALU.max))
                            link(V.reciprocal(ndu[:, DH + 1:DH + 2], ndu[:, DH + 1:DH + 2]))
                            if first_on(s, d):
                                V.tensor_scalar(out, ndu[:, 0:DH], ndu[:, DH + 1:DH + 2], None, ALU.mult).then_inc(h_done, 1)
                            else:
                                V.scalar_tensor_tensor(out, ndu[:, 0:DH], ndu[:, DH + 1:DH + 2], out, ALU.mult, ALU.add).then_inc(h_done, 1)
                        elif first_on(s, d):
                            V.tensor_copy(out, ndu[:, 0:DH]).then_inc(h_done, 1)
                        else:
                            V.tensor_tensor(out, ndu[:, 0:DH], out, ALU.add).then_inc(h_done, 1)
                        ve.wait_ge(h_done, fam * NU + u + 1)
                    hv = lambda t, h: f[:, t, fam * W_A + h * DH:fam * W_A + (h + 1) * DH]
                    for t in range(NT):
                        for h in range(NH):
                            do(V.bn_stats(stat[:, t * NH + h, :], hv(t, h)))
                    settle()
                    for i in range(NT * NH):
                        last = V.bn_aggr(mv[:, i, :], stat[:, i:i + 1, :])
                        if i < NT * NH - 1:
                            do(last)
                    last.then_inc(var_ready, 1)
                    ve.wait_ge(dev_ready, fam + 1)
                    link(V.reciprocal(rstd[:], rstd[:]))
                    for t in range(NT):
                        for h in range(NH):
                            i = t * NH + h
                            do(V.tensor_scalar(hv(t, h), hv(t, h), mv[:, i, 0:1], rstd[:, i:i + 1], ALU.subtract, ALU.mult))
                    settle()
                    ve.wait_ge(og_ready, fam + 1)
                    V.tensor_tensor(f[:, :, fam * W_A:(fam + 1) * W_A], f[:, :, fam * W_A:(fam + 1) * W_A], og, ALU.mult).then_inc(norm_done, 1)
                    ve.wait_ge(norm_done, fam + 1)
                for k in range(KD):
                    ve.wait_ge(products, at["h", 4, k])
                    V.tensor_copy(hT[:, k, P:T], PS[:, 2 * (k % 4) + 1, :]).then_inc(h_evac_v, 1)
                def gated(t):
                    ve.wait_ge(products, at["eo", t])
                    V.tensor_tensor(f[:, t, :].rearrange("p (c d) -> p c d", c=2), PS[:, 2 * (t % 4):2 * (t % 4) + 2, :],
                                    rowsB[:, 2 + (t > 0), :].rearrange("p (c d) -> p c d", c=2), ALU.mult).then_inc(out_evac, 1)
                    ve.wait_ge(out_evac, t + 1)

                layer_norm(0, rowsB, gated)

            def peer(l):
                kind = 2
                for i in range(NT + 1):
                    if i < NT:
                        ve.wait_ge(products, at["h", 2 * l + 1, i])
                        b, g = 2 * ((i + pair_h[2 * l + 1]) % 4) + 1, int(i > 0)
                        for k in range(4, KD):
                            last = V.tensor_scalar(htmp[i][:, k, :], PS[:, b, (k - 4) * P:(k - 3) * P], modT[:, l, kind + 1, k, g:g + 1],
                                                   modT[:, l, kind, k, g:g + 1], ALU.mult, ALU.add)
                            if k < KD - 1:
                                do(last)
                        last.then_inc(h_evac_v, 1)
                    t = i - 1
                    if t >= 0:
                        ve.wait_ge(hh_ready, NT * l + t + 1)
                        V.tensor_tensor(hL[:, :, t * P:(t + 1) * P], htmp[t], hH[:, :, t * P:(t + 1) * P].bitcast(f32), ALU.subtract).then_inc(hl_ready, 1)
                ve.wait_ge(hl_ready, NT * (l + 1))
                ve.wait_ge(iota_ready, l + 1)
                for m in range(2 * H_P):
                    for t in range(NT):
                        if t == 0:
                            ve.wait_ge(products, at["ps", l, m])
                        sc_ = PS[:, 4 + 2 * (m % 2) + (t == NT - 1), (t % 4) * P:(t % 4 + 1) * P]
                        v_, i_ = sv[:, t, m // 2, m % 2, :], si[:, t, m // 2, m % 2, :]
                        link(V.max(v_[:, 0:8], sc_))
                        do(V.max_index(i_[:, 0:8], v_[:, 0:8], sc_))
                        V.match_replace(swork[:], v_[:, 0:8], sc_, NEG).then_inc(s_used, 1)
                        ve.wait_ge(s_used, NT * (l * 2 * H_P + m) + t + 1)
                        link(V.max(v_[:, 8:16], swork[:]))
                        link(V.max_index(i_[:, 8:16], v_[:, 8:16], swork[:]))
                for t in range(NT):
                    hk = hkt[:, t]
                    bt = best[:, t]
                    for h in range(H_P):
                        cd = cand[:, 0, :].rearrange("p (a b) -> p a b", b=TOPK)
                        link(V.tensor_tensor(cd, bc(sv[:, t, h, 0, :], TOPK), sv[:, t, h, 1, :].unsqueeze(1).broadcast_to([P, TOPK, TOPK]), ALU.add))
                        link(V.max(bt[:, h, 0:8], cand[:, 0, :]))
                        do(V.max_index(pos[:, h, 0:8], bt[:, h, 0:8], cand[:, 0, :]))
                        link(V.match_replace(cand[:, 1, :], bt[:, h, 0:8], cand[:, 0, :], NEG))
                        link(V.max(bt[:, h, 8:16], cand[:, 1, :]))
                        link(V.max_index(pos[:, h, 8:16], bt[:, h, 8:16], cand[:, 1, :]))
                    link(V.tensor_copy(ssum[:, t, :], bt[:, :, 0]))
                    link(V.tensor_tensor(bt, bt, bc(ssum[:, t, :], TOPK), ALU.subtract))
                    pf = pos[:].rearrange("p h k -> p (h k)")
                    do(V.tensor_scalar(posi[:, 0, :], pf, 4, None, ALU.logical_shift_right))
                    do(V.tensor_scalar(posi[:, 1, :], pf, 15, None, ALU.bitwise_and))
                    do(V.tensor_copy(sif[:].rearrange("p h c k -> p (h c k)"), si[:, t].rearrange("p h c k -> p (h c k)")))
                    settle()
                    link(V.tensor_copy(posf[:], posi[:]))
                    for c in range(2):
                        link(V.tensor_tensor(eqb, bc(posf[:, c, :], TOPK), iota[:, 0:TOPK].unsqueeze(1).broadcast_to([P, HK, TOPK]), ALU.is_equal))
                        link(V.tensor_tensor(eqc.rearrange("p (h k) b -> p h k b", h=H_P), eqb.rearrange("p (h k) b -> p h k b", h=H_P),
                                             sif[:, :, c, :].unsqueeze(2).broadcast_to([P, H_P, TOPK, TOPK]), ALU.mult))
                        link(V.tensor_reduce(hk[:, c, :], eqc, AX, ALU.add))
                V.tensor_copy(ssum[:, 0, 0:1], best[:, 0, 0, 0:1]).then_inc(sm_sub, 1)
                ve.wait_ge(sm_exp, l + 1)
                link(V.tensor_reduce(ssum[:], best[:], AX, ALU.add))
                link(V.reciprocal(ssum[:], ssum[:]))
                for t in range(NT):
                    last = V.tensor_tensor(hkt[:, t, 2, :].rearrange("p (h k) -> p h k", h=H_P), best[:, t], bc(ssum[:, t, :], TOPK), ALU.mult)
                    if t < NT - 1:
                        do(last)
                last.then_inc(hk_ready, 1)
                for t in range(NT):
                    ve.wait_ge(products, at["hk", l, t])
                    V.tensor_copy(hkT[:, :, t * P:(t + 1) * P], PS[:, 4 + t % 2, 0:3 * P].rearrange("p (c t) -> p c t", c=3)).then_inc(hk_evac, 1)
                ve.wait_ge(hk_evac, l * NT + NT)

                link(V.tensor_copy(gH[:], hkT[:, 2, :]))
                link(V.tensor_tensor(gL[:], hkT[:, 2, :], gH[:].bitcast(f32), ALU.subtract))

                def hots(it, k):
                    for tk in range(8):
                        c = bass.ds(32 * it + 8 * k + tk, 1)
                        do(V.tensor_scalar(hot[:, k % 2, 0, tk, :], iota[:], hkT[:, 0, c], None, ALU.is_equal))
                        do(V.tensor_scalar(hot[:, k % 2, 1, tk, :], iota[:], hkT[:, 1, c], gH[:, c].bitcast(f32), ALU.is_equal, ALU.mult))
                        last = V.tensor_scalar(hot[:, k % 2, 2, tk, :], iota[:], hkT[:, 1, c], gL[:, c], ALU.is_equal, ALU.mult)
                        if tk < 7:
                            do(last)
                    last.then_inc(hot_ready, 1)

                def gates_out(it, k):
                    slot = (k // 2 + 1) % 2
                    for c in range(2):
                        ve.wait_ge(g_high, l * 160 + 8 * it + 2 * (k - 2) + c + 1)
                        high, low = gate_halves(c)
                        first = (k % 2) * 8 + 4 * c
                        out = gst[:, slot, :, first:first + 4].rearrange("p j t -> p t j")
                        V.tensor_tensor(out, out, low, ALU.add).then_inc(g_evac, 1)

                for it in range(2):
                    for k in range(4):
                        if it or k >= 2:
                            gates_out(it, k)
                        hots(it, k)
                n0 = ch.n
                with ve.Fori(2, 20) as it:
                    for k in range(4):
                        gates_out(it, k)
                        hots(it, k)
                ch.n = n0 + 18 * 4 * 23
                for k in range(2):
                    gates_out(20, k)
                settle()
                ve.wait_ge(hot_ready, 80 * (l + 1))
                ve.wait_ge(products, at["v", l])
                for half in range(2):
                    ve.wait_ge(g_stored[half], 16 * 20 * (l + 1))
                for t in range(NT):
                    do(V.memset(f[:, t, :], 0.0))
                settle()

                def weigh(blk, q):
                    js = slice((q % 2) * JV, (q % 2 + 1) * JV)
                    if isinstance(blk, int) and blk < 2:
                        ve.wait_ge(ag_full if blk else ag_first, 32 * (l * NBLK + 1) if blk else 32 * (l + 1))
                    elif q % 2 == 0:
                        ve.wait_ge(ag_full, 32 * (l * NBLK + 1) + 16 * blk)
                    a_ = ab[:, js, :]
                    for j in range(JV):
                        aj = a_[:, j, :].rearrange("p (n t) -> p n t", t=16)
                        last = V.tensor_tensor(aj, aj, gb[:, :, (q % 2) * JV + j, :], ALU.mult)
                        if j < JV - 1:
                            do(last)
                    last.then_inc(wf_ready, 1)
                    ve.wait_ge(wh_ready, l * 32 + blk + 1)
                    V.tensor_tensor(WL[:, q % 2], a_, WH[:, q % 2].bitcast(f32), ALU.subtract).then_inc(w_ready, 1)

                def gather(blk, q, t):
                    pr = (q * NT + t) % 4
                    gg = (l * 32 + blk) * NT + t
                    ve.wait_ge(products, at["v", l] + blk * NT + t + 1)
                    ft = f[:, t, :].rearrange("p (c d) -> p c d", c=2)
                    if not (isinstance(blk, int) and gg < NT):
                        ve.wait_ge(acc_done, gg - NT + 1)
                    V.tensor_tensor(ft, ft, PS[:, 2 * pr:2 * pr + 2, :], ALU.add).then_inc(acc_done, 1)

                def blocks(i, last_pass):
                    for q in range(4):
                        blk = 4 * i + q
                        if not (last_pass and q == 3):
                            weigh(blk + 1, (q + 1) % 4)
                            for t in range(NT):
                                gather(blk, q, t)

                weigh(0, 0)
                blocks(0, False)
                n0 = ch.n
                with ve.Fori(1, 7) as i:
                    blocks(i, False)
                ch.n = n0 + 6 * 4 * (JV - 1)
                blocks(7, True)
                settle()

                def gated(t):
                    gather(31, 3, t)
                    ve.wait_ge(acc_done, (l * 32 + 31) * NT + t + 1)
                    link(V.tensor_tensor(f[:, t, :], f[:, t, :], rowsP[:, 2 + (t > 0), :], ALU.mult))

                layer_norm(2 * l + 1, rowsP, gated)

            def odd():
                modulated(2)
                ve.wait_ge(alog_exp, 1)
                ve.wait_ge(od_consts, 1)
                fl = lambda z: z[:].rearrange("p t d h -> p (t d h)")
                ve.wait_ge(products, at["dt",])
                link(V.tensor_tensor(dtc[:].rearrange("p t d h -> p t (d h)"), PS[:, 0, 0:NT * 64].rearrange("p (t n) -> p t n", t=NT),
                                     brow[:, 0, :].unsqueeze(1).broadcast_to([P, NT, 64]), ALU.add))
                V.scalar_tensor_tensor(fl(av), fl(dtc), -1.0, fl(dtc), ALU.mult, ALU.max).then_inc(dt_abs, 1)
                ve.wait_ge(dt_sp, 1)
                link(V.scalar_tensor_tensor(fl(dtc), fl(dtc), 0.0, fl(av), ALU.max, ALU.add))
                V.scalar_tensor_tensor(av[:].rearrange("p t d h -> p t (d h)"), dtc[:].rearrange("p t d h -> p t (d h)"), -1.0,
                                       brow[:, 1, :].unsqueeze(1).broadcast_to([P, NT, 64]), ALU.mult, ALU.mult).then_inc(a_ready, 1)
                ve.wait_ge(products, at["acum",])
                ac = PS[:, 1, 0:NT * 64]
                do(V.tensor_scalar(fl(nac), ac, -1.0, None, ALU.mult))
                do(V.tensor_copy(fl(win), ac))
                do(V.tensor_copy(fl(dcy), PS[:, 2, 0:NT * 64]))
                settle()
                link(V.tensor_tensor(fl(wup), fl(dcy), fl(nac), ALU.add))
                V.tensor_copy(otmp[:, 0:1], nac[:, 0, 0, 0:1]).then_inc(ac_ready, 1)
                ve.wait_ge(seg_exp, 1)
                link(V.tensor_tensor(fl(wup), fl(wup), fl(dtc), ALU.mult))
                for g in range(G_C):
                    hs = slice(g * J_C, (g + 1) * J_C)
                    for m in range(7):
                        if m < 6:
                            q = g * 6 + m
                            ve.wait_ge(pad_filled, q + 1)
                            if q >= 2:
                                ve.wait_ge(act_done, q - 1)
                            acc = cacc[:, q % 2, :]
                            w0 = g * 6 + m
                            link(V.tensor_scalar(acc, cpad[:, q % 2, 0:T + 2], cw[:, w0, 0:1], None, ALU.mult))
                            for j in range(1, D_CONV):
                                ins = V.scalar_tensor_tensor(acc, cpad[:, q % 2, j:j + T + 2], cw[:, w0, j:j + 1], acc, ALU.mult, ALU.add)
                                if j < D_CONV - 1:
                                    link(ins)
                            ins.then_inc(conv_done, 1)
                        mm = m - 1
                        if 0 <= mm < 5:
                            n = g * 5 + mm
                            ve.wait_ge(products, at["xt", g, mm])
                            dst = xs[:, :, mm * P:(mm + 1) * P] if mm < 4 else Btok[:, :, :]
                            b = 4 + 2 * (n % 2)
                            do(V.tensor_copy(dst[:, 0:4, :], PS[:, b, :].rearrange("p (t c) -> p t c", t=4)))
                            V.tensor_copy(dst[:, 4, :], PS[:, b + 1, 0:P]).then_inc(tr_evac, 1)
                    def between(s, d):
                        t = tile_of(s, d)
                        n, nu = (g * 4 + s - 1) * 2 + d, (g * 4 + s) * 2 + d
                        yt = y[:, t, g * GC:(g + 1) * GC]
                        if s > 0:
                            ve.wait_ge(products, at["inter", g, s, d])
                            if n > 0:
                                ve.wait_ge(inter_done, n)
                            link(V.tensor_tensor(otmp[:].rearrange("p (j c) -> p j c", j=J_C), PS[:, 2, :].rearrange("p (j c) -> p j c", j=J_C),
                                                 bc(win[:, t, d, hs], P_C), ALU.mult))
                            V.tensor_tensor(yt, yt, otmp[:], ALU.add).then_inc(inter_done, 1)
                        if s < NT - 1:
                            ve.wait_ge(products, at["upd", g, s, d])
                            if s == 0:
                                if g >= 1:
                                    ve.wait_ge(hst_stored, 16 * g)
                                V.tensor_copy(hout[:, d, :], PS[:, 3, :]).then_inc(upd_done, 1)
                            else:
                                hv = hst[:, d, :].rearrange("p (j c) -> p j c", j=J_C)
                                link(V.tensor_tensor(hv, hv, bc(dcy[:, t, d, hs], P_C), ALU.mult))
                                V.tensor_tensor(hst[:, d, :], hst[:, d, :], PS[:, 3, :], ALU.add).then_inc(upd_done, 1)

                    ve.wait_ge(tr_evac, g * 5 + 5)
                    ve.wait_ge(skip_ready, g + 1)
                    for t in range(NT):
                        n = g * NT + t
                        between(t, 0)
                        ve.wait_ge(products, at["cb", g, t])
                        for d in range(2):
                            ve.wait_ge(oexp_ready, 2 * n + d + 1)
                            for j in range(J_C):
                                last = V.scalar_tensor_tensor(EP[:, d, j, :], EP[:, d, j, :], dtc[:, t, d, g * J_C + j:g * J_C + j + 1],
                                                              PS[:, 4, 0:P], ALU.mult, ALU.mult)
                                if j < J_C - 1:
                                    do(last)
                            last.then_inc(op_ready, 1)
                        between(t, 1)
                        yt = y[:, t, g * GC:(g + 1) * GC]
                        ve.wait_ge(products, at["intra", g, t])
                        if (g * 4 + t) * 2 > 0 and t > 0:
                            ve.wait_ge(inter_done, (g * 4 + t) * 2)
                        V.tensor_tensor(yt, yt, PS[:, 7, :], ALU.add).then_inc(y_intra, 1)
                    ve.wait_ge(y_intra, g * NT + NT)
                    ve.wait_ge(inter_done, 8 * (g + 1))
                    ve.wait_ge(upd_done, 8 * (g + 1))
                for s in range(D_INNER // SLICE):
                    for t in range(NT):
                        n = s * NT + t
                        ve.wait_ge(z_silu, n + 1)
                        yt = y[:, t, s * SLICE:(s + 1) * SLICE]
                        V.tensor_tensor(yt, yt, zt[:, n % 2, :], ALU.mult).then_inc(z_used, 1)
                ve.wait_ge(nw_loaded, 16)
                for k in range(2 * KD):
                    ve.wait_ge(products, at["yt", k])
                    V.tensor_scalar(yT[:, k, P:T], PS[:, 2 * (k % 4) + 1, :], nw[:, k:k + 1], None, ALU.mult).then_inc(yt_v, 1)
                ve.wait_ge(ssq_done, 1)
                V.reciprocal(ssq[:], ssq[:]).then_inc(rr_ready, 1)
                ve.wait_ge(rr_ready, 1)

                def gated(t):
                    ve.wait_ge(products, at["oo", t])
                    V.scalar_tensor_tensor(f[:, t, :].rearrange("p (c d) -> p c d", c=2), PS[:, 2 * (t % 4):2 * (t % 4) + 2, :], ssq[:, t:t + 1],
                                           rowsO[:, 2 + (t > 0), :].rearrange("p (c d) -> p c d", c=2), ALU.mult, ALU.mult).then_inc(oo_evac, 1)
                    ve.wait_ge(oo_evac, t + 1)

                layer_norm(2, rowsO, gated)

            if "even" in run:
                even()
            if "peer0" in run:
                peer(0)
            if "odd" in run:
                odd()
            if "peer1" in run:
                peer(1)

        @block.scalar
        def _(act):
            S = nc.scalar
            ch = Chain(act, act_chain)
            do, link, settle = ch.do, ch.link, ch.settle

            act.dma_start(cT[:], a["c"]).then_inc(small_loaded, 16)
            act.dma_start(bmod, a["b_mod"][:, 0]).then_inc(small_loaded, 16)
            act.dma_start(x[:, 0, :], a["x_prompt"]).then_inc(x_loaded, 16)
            act.dma_start(x[:, 1:NT, :], a["x_sample"]).then_inc(x_loaded, 16)
            act.dma_start(f[:, 0:NT - 1, :], a["pos"]).then_inc(x_loaded, 16)
            act.wait_ge(small_loaded, 32)
            S.activation(cT[:], cT[:], ACT.Silu).then_inc(c_ready, 1)
            for l in range(DEPTH):
                act.wait_ge(mod_rows, l + 1)
                if l + 1 < DEPTH:
                    act.dma_start(bmod, a["b_mod"][:, l + 1]).then_inc(small_loaded, 16)
                act.dma_start(gdram[l, 0], mrow[:, 2 * D:3 * D]).then_inc(gates_stored, 16)
                act.dma_start(gdram[l, 1], mrow[:, 5 * D:6 * D]).then_inc(gates_stored, 16)
            act.wait_ge(mod_cols, DEPTH)
            act.wait_ge(gates_stored, 32 * DEPTH)

            def modulated(n):
                l, kind = n // 2, 2 * (n % 2)
                for t in range(NT):
                    act.wait_ge(products, at["h", n, t])
                    b, g = 2 * ((t + pair_h[n]) % 4), int(t > 0)
                    for k in range(4):
                        last = S.activation(hT[:, k, t * P:(t + 1) * P], PS[:, b, k * P:(k + 1) * P], ACT.Identity, bias=modT[:, l, kind, k, g:g + 1],
                                            scale=modT[:, l, kind + 1, k, g:g + 1])
                        if k < 3:
                            do(last)
                    last.then_inc(h_evac_a, 1)

            def load_rows(n, rows):
                l, second = n // 2, n % 2
                act.dma_start(rows[:, 0, :], a["ln_g"][n].partition_broadcast(P)).then_inc(rows_loaded, 16)
                act.dma_start(rows[:, 1, :], a["ln_b"][n].partition_broadcast(P)).then_inc(rows_loaded, 16)
                act.dma_start(rows[:, 2:4, :].rearrange("p a d -> p (a d)"),
                              gdram[l, second].rearrange("a d -> (a d)").partition_broadcast(P)).then_inc(rows_loaded, 16)

            def layer_norm(n):
                for t in range(NT):
                    act.wait_ge(ln_stats, n * NT + t + 1)
                    S.activation(rstd[:, t:t + 1], mv[:, t, 1:2], ACT.Sqrt, bias=eps[:, 0:1]).then_inc(dev_ready, 1)
                    act.wait_ge(ln_factors, n * NT + t + 1)
                    S.activation(x[:, t, :], x[:, t, :], ACT.Identity, bias=nmr[:, t:t + 1], scale=rstd[:, t:t + 1]).then_inc(ln_normed, 1)

            def deviation(n_var, n):
                act.wait_ge(var_ready, n_var)
                S.activation(rstd[:, 0:n], mv[:, 0:n, 1], ACT.Sqrt, bias=eps[:, 0:1]).then_inc(dev_ready, 1)

            def even():
                modulated(0)
                for dst, name in ((m0[:], "m0"), (gbias[:], "gate_bias"), (gn[:].rearrange("p a d -> p (a d)"), "gn"),
                                  (lg[:].rearrange("p d h -> p (d h)"), "log_decay"), (Cst[:], "Cn0")):
                    src = a[name].partition_broadcast(P) if name in ("gn", "log_decay") else a[name]
                    act.dma_start(dst, src).then_inc(even_loaded, 16)
                L, F, t1, t2 = (grow[:, i] for i in range(4))
                for fam in range(2):
                    def pair_out(kind, i, dst, scale):
                        act.wait_ge(products, at[kind, fam, i])
                        pr = proj_count[kind, fam, i][0] % 4
                        S.activation(dst.rearrange("p (a t) -> p a t", a=2), PS[:, 2 * pr:2 * pr + 2, 0:HT], ACT.Copy,
                                     scale=scale).then_inc(proj_a, 1)
                    for i in range(NH):
                        pair_out("q", i, qT[:, i, :], 1.0 if fam == 0 else DH ** -0.5)
                    if fam == 0:
                        act.wait_ge(gate_exp, 1)
                        link(S.activation(t1, t1, ACT.Exp, scale=-1.0))
                        S.activation(t1, t1, ACT.Ln, bias=1.0).then_inc(gate_act, 1)
                    for i in range(NH):
                        pair_out("k", i, kT[:, i, :], DH ** -0.5 if fam == 0 else 1.0)
                    if fam == 0:
                        act.wait_ge(gate_exp, 2)
                        do(S.activation(L, L, ACT.Exp))
                        do(S.activation(F, F, ACT.Exp))
                        do(S.activation(t2, b_m[:, 1], ACT.Exp, scale=-1.0))
                        S.activation(DEC_, DEC_, ACT.Exp).then_inc(gates_done, 1)
                        act.wait_ge(gates_done, 1)
                        settle()
                        for i in range(8):
                            act.dma_start(gcol[i * NH:(i + 1) * NH, :], grow[:, i // 2, i % 2, :]).then_inc(rows_moved, 16)
                        act.dma_start(o["new_m"], ML[:, :, 0], allow_slow_non_contiguous=True).then_inc(stored, 16)
                    else:
                        act.wait_ge(even_loaded, 80)
                        S.activation(lg[:], lg[:], ACT.Exp).then_inc(diff_ready, 1)
                        act.wait_ge(norm_done, 1)
                    for s in range(2):
                        for t in range(NT):
                            act.wait_ge(products, at["o", fam, (s, t)])
                            pr = proj_count["o", fam, (s, t)][0] % 4
                            S.activation(og[:, t, s * SLICE:(s + 1) * SLICE], PS[:, 2 * pr, 0:SLICE],
                                         ACT.Sigmoid if fam == 0 else ACT.Silu).then_inc(proj_a, 1)
                    if fam == 0:
                        for u in range(NU):
                            act.wait_ge(e_ready, u + 1)
                            S.activation(eb[:, u % 2, :], eb[:, u % 2, :], ACT.Exp).then_inc(exp_ready, 1)
                            if u == 2 * NH + 4:
                                act.wait_ge(state_ready, 2 * NH)
                                act.dma_start(o["new_Cn"], Cout[:]).then_inc(stored, 16)
                        act.wait_ge(h_done, NU)
                        act.dma_start(Cst[:, :, :, 0:DH], a["S0"]).then_inc(ret_ready, 16)
                    else:
                        act.wait_ge(decay_ready, 1)
                        do(S.activation(xz[:], xz[:], ACT.Exp))
                        for d in range(2):
                            for h in range(NH):
                                last = S.activation(Dm[:, d, h, :], diff[:, d, :], ACT.Exp, scale=lg[:, d, h:h + 1])
                                if (d, h) != (1, NH - 1):
                                    do(last)
                        last.then_inc(decay_exp, 1)
                        act.wait_ge(state_ready, NU - 2 * NH + 2 * NH)
                        act.dma_start(o["new_ret"], Cout[:, :, :, 0:DH]).then_inc(stored, 16)
                    deviation(fam + 1, NT * NH)
                act.wait_ge(products, at["H", 1, NU - 1])
                load_rows(0, rowsB)
                for k in range(KD):
                    act.wait_ge(products, at["h", 4, k])
                    S.activation(hT[:, k, 0:P], PS[:, 2 * (k % 4), 0:P], ACT.Copy).then_inc(h_evac_a, 1)
                layer_norm(0)

            def peer(l):
                def high(n, slot, freed):
                    act.wait_ge(raw_full[slot % NRAW], 16 * (l * 18 + 1) + 4 * (n - slot % NRAW))
                    if freed is not None:
                        act.wait_ge(products, freed)
                    S.activation(wH[:, slot % NSPLIT, :], raw[:, slot % NRAW, :], ACT.Copy).then_inc(hi_ready, 1)

                kind = 2
                for t in range(NT):
                    if t == NT - 1:
                        act.wait_ge(x_ready, 2 * l + 2)
                        act.dma_start(keys, a["keys"][l]).then_inc(keys_loaded, 16)
                        for k in range(NSPLIT):
                            high(k, k, None)
                    act.wait_ge(products, at["h", 2 * l + 1, t])
                    b, g = 2 * ((t + pair_h[2 * l + 1]) % 4), int(t > 0)
                    for k in range(4):
                        last = S.activation(htmp[t][:, k, :], PS[:, b, k * P:(k + 1) * P], ACT.Identity, bias=modT[:, l, kind, k, g:g + 1],
                                            scale=modT[:, l, kind + 1, k, g:g + 1])
                        if k < 3:
                            do(last)
                    last.then_inc(h_evac_a, 1)
                    act.wait_ge(h_evac_v, at_h[2 * l + 1] + t + 1)
                    act.wait_ge(h_evac_a, at_h[2 * l + 1] + t + 1)
                    settle()
                    S.activation(hH[:, :, t * P:(t + 1) * P], htmp[t], ACT.Copy).then_inc(hh_ready, 1)
                for m in range(2 * H_P):
                    if m % 2 == 0 and m >= 2:
                        high(m // 2 + 1, m // 2 + 1, at["pq", l, m - 1])
                    act.wait_ge(products, at["pq", l, m])
                    if m >= 2:
                        act.wait_ge(products, at["ps", l, m - 2])
                    S.activation(qb[:, m % 2, :].rearrange("p (a t) -> p a t", a=2), PS[:, 2 * (m % 2):2 * (m % 2) + 2, 0:HT],
                                 ACT.Copy).then_inc(q_evac, 1)

                def product_of(i, jj, build):
                    return at["ub", l] + (i - 3) * 48 + 3 * jj + 1 if build else at["u", l] + i * 16 + jj + 1

                def gelus(i, build, final=False):
                    static = isinstance(i, int)
                    for jj in range(16):
                        gj = l * N_KEYS + i * 16 + jj
                        pr, half = jj // 2, jj % 2
                        n = product_of(i, jj, build)
                        if half == 0 and not (final and pr == 7):
                            if pr:
                                freed = product_of(i, jj - 1, build)
                            elif static and i == 0:
                                freed = at["pq", l, 2 * H_P - 1]
                            else:
                                freed = product_of(i - 1, 15, build and not (static and i == 3))
                            high(8 + 8 * i + pr + 1, pr + 1, freed)
                        act.wait_ge(products, n)
                        if half == 0 and not (static and i == 0 and l == 0 and pr < 2):
                            act.wait_ge(a_stored[pr % 2], 16 * (l * 32 + i * 4 + pr // 2))
                        S.activation(abuf[:, pr % 2, half, :].rearrange("p (a t) -> p a t", a=2), PS[:, 2 * half:2 * half + 2, 0:HT],
                                     ACT.Gelu).then_inc(act_gelu, 1)
                        if half == 1:
                            act.wait_ge(act_gelu, gj + 1)
                            act.dma_start(Ad[2 * i + pr // 4, :, 2 * (pr % 4):2 * (pr % 4) + 2, :], abuf[:, pr % 2]).then_inc(a_stored[pr % 2], 16)
                        if build:
                            for c in range(2):
                                act.wait_ge(products, n + 1 + c)
                                if c == 0 and half == 0 and not (static and i == 3 and l == 0 and pr < 2):
                                    act.wait_ge(g_stored[pr % 2], 16 * (l * 20 + (i - 3) * 4 + pr // 2))
                                first = half * 8 + 4 * c
                                S.activation(gst[:, pr % 2, :, first:first + 4].rearrange("p j t -> p t j"), gate_halves(c)[0], ACT.Copy).then_inc(g_high, 1)
                        if build and half == 1:
                            act.wait_ge(g_evac, l * 160 + 2 * ((i - 3) * 16 + jj + 1))
                            act.dma_start(Gd[:, :, (i - 3) * 8 + pr].rearrange("b p j t -> p b (j t)"),
                                          gst[:, pr % 2].rearrange("p (b j) t -> p b (j t)", j=JB)).then_inc(g_stored[pr % 2], 16)

                gelus(0, False)
                with act.Fori(1, 3) as i:
                    gelus(i, False)
                act.wait_ge(sm_sub, l + 1)
                S.activation(best[:], best[:], ACT.Exp).then_inc(sm_exp, 1)
                gelus(3, True)
                with act.Fori(4, 7) as i:
                    gelus(i, True)
                gelus(7, True, final=True)
                for half in range(2):
                    act.wait_ge(a_stored[half], 16 * 32 * (l + 1))
                    act.wait_ge(g_stored[half], 16 * 20 * (l + 1))
                act.wait_ge(products, at["v", l])
                act.wait_ge(hot_ready, 80 * (l + 1))

                def highs(blk, q):
                    for c in range(2):
                        act.wait_ge(vraw_full[c], 16 * (l * 32 + 1) + 16 * blk)
                        if not (isinstance(blk, int) and blk < 2):
                            act.wait_ge(products, at["v", l] + (blk - 1) * NT)
                        S.activation(wHv[:, 2 * (q % 2) + c, :], rawV[:, c, :], ACT.Copy).then_inc(hi_ready, 1)
                    act.wait_ge(wf_ready, l * 32 + blk + 1)
                    S.activation(WH[:, q % 2], ab[:, (q % 2) * JV:(q % 2 + 1) * JV, :], ACT.Copy).then_inc(wh_ready, 1)

                for q in range(4):
                    highs(q, q)
                with act.Fori(1, 8) as i:
                    for q in range(4):
                        highs(4 * i + q, q)
                act.wait_ge(w_ready, 32 * (l + 1))
                load_rows(2 * l + 1, rowsP)
                layer_norm(2 * l + 1)

            def odd():
                modulated(2)
                act.wait_ge(x_ready, 3)
                act.dma_start(brow[:].rearrange("p a n -> p (a n)"), a["odd_rows"].partition_broadcast(P)).then_inc(odd_loaded, 16)
                act.dma_start(cw[:], a["conv"]).then_inc(odd_loaded, 16)
                act.wait_ge(odd_loaded, 32)
                S.activation(brow[:, 1, :], brow[:, 1, :], ACT.Exp).then_inc(alog_exp, 1)
                fl = lambda z: z[:].rearrange("p t d h -> p (t d h)")
                act.wait_ge(dt_abs, 1)
                link(S.activation(fl(av), fl(av), ACT.Exp, scale=-1.0))
                S.activation(fl(av), fl(av), ACT.Ln, bias=1.0).then_inc(dt_sp, 1)
                act.wait_ge(ac_ready, 1)
                do(S.activation(fl(win), fl(win), ACT.Exp))
                do(S.activation(fl(dcy), fl(dcy), ACT.Exp))
                S.activation(fl(wup), fl(wup), ACT.Exp).then_inc(seg_exp, 1)
                for g in range(G_C):
                    if g:
                        act.wait_ge(products, at["inter", g - 1, NT - 1, 1])
                        act.wait_ge(upd_done, 8 * g)
                    act.dma_start(hst[:], a["h0"][g]).then_inc(hst_loaded, 16)
                    for m in range(7):
                        mm = m - 1
                        if mm >= 0:
                            q = g * 6 + mm
                            act.wait_ge(conv_done, q + 1)
                            if mm < 4:
                                if mm >= 2:
                                    act.wait_ge(products, at["xt", g, mm - 2])
                                dst = sx[:, mm % 2, :]
                            else:
                                dst = BC[:, mm - 4, :]
                            do(S.activation(dst[:, 0:P], cacc[:, q % 2, 0:P], ACT.Silu, bias=cw[:, q, D_CONV:D_CONV + 1]))
                            S.activation(dst[:, P:T], cacc[:, q % 2, P + 2:T + 2], ACT.Silu, bias=cw[:, q, D_CONV:D_CONV + 1]).then_inc(act_done, 1)
                        if m < 6:
                            q = g * 6 + m
                            act.wait_ge(products, at["xbc", g, m])
                            if q >= 2:
                                act.wait_ge(conv_done, q - 1)
                            do(S.activation(cpad[:, q % 2, 2:2 + P], PS[:, 2 * (m % 2), 0:P], ACT.Copy))
                            S.activation(cpad[:, q % 2, 4 + P:4 + T], PS[:, 2 * (m % 2) + 1, :], ACT.Copy).then_inc(pad_filled, 1)
                    for t in range(NT):
                        for d in range(2):
                            n = (g * NT + t) * 2 + d
                            act.wait_ge(products, at["seg", g, t, d])
                            if t:
                                act.wait_ge(products, at["intra", g, t - 1])
                            for j in range(J_C):
                                last = S.activation(EP[:, d, j, :], PS[:, seg_bank[d] + j // 4, (j % 4) * P:(j % 4 + 1) * P], ACT.Exp,
                                                    bias=nac[:, t, d, g * J_C + j:g * J_C + j + 1])
                                if j < J_C - 1:
                                    do(last)
                            last.then_inc(oexp_ready, 1)
                    act.wait_ge(upd_done, 8 * g + 2)
                    act.dma_start(o["new_ssd"][g], hout[:]).then_inc(hst_stored, 16)
                act.wait_ge(products, at["inter", G_C - 1, NT - 1, 1])
                act.wait_ge(inter_done, 8 * G_C)
                act.wait_ge(hst_stored, 16 * G_C)
                act.dma_start(nw[:], a["norm_w"]).then_inc(nw_loaded, 16)
                load_rows(2, rowsO)
                for s in range(D_INNER // SLICE):
                    for t in range(NT):
                        n = s * NT + t
                        act.wait_ge(products, at["z", s, t])
                        if n >= 2:
                            act.wait_ge(z_used, n - 1)
                        S.activation(zt[:, n % 2, :], PS[:, n % 4, 0:SLICE], ACT.Silu).then_inc(z_silu, 1)
                act.wait_ge(z_used, D_INNER // SLICE * NT)
                act.wait_ge(products, at["z", D_INNER // SLICE - 1, NT - 1])
                act.wait_ge(nw_loaded, 16)
                for k in range(2 * KD):
                    act.wait_ge(products, at["yt", k])
                    S.activation(yT[:, k, 0:P], PS[:, 2 * (k % 4), 0:P], ACT.Copy, scale=nw[:, k:k + 1]).then_inc(yt_a, 1)
                junk = hT[:, 0:4, 0:512]
                for t in range(NT):
                    link(S.activation(junk, y[:, t, :].rearrange("p (a b) -> p a b", a=4), ACT.Square, accum_out=ssq[:, t:t + 1]))
                S.activation(ssq[:], ssq[:], ACT.Sqrt, bias=eps[:, 0:1], scale=1.0 / D_INNER).then_inc(ssq_done, 1)
                layer_norm(2)

            if "even" in run:
                even()
            if "peer0" in run:
                peer(0)
            if "odd" in run:
                odd()
            if "peer1" in run:
                peer(1)
            n = len(run) - 1
            for t in range(NT):
                if t < NT - 1 and n > 0:
                    act.wait_ge(x_tile, (n - 1) * (NT - 1) + t + 1)
                else:
                    act.wait_ge(x_ready, n + 1)
                act.dma_start(o["y_prompt"] if t == 0 else o["y_sample"][:, t - 1, :], x[:, t, :]).then_inc(stored, 16)
            act.wait_ge(stored, 16 * NT + (48 if "even" in run else 0))

        @block.gpsimd
        def _(pool):
            G = nc.gpsimd
            ch = Chain(pool, pool_chain)
            do, link, settle = ch.do, ch.link, ch.settle
            do(G.memset(ident[:], 0.0))
            do(G.memset(eps[:], EPS))
            link(G.memset(ones[:], 1.0))
            G.affine_select(out=ident[:], in_=ident[:], compare_op=ALU.not_equal, fill=1.0, base=0,
                            pattern=[[-1, P]], channel_multiplier=1).then_inc(consts_ready, 1)

            def one_sided(dst, src, d, fill):
                sign = 1 if d == 0 else -1
                return G.affine_select(out=dst, in_=src, compare_op=ALU.is_ge, fill=fill, base=0,
                                       pattern=[[sign, P]], channel_multiplier=-sign)

            def layer_norm(n, rows):
                for t in range(NT - 1):
                    pool.wait_ge(x_scaled, n * (NT - 1) + t + 1)
                    G.tensor_tensor(x[:, t, :], x[:, t, :], rows[:, 1, :], ALU.add).then_inc(x_tile, 1)

            def even():
                pool.wait_ge(mod_cols, DEPTH)
                pool.wait_ge(gates_stored, 32 * DEPTH)
                do(G.memset(mask[:], 0.0))
                do(G.memset(sel4[:], 0.0))
                do(G.iota(diff[:, 0, :], [[1, P]], base=0, channel_multiplier=-1, allow_small_or_imprecise_dtypes=True))
                do(G.iota(diff[:, 1, :], [[-1, P]], base=0, channel_multiplier=1, allow_small_or_imprecise_dtypes=True))
                for i, (b, m) in enumerate(((1, 1), (P, -1), (P - 1, -1), (0, 1))):
                    do(G.iota(icol[:, i:i + 1], [[0, 1]], base=b, channel_multiplier=m, allow_small_or_imprecise_dtypes=True))
                settle()
                for d in range(2):
                    do(one_sided(mask[:, d, :], mask[:, d, :], d, NEG))
                do(G.tensor_scalar(diff[:], diff[:], 0.0, None, ALU.max))
                G.affine_select(out=sel4[:], in_=sel4[:], compare_op=ALU.not_equal, fill=1.0, base=0,
                                pattern=[[-1, NH], [0, P]], channel_multiplier=1).then_inc(ev_consts, 1)
                for fam in range(2):
                    if fam == 1:
                        pool.wait_ge(decay_exp, 1)
                        for d in range(2):
                            for h in range(NH):
                                last = one_sided(Dm[:, d, h, :], Dm[:, d, h, :], d, 0.0)
                                if (d, h) != (1, NH - 1):
                                    do(last)
                        last.then_inc(dm_ready, 1)
                    pool.wait_ge(proj_v, proj_count["kt", fam, NT - 1][2])
                    pool.wait_ge(cols_ready, 1)
                    if fam == 1:
                        pool.wait_ge(dm_ready, 1)
                    for u in range(NU - 2 * NH):
                        s, h, d = UNITS[u]
                        t = tile_of(s, d)
                        if u >= 2:
                            pool.wait_ge(products, at["H", fam, u - 2])
                        w = cols[:, t, 0, d, h:h + 1] if fam == 0 else xz[:, 1, d, h:h + 1]
                        G.tensor_scalar(kw[:, u % 2, :], ktok[:, t, h, :], w, None, ALU.mult).then_inc(kw_ready, 1)
                    pool.wait_ge(proj_a, proj_count["o", fam, (1, NT - 1)][2])
                    pool.wait_ge(even_loaded, 80)
                    G.tensor_tensor(og, og, gn[:, fam, :].unsqueeze(1).broadcast_to([P, NT, W_A]), ALU.mult).then_inc(og_ready, 1)
                layer_norm(0, rowsB)

            def peer(l):
                pool.wait_ge(x_ready, 2 * l + 2)
                G.iota(iota[:], [[1, N_KEYS]], base=0, channel_multiplier=0, allow_small_or_imprecise_dtypes=True).then_inc(iota_ready, 1)

                def low(n, k):
                    pool.wait_ge(hi_ready, l * NB + n + 1)
                    G.tensor_tensor(wL[:, k % NSPLIT, :], raw[:, k % NRAW, :], wH[:, k % NSPLIT, :].bitcast(f32), ALU.subtract).then_inc(lo_ready, 1)

                with pool.Fori(0, 9) as i:
                    for k in range(8):
                        low(8 * i + k, k)
                pool.wait_ge(products, at["v", l])
                with pool.Fori(0, 16) as i:
                    for k in range(4):
                        pool.wait_ge(hi_ready, l * NB + 72 + 4 * i + k + 1)
                        G.tensor_tensor(wLv[:, k, :], rawV[:, k % 2, :], wHv[:, k, :].bitcast(f32), ALU.subtract).then_inc(lo_ready, 1)
                layer_norm(2 * l + 1, rowsP)

            def odd():
                pool.wait_ge(x_ready, 3)
                for i in range(2):
                    do(G.memset(cpad[:, i, :], 0.0))
                do(G.memset(EP[:, :, 0, :], 0.0))
                settle()
                for d in range(2):
                    do(one_sided(EP[:, d, 0, :], EP[:, d, 0, :], d, NEG))
                do(G.tensor_copy(identB[:], ident[:]))
                settle()
                do(G.tensor_copy(maskB[:], EP[:, :, 0, :]))
                do(one_sided(tri[:, 0, :], ones[:], 0, 0.0))
                one_sided(tri[:, 1, :], ones[:], 1, 0.0).then_inc(od_consts, 1)
                for g in range(G_C):
                    pool.wait_ge(tr_evac, g * 5 + 5)
                    def skip(t):
                        return G.tensor_tensor(y[:, t, g * GC:(g + 1) * GC].rearrange("p (j c) -> p j c", j=J_C),
                                               xs[:, t, :].rearrange("p (j c) -> p j c", j=J_C), bc(brow[:, 2, g * J_C:(g + 1) * J_C], P_C), ALU.mult)
                    for t in range(NT):
                        if t < NT - 1:
                            do(skip(t))
                        else:
                            skip(t).then_inc(skip_ready, 1)
                    for s in range(NT - 1):
                        for d in range(2):
                            t = tile_of(s, d)
                            nu = (g * 4 + s) * 2 + d
                            if nu >= 1:
                                gg, ss = divmod((nu - 1) // 2, 4)
                                pool.wait_ge(products, at["upd", gg, ss, (nu - 1) % 2])
                            G.tensor_tensor(xw[:].rearrange("p (j c) -> p j c", j=J_C), xs[:, t, :].rearrange("p (j c) -> p j c", j=J_C),
                                            bc(wup[:, t, d, g * J_C:(g + 1) * J_C], P_C), ALU.mult).then_inc(xw_ready, 1)
                layer_norm(2, rowsO)

            if "even" in run:
                even()
            if "peer0" in run:
                peer(0)
            if "odd" in run:
                odd()
            if "peer1" in run:
                peer(1)

        @block.sync
        def _(sp):
            freed = []

            def load(src, k, before=None):
                n = len(freed) if k is None else k
                if before is not None:
                    sp.wait_ge(products, before)
                elif n >= NSLOT:
                    sp.wait_ge(products, freed[n - NSLOT])
                w = src.shape[-1]
                sp.dma_start(ring[:, n % NSLOT, 0:w], src).then_inc(slot_full[n % NSLOT], 16)

            for entry in slices:
                src = entry[0]
                if src == "peer":
                    l = entry[1]
                    sp.wait_ge(products, at["eo" if l == 0 else "oo", NT - 1])
                    if l:
                        sp.wait_ge(ssq_done, 1)
                    for n in range(8):
                        if n >= NRAW:
                            sp.wait_ge(lo_ready, l * NB + n - NRAW + 1)
                        sp.dma_start(raw[:, n % NRAW, :], a["w_pq"][l, n]).then_inc(raw_full[n % NRAW], 16)
                    with sp.Fori(0, 8) as i:
                        for k in range(8):
                            sp.wait_ge(lo_ready, l * NB + 8 + 8 * i + k - NRAW + 1)
                            sp.dma_start(raw[:, k % NRAW, :], a["u"][l, 8 * i + k]).then_inc(raw_full[k % NRAW], 16)
                    sp.wait_ge(products, at["v", l])

                    def value_loads(i, first):
                        if first:
                            sp.dma_start(rawV[:, 0, :], a["v"][l, 0]).then_inc(vraw_full[0], 16)
                            for half in range(2):
                                sp.wait_ge(a_stored[half], 16 * (l * 32 + 2))
                            sp.dma_start(ab[:, 0:JV, :], Ad[i, :, 0:JV]).then_inc(ag_first, 16)
                            for half in range(2):
                                sp.wait_ge(g_stored[half], 16 * 20 * (l + 1))
                                sp.wait_ge(a_stored[half], 16 * 32 * (l + 1))
                            sp.dma_start(gb[:], Gd[i]).then_inc(ag_first, 16)
                            sp.dma_start(rawV[:, 1, :], a["v"][l, 1]).then_inc(vraw_full[1], 16)
                            for j in (JV, JV + 2):
                                sp.dma_start(ab[:, j:j + 2, :], Ad[i, :, j:j + 2]).then_inc(ag_full, 16)
                        else:
                            sp.wait_ge(w_ready, l * 32 + 2 * i)
                            sp.dma_start(ab, Ad[i]).then_inc(ag_full, 16)
                            sp.dma_start(gb[:], Gd[i]).then_inc(ag_full, 16)
                        for k in range(NVRAW if first else 0, 4):
                            if not (first and k < NVRAW):
                                sp.wait_ge(lo_ready, l * NB + 72 + 4 * i + k - NVRAW + 1)
                            sp.dma_start(rawV[:, k % NVRAW, :], a["v"][l, 4 * i + k]).then_inc(vraw_full[k % NVRAW], 16)

                    value_loads(0, True)
                    with sp.Fori(1, NBLK) as i:
                        value_loads(i, False)
                    sp.wait_ge(products, at["v_end", l])
                else:
                    load(src, None)
                    freed.append(at[entry[1]])


def kernel(**inputs):
    import numpy as _np
    import concourse.bacc as _bacc
    from concourse import mybir as _mybir
    from concourse.bass_utils import run_bass_kernel_spmd as _run
    return launch(inputs, _np, _bacc, _mybir, _run, None)


def layouts(i):
    c_ = np.ascontiguousarray

    def rows(w, ncol):
        lead, (K, N) = w.shape[:-2], w.shape[-2:]
        w = w.reshape(*lead, K // P, P, N // ncol, ncol)
        n = len(lead)
        w = w.transpose(*range(n), n + 2, n + 1, n, n + 3)
        return c_(w.reshape(*lead, N // ncol, P, K // P * ncol))

    r = {k: np.asarray(v) for k, v in i.items()}
    a = {}
    a["c"] = c_(np.stack([r["c_ctx"].reshape(KD, P), r["c"][0].reshape(KD, P)], -1).transpose(1, 0, 2))
    a["b_mod"] = c_(np.stack([r["b_mod"]] * 2, 0))
    a["x_prompt"] = c_(r["x_prompt"][0])
    a["x_sample"] = c_(r["x_sample"][0].reshape(NT - 1, P, D).transpose(1, 0, 2))
    a["w_mod"] = rows(r["w_mod"], SLICE)
    w = r["even_w_in"][0]
    sizes = [W_A] * 4 + [2 * NH] * 2 + [W_A] * 4
    at = np.cumsum([0] + sizes)
    part = [w[:, at[n]:at[n + 1]] for n in range(10)]
    a["w_even"] = np.stack([np.stack([rows(q, SLICE) for q in part[0:4]]), np.stack([rows(q, SLICE) for q in part[6:10]])])
    wg = np.zeros((D, P), np.float32)
    for q in range(4):
        src = part[4 + q // 2]
        wg[:, 32 * q:32 * q + NH] = src[:, (q % 2) * NH:(q % 2 + 1) * NH]
    a["w_gate"] = rows(wg, P)[0]
    a["gate_bias"] = c_(np.concatenate([r["mlstm_i_bias"][0], r["mlstm_f_bias"][0]], 0).T)
    a["m0"] = c_(r["state_mlstm_m"][0, 0].T)
    a["gn"] = c_(np.stack([r["even_gn_a"][0], r["even_gn_b"][0]]).reshape(-1))
    a["log_decay"] = c_(r["ret_log_decay"][0].reshape(-1))
    a["Cn0"] = c_(np.concatenate([r["state_mlstm_C"][0, 0], r["state_mlstm_n"][0, 0][..., None]], -1).transpose(2, 0, 1, 3))
    a["S0"] = c_(r["state_ret"][0, 0].transpose(2, 0, 1, 3))
    a["w_eout"] = rows(r["even_w_out"][0], SLICE)
    a["ln_g"] = c_(np.stack([r["ln1_g"][0], r["ln2_g"][0], r["ln1_g"][1], r["ln2_g"][1]]))
    a["ln_b"] = c_(np.stack([r["ln1_b"][0], r["ln2_b"][0], r["ln1_b"][1], r["ln2_b"][1]]))
    w = r["odd_w_in"][0]
    a["w_z"] = rows(w[:, 0:D_INNER], SLICE)
    xbc = w[:, D_INNER:D_INNER + CONV_DIM]
    order = []
    for g in range(G_C):
        order += list(range(g * GC, (g + 1) * GC))
        order += list(range(D_INNER + g * N_C, D_INNER + (g + 1) * N_C))
        order += list(range(D_INNER + G_C * N_C + g * N_C, D_INNER + G_C * N_C + (g + 1) * N_C))
    a["w_xbc"] = c_(rows(xbc[:, order], SLICE).reshape(G_C, 3, P, KD * SLICE))
    a["w_dt"] = rows(w[:, D_INNER + CONV_DIM:], 64)[0]
    cw_ = np.concatenate([r["odd_conv_w"][0], r["odd_conv_b"]], 0)[:, order]
    a["conv"] = c_(cw_.reshape(D_CONV + 1, 24, P).transpose(2, 1, 0))
    a["odd_rows"] = c_(np.concatenate([r["odd_dt_bias"].reshape(-1), r["odd_a_log"].reshape(-1), r["odd_d"].reshape(-1), r["odd_d"].reshape(-1)]))
    a["h0"] = c_(r["state_ssd"][0, 0].reshape(2, G_C, GC, N_C).transpose(1, 3, 0, 2))
    a["norm_w"] = c_(r["odd_norm_w"][0].reshape(2 * KD, P).T)
    a["w_oout"] = rows(r["odd_w_out"][0], P)
    a["w_pq"] = rows(r["peer_w_q"], SLICE)
    a["keys"] = c_(r["peer_sub_keys"].transpose(0, 4, 1, 2, 3).reshape(DEPTH, P, 2 * H_P, N_KEYS))
    u = r["peer_u"].reshape(DEPTH, N_KEYS, N_KEYS // 2, 2, KD, P)
    a["u"] = c_(u.transpose(0, 2, 5, 4, 3, 1)).reshape(DEPTH, N_KEYS // 2, P, KD * SLICE)
    v = r["peer_v"].reshape(DEPTH, N_KEYS, N_KEYS // 2, 2, D)
    a["v"] = c_(v.transpose(0, 2, 1, 3, 4)).reshape(DEPTH, N_KEYS // 2, P, 2 * D)
    rr = np.repeat(np.arange(DEC // GRID_W, dtype=np.float32), GRID_W)
    cc = np.tile(np.arange(GRID_W, dtype=np.float32), DEC // GRID_W)
    fr = (1.0 / (10000.0 ** (np.arange(D // 4, dtype=np.float32) / (D // 4)))).astype(np.float32)
    er, ec = rr[:, None] * fr, cc[:, None] * fr
    pos_ = np.concatenate([np.sin(er), np.cos(er), np.sin(ec), np.cos(ec)], -1).astype(np.float32)
    a["pos"] = c_(pos_.reshape(NT - 1, P, D).transpose(1, 0, 2))
    return a


OUTS = {"y_prompt": [P, D], "y_sample": [P, NT - 1, D], "new_Cn": [P, 2, NH, DH + 1], "new_m": [NH, 2],
        "new_ret": [P, 2, NH, DH], "new_ssd": [G_C, P, 2, GC]}


def program(nc, arrays, mybir_, upto):
    f32 = mybir_.dt.float32
    a = {n: nc.dram_tensor(f"in_{n}", list(v.shape), f32, kind="ExternalInput").ap() for n, v in arrays.items()}
    o = {n: nc.dram_tensor(f"out_{n}", s, f32, kind="ExternalOutput").ap() for n, s in OUTS.items()}
    trunk(nc, a, o, upto)


def launch(inputs, np_, bacc, mybir_, run, upto):
    arrays = layouts(inputs)
    nc = bacc.Bacc("TRN2", target_bir_lowering=False, num_devices=1)
    program(nc, arrays, mybir_, upto)
    r = run(nc, [{f"in_{n}": v for n, v in arrays.items()}], core_ids=[0]).results[0]
    got = {n: r[f"out_{n}"] for n in OUTS}
    c_ = np_.ascontiguousarray
    Cn = got["new_Cn"].transpose(1, 2, 0, 3)
    return (
        got["y_prompt"][None],
        c_(got["y_sample"].transpose(1, 0, 2)).reshape(1, DEC, D),
        c_(Cn[..., 0:DH])[None, None],
        c_(Cn[..., DH])[None, None],
        c_(got["new_m"].T)[None, None],
        c_(got["new_ret"].transpose(1, 2, 0, 3))[None, None],
        c_(got["new_ssd"].transpose(2, 0, 3, 1)).reshape(1, 1, 2, H_C, P_C, N_C),
    )
```
